# Optimizing a Trainium2 kernel written in Bass

```python
import jax, jax.numpy as jnp
from jax import lax
import numpy as np

D_MODEL = 1024
BATCH = 1
SEQ = 512
DEPTH = 2

D_LRU = D_MODEL // 2
D_SC = D_MODEL - D_LRU
D_MIX = D_LRU + D_SC
LRU_HEADS = 8
LRU_HEAD_DIM = D_LRU // LRU_HEADS
SC_GROUPS = 8
LRU_CONV = 4
SC_CONV = 3
LRU_C = 8.0
D_IN = 2 * D_LRU + 3 * D_SC
D_FF = 2816
N_EXPERTS = 8
TOP_K = 2
D_FF_EXPERT = 1408
N_DENSE = (DEPTH + 1) // 2
N_MOE = DEPTH // 2
EPS = 1e-6

kernel_name = "hymba_rglru_shortconv_moe_adaln"

def rms_norm(x, g):
    xf = x.astype(jnp.float32)
    y = xf * lax.rsqrt(jnp.mean(xf * xf, axis=-1, keepdims=True) + EPS)
    return (y * g.astype(jnp.float32)).astype(x.dtype)

def group_rms_norm(y, g, n_groups):
    b, s, ch = y.shape
    yf = y.astype(jnp.float32).reshape(b, s, n_groups, ch // n_groups)
    yf = yf * lax.rsqrt(jnp.mean(yf * yf, axis=-1, keepdims=True) + EPS)
    return (yf.reshape(b, s, ch) * g.astype(jnp.float32)).astype(y.dtype)

def causal_depthwise_conv(x, w):
    k, ch = w.shape
    return lax.conv_general_dilated(
        x, w[:, None, :].astype(x.dtype), window_strides=(1,), padding=[(k - 1, 0)],
        dimension_numbers=("NWC", "WIO", "NWC"), feature_group_count=ch)

def adaln(c, w_mod, b_mod):
    m = jax.nn.silu(c) @ w_mod + b_mod
    shift, scale, gate = jnp.split(m, 3, axis=-1)
    return shift[:, None, :], scale[:, None, :], gate[:, None, :]

def rg_lru(x, w_a, b_a, w_i, b_i, lam):
    b, s, _ = x.shape
    xh = x.reshape(b, s, LRU_HEADS, LRU_HEAD_DIM)
    r = jax.nn.sigmoid(jnp.einsum("bshi,hij->bshj", xh, w_a) + b_a).reshape(b, s, D_LRU)
    i = jax.nn.sigmoid(jnp.einsum("bshi,hij->bshj", xh, w_i) + b_i).reshape(b, s, D_LRU)
    log_a = -LRU_C * r.astype(jnp.float32) * jax.nn.softplus(-lam.astype(jnp.float32))
    a = jnp.exp(log_a)
    u = jnp.sqrt(-jnp.expm1(2.0 * log_a)) * (i * x).astype(jnp.float32)

    def combine(left, right):
        a1, b1 = left
        a2, b2 = right
        return a1 * a2, a2 * b1 + b2

    _, h = lax.associative_scan(combine, (a, u), axis=1)
    return h.astype(x.dtype)

def hybrid_mixer(h, w_in, lru_conv_w, lru_conv_b, lru_wa, lru_ba, lru_wi, lru_bi, lru_lambda,
                 sc_conv_w, gn_lru, gn_sc, w_out):
    u = h @ w_in
    x_lru, g_lru, b_sc, c_sc, x_sc = jnp.split(
        u, [D_LRU, 2 * D_LRU, 2 * D_LRU + D_SC, 2 * D_LRU + 2 * D_SC], axis=-1)
    xc = causal_depthwise_conv(x_lru, lru_conv_w) + lru_conv_b
    y_lru = jax.nn.gelu(g_lru) * rg_lru(xc, lru_wa, lru_ba, lru_wi, lru_bi, lru_lambda)
    y_sc = b_sc * causal_depthwise_conv(c_sc * x_sc, sc_conv_w)
    y = jnp.concatenate([group_rms_norm(y_lru, gn_lru, LRU_HEADS),
                         group_rms_norm(y_sc, gn_sc, SC_GROUPS)], axis=-1)
    return y @ w_out

def swiglu(h, w1, w3, w2):
    return (jax.nn.silu(h @ w1) * (h @ w3)) @ w2

def moe_swiglu(h, w_router, b_router, w1, w3, w2):
    b, s, d = h.shape
    t = h.reshape(b * s, d)
    logits = t.astype(jnp.float32) @ w_router.astype(jnp.float32) + b_router.astype(jnp.float32)
    vals, idx = lax.top_k(logits, TOP_K)
    wts = jax.nn.softmax(vals, axis=-1)
    combine = jnp.sum(jax.nn.one_hot(idx, N_EXPERTS, dtype=jnp.float32) * wts[..., None],
                      axis=1).astype(h.dtype)
    out = jnp.zeros_like(t)
    for e in range(N_EXPERTS):
        out = out + combine[:, e:e + 1] * swiglu(t, w1[e], w3[e], w2[e])
    return out.reshape(b, s, d)

def setup_inputs(seed: int = 0) -> dict:
    key = jax.random.key(seed)
    ks = iter(jax.random.split(key, 40))
    f32 = jnp.float32

    def nrm(shape, scale):
        return jax.random.normal(next(ks), shape, f32) * scale

    def gain(shape):
        return 1.0 + nrm(shape, 0.02)

    x = nrm((BATCH, SEQ, D_MODEL), 1.0)
    c = nrm((BATCH, D_MODEL), 1.0)
    mix_norm = gain((DEPTH, D_MODEL))
    mix_mod_w = nrm((DEPTH, D_MODEL, 3 * D_MODEL), 0.5 * D_MODEL ** -0.5)
    mix_mod_b = nrm((DEPTH, 3 * D_MODEL), 0.02)
    w_in = nrm((DEPTH, D_MODEL, D_IN), D_MODEL ** -0.5)
    lru_conv_w = nrm((DEPTH, LRU_CONV, D_LRU), LRU_CONV ** -0.5)
    lru_conv_b = nrm((DEPTH, D_LRU), 0.02)
    lru_wa = nrm((DEPTH, LRU_HEADS, LRU_HEAD_DIM, LRU_HEAD_DIM), LRU_HEAD_DIM ** -0.5)
    lru_ba = nrm((DEPTH, LRU_HEADS, LRU_HEAD_DIM), 0.02)
    lru_wi = nrm((DEPTH, LRU_HEADS, LRU_HEAD_DIM, LRU_HEAD_DIM), LRU_HEAD_DIM ** -0.5)
    lru_bi = nrm((DEPTH, LRU_HEADS, LRU_HEAD_DIM), 0.02)
    a_c = jax.random.uniform(next(ks), (DEPTH, D_LRU), f32, 0.9, 0.999)
    a_base = a_c ** (1.0 / LRU_C)
    lru_lambda = jnp.log(a_base) - jnp.log1p(-a_base)
    sc_conv_w = nrm((DEPTH, SC_CONV, D_SC), SC_CONV ** -0.5)
    gn_lru = gain((DEPTH, D_LRU))
    gn_sc = gain((DEPTH, D_SC))
    w_out = nrm((DEPTH, D_MIX, D_MODEL), D_MIX ** -0.5)
    ffn_norm = gain((DEPTH, D_MODEL))
    ffn_mod_w = nrm((DEPTH, D_MODEL, 3 * D_MODEL), 0.5 * D_MODEL ** -0.5)
    ffn_mod_b = nrm((DEPTH, 3 * D_MODEL), 0.02)
    dense_w1 = nrm((N_DENSE, D_MODEL, D_FF), D_MODEL ** -0.5)
    dense_w3 = nrm((N_DENSE, D_MODEL, D_FF), D_MODEL ** -0.5)
    dense_w2 = nrm((N_DENSE, D_FF, D_MODEL), D_FF ** -0.5)
    router_w = nrm((N_MOE, D_MODEL, N_EXPERTS), D_MODEL ** -0.5)
    router_b = nrm((N_MOE, N_EXPERTS), 0.01)
    exp_w1 = nrm((N_MOE, N_EXPERTS, D_MODEL, D_FF_EXPERT), D_MODEL ** -0.5)
    exp_w3 = nrm((N_MOE, N_EXPERTS, D_MODEL, D_FF_EXPERT), D_MODEL ** -0.5)
    exp_w2 = nrm((N_MOE, N_EXPERTS, D_FF_EXPERT, D_MODEL), D_FF_EXPERT ** -0.5)
    final_norm = gain((D_MODEL,))
    return {"x": x, "c": c, "mix_norm": mix_norm, "mix_mod_w": mix_mod_w, "mix_mod_b": mix_mod_b,
            "w_in": w_in, "lru_conv_w": lru_conv_w, "lru_conv_b": lru_conv_b,
            "lru_wa": lru_wa, "lru_ba": lru_ba, "lru_wi": lru_wi, "lru_bi": lru_bi,
            "lru_lambda": lru_lambda, "sc_conv_w": sc_conv_w, "gn_lru": gn_lru, "gn_sc": gn_sc,
            "w_out": w_out, "ffn_norm": ffn_norm, "ffn_mod_w": ffn_mod_w, "ffn_mod_b": ffn_mod_b,
            "dense_w1": dense_w1, "dense_w3": dense_w3, "dense_w2": dense_w2,
            "router_w": router_w, "router_b": router_b,
            "exp_w1": exp_w1, "exp_w3": exp_w3, "exp_w2": exp_w2, "final_norm": final_norm}

def reference(x, c, mix_norm, mix_mod_w, mix_mod_b, w_in, lru_conv_w, lru_conv_b,
              lru_wa, lru_ba, lru_wi, lru_bi, lru_lambda, sc_conv_w, gn_lru, gn_sc, w_out,
              ffn_norm, ffn_mod_w, ffn_mod_b, dense_w1, dense_w3, dense_w2,
              router_w, router_b, exp_w1, exp_w3, exp_w2, final_norm):
    for l in range(DEPTH):
        shift, scale, gate = adaln(c, mix_mod_w[l], mix_mod_b[l])
        h = rms_norm(x, mix_norm[l]) * (1.0 + scale) + shift
        y = hybrid_mixer(h, w_in[l], lru_conv_w[l], lru_conv_b[l], lru_wa[l], lru_ba[l],
                         lru_wi[l], lru_bi[l], lru_lambda[l], sc_conv_w[l], gn_lru[l], gn_sc[l],
                         w_out[l])
        x = x + gate * y
        shift, scale, gate = adaln(c, ffn_mod_w[l], ffn_mod_b[l])
        h = rms_norm(x, ffn_norm[l]) * (1.0 + scale) + shift
        j = l // 2
        if l % 2 == 0:
            f = swiglu(h, dense_w1[j], dense_w3[j], dense_w2[j])
        else:
            f = moe_swiglu(h, router_w[j], router_b[j], exp_w1[j], exp_w3[j], exp_w2[j])
        x = x + gate * f
    return rms_norm(x, final_norm)


_drawn_inputs = setup_inputs


def setup_inputs(seed=0):
    import zlib

    import numpy as np

    out = dict(_drawn_inputs(seed))
    spreads = {}
    factors = {'mix_norm': 3.703,
     'lru_ba': 8.0,
     'lru_bi': 8.0,
     'gn_lru': 6.511,
     'gn_sc': 7.955,
     'ffn_norm': 3.774,
     'router_b': 7.021,
     'final_norm': 2.754}
    for name, (base, spread) in spreads.items():
        noise = np.random.default_rng([zlib.crc32(name.encode()), seed]).standard_normal(out[name].shape)
        drawn = base * np.exp(spread * noise) if base else spread * noise
        out[name] = __import__('jax').numpy.asarray(drawn.astype(out[name].dtype))
    for name, factor in factors.items():
        out[name] = (out[name] * factor).astype(out[name].dtype)
    return out
```

```python
from contextlib import ExitStack

import concourse.bass as bass
from concourse import mybir

F32 = mybir.dt.float32
F32R = mybir.dt.float32r
I32 = mybir.dt.int32
U32 = mybir.dt.uint32
ALU = mybir.AluOpType
ACT = mybir.ActivationFunctionType
AX = mybir.AxisListType

P = 128
EPS = 1e-6
LRU_C = 8.0


def trunk_kernel(nc, x, c, mix_norm, mix_mod_w, mix_mod_b, w_in, lru_conv_w, lru_conv_b, lru_wa, lru_ba,
                 lru_wi, lru_bi, lru_lambda, sc_conv_w, gn_lru, gn_sc, w_out, ffn_norm, ffn_mod_w,
                 ffn_mod_b, dense_w1, dense_w3, dense_w2, router_w, router_b, exp_w1, exp_w3, exp_w2,
                 final_norm, out):
    _, T, D = x.shape
    DEPTH = w_in.shape[0]
    K = D // P
    TT = T // P
    DL = lru_conv_w.shape[2]
    J = DL // P
    LT, ST = lru_conv_w.shape[1], sc_conv_w.shape[1]
    HD = lru_wa.shape[2]
    FF = dense_w1.shape[2]
    FB = FF // P
    assert T == 512 and K == 8 and J == 4 and HD * 2 == P and DEPTH == 2 and FB == 22

    E = router_w.shape[2]
    FE = exp_w1.shape[3]
    FEB = FE // P
    EG = 4
    EC = FE // EG
    assert E == 8 and FE % P == 0 and FE % EG == 0 and EC <= 512 and D == 1024
    MAX_TILES = 2 * T // P + E - 1
    MIN_TILES = 2 * T // P
    MAX_TRIPS = 2 * T // (2 * P) + E - 1
    TR = MAX_TRIPS + 1
    W2_CUT = [0, 3, 6, 9, FEB]
    WHOLE = [0] + [(g + 1) * EC // P for g in range(EG)]
    EU = 2 * EG + len(W2_CUT) - 1
    EUF = max(K * EC, 3 * D)
    RAWS = 4
    assert EU % RAWS == 0 and EU % 2 == 0 and max(b - a for a, b in zip(WHOLE, WHOLE[1:])) * P <= 512

    UF = 2048
    WIN_U = w_in.shape[2] // (2 * P)
    WOUT_U = D // (2 * P)
    UP_U = FB
    DOWN_U = 2 * K
    U_WIN, U_WOUT = [0, 0], [0, 0]
    U_WOUT[0] = WIN_U
    U_UP = U_WOUT[0] + WOUT_U
    U_DOWN = U_UP + UP_U
    U_WIN[1] = U_DOWN + DOWN_U
    U_WOUT[1] = U_WIN[1] + WIN_U
    U_END = U_WOUT[1] + WOUT_U
    MC = 3 * P
    MG = 3 * D // MC
    KH = K // 2

    with ExitStack() as ctx:
        def sem(name):
            return ctx.enter_context(nc.semaphore(name))

        top = [-(-nc.sbuf_base // 32) * 32]

        def at(name, shape, dt, offset):
            return nc.alloc_sbuf_tensor_at(name, shape, dt, offset=offset)

        def place(name, shape, dt=F32):
            size = 4
            for n in shape[1:]:
                size *= n
            t = at(name, shape, dt, top[0])
            top[0] += -(-size // 32) * 32
            assert top[0] <= nc.sbuf_usable_end, (name, top[0])
            return t

        ident = place("ident", [P, P])
        mean_all = place("mean_all", [P, P])
        mean_head = place("mean_head", [P, P])
        PT1R = 4 * 24 + 4 * K
        par1 = place("par1", [P, PT1R])
        R_CW, R_CB, R_BA, R_BI, R_LAM, R_SW, R_GL, R_GS, R_C, R_FN, R_END = (
            0, 32, 40, 48, 56, 64, 88, 96, 104, 112, 120)
        par2 = place("par2", [P, R_END])
        eps = place("eps", [P, 1])
        ones = place("ones", [P, 1])
        silu_c = place("silu_c", [P, K])
        ones_all = place("ones_all", [P, P])
        before = place("before", [P, P])
        rw = place("rw", [P, K, E])
        rb = place("rb", [P, E])
        iota_i = place("iota_i", [P, 16], I32)
        iota_f = place("iota_f", [P, 16])
        pick_w = place("pick_w", [P, 2, TT])
        slots_i = place("slots_i", [P, 2, TT], U32)
        table = place("table", [P, 4, TR], I32)
        decay = place("decay", [P, 2, 2 * J])
        small = place("small", [P, 6, 2 * J])
        mods = place("mods", [P, 4, 24])
        mod_gain = place("mod_gain", [P, 4, K])
        tmp_a = place("tmp_a", [P, T])
        tmp_b = place("tmp_b", [P, T])
        xT = place("xT", [P, K, T])
        dense_at = top[0]
        h_hi = place("h_hi", [P, K, T], F32R)
        h_lo = place("h_lo", [P, K, T], F32R)
        mod_acc = place("mod_acc", [P, MC])
        mod_buf = place("mod_buf", [P, 2, KH, MC])
        raw = place("raw", [P, 2, UF])
        w_hi = place("w_hi", [P, 2, UF], F32R)
        w_lo = place("w_lo", [P, 2, UF], F32R)
        area = top[0]
        act_hi = place("act_hi", [P, FB, T], F32R)
        act_lo = place("act_lo", [P, FB, T], F32R)
        top[0] = area
        y_hi = place("y_hi", [P, K, T], F32R)
        y_lo = place("y_lo", [P, K, T], F32R)
        gate_w = place("gate_w", [P, 2, J, P])
        XPW = LT - 1 + T
        xpad = place("xpad", [P, J, XPW + 1])
        xc = place("xc", [P, J, T])
        gel = place("gel", [P, J, T])
        bsc = place("bsc", [P, J, T])
        tr = place("tr", [P, 2, T])
        ti = place("ti", [P, 2, T])
        tt = place("tt", [P, 2, T])
        ta = place("ta", [P, 2, T])
        CXW = ST - 1 + T
        cxpad = place("cxpad", [P, 2, CXW])
        csc = at("csc", [P, J, T], F32, area + 2 * 4 * K * T + 4 * 2 * J * P)
        hf = at("hf", [P, K, T], F32, area + 2 * 4 * K * T + 4 * 2 * J * P)
        rstd = at("rstd", [P, T], F32, area + 2 * 4 * K * T + 4 * 2 * J * P + 4 * K * T)
        xrow = at("xrow", [P, TT, D], F32, area)
        rows = at("rows", [P, 2, P], F32, area + 4 * TT * D)

        ZT = 2 * KH * MC // D
        ZEROS = -(-(MAX_TILES + 1) // ZT) + -(-(MAX_TILES + 1 - MIN_TILES) // ZT)
        top[0] = dense_at
        x_tok = place("x_tok", [P, TT, D])
        ht_hi = place("ht_hi", [P, K, 2 * P], F32R)
        ht_lo = place("ht_lo", [P, K, 2 * P], F32R)
        e_raw = place("e_raw", [P, RAWS, EUF])
        e_hi = place("e_hi", [P, 2, EUF], F32R)
        e_lo = place("e_lo", [P, 2, EUF], F32R)
        at_at = top[0]
        at_hi = place("at_hi", [P, FEB, 2 * P], F32R)
        at_lo = place("at_lo", [P, FEB, 2 * P], F32R)
        rows_at = top[0]
        h_rows = place("h_rows", [P, 2, D])
        hid = place("hid", [P, 2, FE])
        e_silu = place("e_silu", [P, 2, EC])
        y_rows = place("y_rows", [P, 2, D])
        hf3 = at("hf3", [P, K, T], F32, at_at)
        h_tok = at("h_tok", [P, TT, D], F32, rows_at)
        rstd3 = at("rstd3", [P, T], F32, at_at + 4 * K * T)
        route_at = at_at + 4 * K * T + 4 * T
        rt = at("rt", [P, 16, TT, E], F32, route_at)
        rt_u = at("rt_u", [P, TT, E], U32, route_at + 4 * 16 * TT * E)
        ex = at("ex", [P, 16, E], F32, route_at + 4 * 17 * TT * E)
        tb = at("tb", [P, 8, TR], F32, route_at + 4 * 17 * TT * E + 4 * 16 * E)
        raw_at = dense_at + 4 * TT * D + 2 * 4 * K * 2 * P
        picked = at("picked", [P, 2, 2, D], F32, raw_at)
        gate_row = at("gate_row", [P, D], F32, raw_at + 16 * D)
        gain_row = at("gain_row", [P, D], F32, raw_at + 20 * D)
        diag = at("diag", [P, 2, K, P], F32, raw_at + 24 * D)
        mix = at("mix", [P, 2, D], F32, raw_at + 32 * D)
        sums = at("sums", [P, 3, TT], F32, raw_at + 40 * D)

        h_sorted = nc.dram_tensor("h_sorted", ((MAX_TILES + 1) * P, D), F32)
        y_sorted = nc.dram_tensor("y_sorted", ((MAX_TILES + 1) * P, D), F32)

        banks = ctx.enter_context(nc.psum_tensor("banks", [P, 8, 512], F32))
        MODS_BANK = 7
        TOK_BANKS = (1, 2, 3, 7)

        const_ready = sem("const_ready")
        x_loaded = sem("x_loaded")
        rows_loaded = sem("rows_loaded")
        rows_turned = sem("rows_turned")
        par_ready = sem("par_ready")
        vec_link = sem("vec_link")
        act_link = sem("act_link")
        silu_ready = sem("silu_ready")
        decay_step = sem("decay_step")
        decay_ready = sem("decay_ready")
        xt_turned = sem("xt_turned")
        xt_read = sem("xt_read")
        raw_loaded = [sem("raw_loaded0"), sem("raw_loaded1")]
        hi_done = sem("hi_done")
        lo_done = sem("lo_done")
        gemm_done = sem("gemm_done")
        proj_read = sem("proj_read")
        res_read = sem("res_read")
        pair_read = sem("pair_read")
        mod_loaded = [sem("mod_loaded0"), sem("mod_loaded1")]
        mod_step = sem("mod_step")
        mod_mm = sem("mod_mm")
        mods_ready = sem("mods_ready")
        x_upd = sem("x_upd")
        sq_done = sem("sq_done")
        ssq_acc = sem("ssq_acc")
        stat_done = sem("stat_done")
        stat_read = sem("stat_read")
        rstd_ready = sem("rstd_ready")
        xr_ready = sem("xr_ready")
        hf_done = sem("hf_done")
        hh_done = sem("hh_done")
        hl_done = sem("hl_done")
        gw_zero = sem("gw_zero")
        gw_loaded = sem("gw_loaded")
        xpad_ready = sem("xpad_ready")
        pad_ready = sem("pad_ready")
        xc_ready = sem("xc_ready")
        gate_done = sem("gate_done")
        gate_read = sem("gate_read")
        ta_ready = sem("ta_ready")
        v_ready = sem("v_ready")
        s_ready = sem("s_ready")
        scan_done = sem("scan_done")
        y_ready = sem("y_ready")
        ysq_done = sem("ysq_done")
        yn_done = sem("yn_done")
        yh_done = sem("yh_done")
        yl_done = sem("yl_done")
        silu_done = sem("silu_done")
        prod_done = sem("prod_done")
        ah_done = sem("ah_done")
        al_done = sem("al_done")
        out_stored = [sem("out_stored0"), sem("out_stored1")]
        rw_loaded = sem("rw_loaded")
        iota_ready = sem("iota_ready")
        zeros_ready = sem("zeros_ready")
        zeros_stored = sem("zeros_stored")
        logits_done = sem("logits_done")
        tok_turned = sem("tok_turned")
        tok_read = sem("tok_read")
        mask_ready = sem("mask_ready")
        diff_ready = sem("diff_ready")
        diff_exp = sem("diff_exp")
        count_done = sem("count_done")
        slots_ready = sem("slots_ready")
        table_ready = sem("table_ready")
        sorted_stored = sem("sorted_stored")
        rows_in = sem("rows_in")
        ht_turned = sem("ht_turned")
        ht_hi_done = sem("ht_hi_done")
        ht_lo_done = sem("ht_lo_done")
        e_loaded = [sem(f"e_loaded{i}") for i in range(RAWS)]
        e_hi_done = sem("e_hi_done")
        e_lo_done = sem("e_lo_done")
        e_used = sem("e_used")
        e_silu_done = sem("e_silu_done")
        hid_done = sem("hid_done")
        at_turned = sem("at_turned")
        at_hi_done = sem("at_hi_done")
        at_lo_done = sem("at_lo_done")
        y_read = sem("y_read")
        y_stored = sem("y_stored")
        y_free = sem("y_free")
        trips_over = sem("trips_over")
        diag_ready = sem("diag_ready")
        row_done = sem("row_done")
        row_ready = sem("row_ready")
        picked_in = [sem("picked_in0"), sem("picked_in1")]
        mix_done = sem("mix_done")
        xo_ready = sem("xo_ready")
        osum_ready = sem("osum_ready")
        oroot_ready = sem("oroot_ready")
        o_ready = sem("o_ready")

        win_v = [w_in[l].rearrange("(k p) n -> p k n", p=P) for l in range(2)]
        wout_v = [w_out[l].rearrange("(k p) n -> p k n", p=P) for l in range(2)]
        w1_v = dense_w1[0].rearrange("(k p) n -> p k n", p=P)
        w3_v = dense_w3[0].rearrange("(k p) n -> p k n", p=P)
        w2_v = dense_w2[0].rearrange("(h f p) n -> p h f n", p=P, h=2)
        mod_w = [mix_mod_w[0], ffn_mod_w[0], mix_mod_w[1], ffn_mod_w[1]]
        mod_b = [mix_mod_b[0], ffn_mod_b[0], mix_mod_b[1], ffn_mod_b[1]]
        e1_v = exp_w1[0].rearrange("e (k p) n -> e p k n", p=P)
        e3_v = exp_w3[0].rearrange("e (k p) n -> e p k n", p=P)
        e2_v = exp_w2[0].rearrange("e (f p) n -> e p f n", p=P)
        hs_v = h_sorted.ap().rearrange("(t p) d -> p t d", p=P)
        ys_v = y_sorted.ap().rearrange("(t p) d -> p t d", p=P)
        FH = FB // 2
        DOWN_F = FH * P

        def k_of(t, s, n=K):
            return t[:, s, 0:n * (UF // K if n == K else P)].rearrange("p (k n) -> p k n", k=n)

        def block_of(t, n):
            return t[:, bass.ds(n, 1), :].rearrange("p a t -> p (a t)")

        block = ctx.enter_context(nc.Block())

        @block.sync
        def _(sp):
            sp.dma_start(rows[0:24, 0, :], mod_b[0].rearrange("(r q) -> r q", q=P)).then_inc(rows_loaded, 16)
            for m in range(1, 4):
                sp.dma_start(rows[24 * m:24 * m + 24, 0, :],
                             mod_b[m].rearrange("(r q) -> r q", q=P)).then_inc(rows_loaded, 16)
            sp.dma_start(rows[96:96 + 2 * K, 0, :],
                         mix_norm.rearrange("l (r q) -> (l r) q", q=P)).then_inc(rows_loaded, 16)
            sp.dma_start(rows[96 + 2 * K:96 + 4 * K, 0, :],
                         ffn_norm.rearrange("l (r q) -> (l r) q", q=P)).then_inc(rows_loaded, 16)
            for at_row, src in ((R_CW, lru_conv_w.rearrange("l t (r q) -> (l t r) q", q=P)),
                                (R_CB, lru_conv_b.rearrange("l (r q) -> (l r) q", q=P)),
                                (R_BA, lru_ba.rearrange("l (r h) q -> (l r) (h q)", h=2)),
                                (R_BI, lru_bi.rearrange("l (r h) q -> (l r) (h q)", h=2)),
                                (R_LAM, lru_lambda.rearrange("l (r q) -> (l r) q", q=P)),
                                (R_SW, sc_conv_w.rearrange("l t (r q) -> (l t r) q", q=P)),
                                (R_GL, gn_lru.rearrange("l (r q) -> (l r) q", q=P)),
                                (R_GS, gn_sc.rearrange("l (r q) -> (l r) q", q=P)),
                                (R_C, c.rearrange("b (r q) -> (b r) q", q=P)),
                                (R_FN, final_norm.rearrange("(r q) -> r q", q=P))):
                sp.dma_start(rows[at_row:at_row + src.shape[0], 1, :], src).then_inc(rows_loaded, 16)
            sp.dma_start(xrow[:], x[0].rearrange("(a p) d -> p a d", p=P)).then_inc(x_loaded, 16)

            def free(u):
                if not isinstance(u, int) or u >= 2:
                    sp.wait_ge(lo_done, u - 1)

            def load_cols(view, col, s, u):
                free(u)
                sp.dma_start(k_of(raw, s), view[:, :, bass.ds(col, 2 * P)]).then_inc(raw_loaded[s], 16)

            def mixer_loads(l):
                for s in range(2):
                    load_cols(win_v[l], 2 * P * s, s, U_WIN[l] + s)
                with sp.Fori(1, WIN_U // 2) as q:
                    for s in range(2):
                        load_cols(win_v[l], q * 4 * P + 2 * P * s, s, q * 2 + (U_WIN[l] + s))
                with sp.Fori(0, WOUT_U // 2) as q:
                    for s in range(2):
                        load_cols(wout_v[l], q * 4 * P + 2 * P * s, s, q * 2 + (U_WOUT[l] + s))

            mixer_loads(0)
            with sp.Fori(0, UP_U // 2) as g:
                for s in range(2):
                    free(g * 2 + (U_UP + s))
                    pair = raw[:, s, :].rearrange("p (w k n) -> p w k n", w=2, k=K)
                    for w, view in enumerate((w1_v, w3_v)):
                        sp.dma_start(pair[:, w], view[:, :, bass.ds(g * 2 * P + P * s, P)]).then_inc(raw_loaded[s], 16)
            with sp.Fori(0, K) as m:
                for s in range(2):
                    free(m * 2 + (U_DOWN + s))
                    sp.dma_start(raw[:, s, 0:DOWN_F].rearrange("p (f n) -> p f n", f=FH),
                                 w2_v[:, s, :, bass.ds(m * P, P)]).then_inc(raw_loaded[s], 16)
            mixer_loads(1)

            sp.wait_ge(table_ready, 1)
            sp.wait_ge(zeros_stored, 16 * ZEROS)
            trips = sp.value_load(table[0:1, 3, 0:1], min_val=1, max_val=MAX_TRIPS)
            with sp.Fori(0, trips) as i:
                e = sp.value_load(table[0:1, 0, bass.ds(i, 1)], min_val=0, max_val=E - 1)
                for j in range(EU):
                    sp.wait_ge(e_lo_done, i * EU + (j + 1))
                    if j < 2 * EG:
                        view = e1_v if j % 2 == 0 else e3_v
                        src = view[bass.ds(e, 1), :, :, EC * (j // 2):EC * (j // 2 + 1)].rearrange("e p k n -> p (e k) n")
                        dst = e_raw[:, j % RAWS, 0:K * EC].rearrange("p (k n) -> p k n", k=K)
                    else:
                        f0, f1 = W2_CUT[j - 2 * EG], W2_CUT[j - 2 * EG + 1]
                        src = e2_v[bass.ds(e, 1), :, f0:f1, :].rearrange("e p f n -> p (e f) n")
                        dst = e_raw[:, j % RAWS, 0:(f1 - f0) * D].rearrange("p (f n) -> p f n", n=D)
                    sp.dma_start(dst, src).then_inc(e_loaded[j % RAWS], 16)
            for a in range(TT):
                sp.wait_ge(o_ready, a + 1)
                sp.dma_start(out[0, a * P:(a + 1) * P, :], mix[:, a % 2]).then_inc(out_stored[a % 2], 16)
            for n in range(2):
                sp.wait_ge(out_stored[n], 16 * TT // 2)

        @block.gpsimd
        def _(pool):
            made = [0]

            def make(ins):
                made[0] += 1
                ins.then_inc(const_ready, 1)
                pool.wait_ge(const_ready, made[0])

            make(nc.gpsimd.memset(mean_all[:], 1.0 / D))
            make(nc.gpsimd.memset(ident[:], 0.0))
            make(nc.gpsimd.affine_select(out=ident[:], in_=ident[:], compare_op=ALU.not_equal, fill=1.0, base=0,
                                         pattern=[[-1, P]], channel_multiplier=1))
            make(nc.gpsimd.memset(mean_head[:], 0.0))
            for h in range(2):
                part = slice(HD * h, HD * h + HD)
                make(nc.gpsimd.memset(mean_head[part, part], 1.0 / HD))
            make(nc.gpsimd.memset(eps[:], EPS))
            make(nc.gpsimd.memset(ones[:], 1.0))
            make(nc.gpsimd.memset(ones_all[:], 1.0))
            make(nc.gpsimd.memset(before[:], 1.0))
            make(nc.gpsimd.affine_select(out=before[:], in_=before[:], compare_op=ALU.is_gt, fill=0.0, base=0,
                                         pattern=[[1, P]], channel_multiplier=-1))
            nc.gpsimd.iota(iota_i[:], pattern=[[1, 16]], base=0, channel_multiplier=0).then_inc(iota_ready, 1)
            pool.dma_start(rw[:], router_w[0].rearrange("(k p) e -> p k e", p=P)).then_inc(rw_loaded, 16)
            pool.dma_start(rb[:], router_b[0:1, :].partition_broadcast(P)).then_inc(rw_loaded, 16)

            def mod_loads(m):
                view = mod_w[m].rearrange("(h k p) n -> p h k n", p=P, h=2)

                def load(g, h, n):
                    if n is not None:
                        pool.wait_ge(mod_step, n)
                    pool.dma_start(mod_buf[:, h], view[:, h, :, bass.ds(g * MC, MC)]).then_inc(mod_loaded[h], 16)

                if m == 0:
                    for h in range(2):
                        load(0, h, None)
                with pool.Fori(0 if m else 1, MG) as g:
                    for h in range(2):
                        load(g, h, g * 8 + (8 * MG * m + 4 * h - 4))

            def gate_loads(l):
                if l:
                    pool.wait_ge(gemm_done, 2 * U_WIN[1])
                    pool.wait_ge(hl_done, K * 3)
                else:
                    pool.wait_ge(x_upd, K)
                nc.gpsimd.memset(gate_w[:], 0.0).then_inc(gw_zero, 1)
                pool.wait_ge(gw_zero, l + 1)
                for g, w in enumerate((lru_wa, lru_wi)):
                    v = w[l].rearrange("(j h) i o -> h i j o", h=2)
                    for h in range(2):
                        part = slice(HD * h, HD * h + HD)
                        pool.dma_start(gate_w[part, g, :, part], v[h]).then_inc(gw_loaded, 16)

            def pads(l):
                pool.wait_ge(hl_done, K * (2 * l + 1))
                nc.gpsimd.memset(xpad[:, :, 0:LT - 1], 0.0).then_inc(pad_ready, 1)
                pool.wait_ge(pad_ready, 2 * l + 1)
                nc.gpsimd.memset(cxpad[:, :, 0:ST - 1], 0.0).then_inc(pad_ready, 1)
                pool.wait_ge(pad_ready, 2 * l + 2)

            mod_loads(0)
            gate_loads(0)
            pads(0)
            mod_loads(1)
            mod_loads(2)
            gate_loads(1)
            pads(1)
            mod_loads(3)

            pool.wait_ge(mod_step, 8 * MG * 4)
            nc.gpsimd.memset(mod_buf[:], 0.0).then_inc(zeros_ready, 1)
            pool.wait_ge(zeros_ready, 1)
            zeros = mod_buf[:].rearrange("p h k n -> p (h k n)")
            for view, t0 in ((hs_v, 0), (ys_v, MIN_TILES)):
                for t in range(t0, MAX_TILES + 1, ZT):
                    n = min(ZT, MAX_TILES + 1 - t)
                    pool.dma_start(view[:, t:t + n, :], zeros[:, 0:n * D].rearrange("p (t d) -> p t d", t=n)
                                   ).then_inc(zeros_stored, 16)
            pool.wait_ge(zeros_stored, 16 * ZEROS)
            pool.wait_ge(slots_ready, 1)
            pool.wait_ge(tok_read, 2 * TT)
            for a in range(TT):
                for which in range(2):
                    pool.indirect_dma_start(
                        out=h_sorted.ap(), out_offset=bass.IndirectOffsetOnAxis(ap=slots_i[:, which, a:a + 1], axis=0),
                        in_=h_tok[:, a, :], in_offset=None).then_inc(sorted_stored, 16)
            pool.wait_ge(sorted_stored, 16 * 2 * TT)
            pool.wait_ge(table_ready, 1)

            def load_rows(i):
                t0 = pool.value_load(table[0:1, 1, bass.ds(i, 1)], min_val=0, max_val=MAX_TILES - 1)
                pool.dma_start(h_rows[:], hs_v[:, bass.ds(t0, 2), :]).then_inc(rows_in, 16)

            pool.sem_inc(y_free, 1)
            load_rows(0)
            trips = pool.value_load(table[0:1, 3, 0:1], min_val=1, max_val=MAX_TRIPS)
            with pool.Fori(0, trips) as i:
                pool.wait_ge(ht_turned, i * 4 + 4)
                load_rows(i + 1)
                pool.wait_ge(y_read, i + 2)
                t0 = pool.value_load(table[0:1, 1, bass.ds(i, 1)], min_val=0, max_val=MAX_TILES - 1)
                two = pool.value_load(table[0:1, 2, bass.ds(i, 1)], min_val=0, max_val=1)
                with pool.If(two > 0):
                    pool.dma_start(ys_v[:, bass.ds(t0, 2), :], y_rows[:]).then_inc(y_stored, 16)
                with pool.Else():
                    pool.dma_start(ys_v[:, bass.ds(t0, 1), :], y_rows[:, 0:1]).then_inc(y_stored, 16)
                pool.nop()
                pool.wait_ge(y_stored, i * 16 + 16)
                pool.sem_inc(y_free, 1)
            pool.wait_ge(rows_in, trips * 16 + 16)
            pool.sem_inc(trips_over, 1)
            pool.wait_ge(trips_over, 1)
            for a in range(TT):
                if a >= 2:
                    pool.wait_ge(xo_ready, a - 1)
                for which in range(2):
                    pool.indirect_dma_start(
                        out=picked[:, a % 2, which, :], out_offset=None, in_=y_sorted.ap(),
                        in_offset=bass.IndirectOffsetOnAxis(ap=slots_i[:, which, a:a + 1], axis=0)
                    ).then_inc(picked_in[a % 2], 16)

        def stat_of(l, n):
            return 10 * l + n

        BASE = {}
        BASE["win0"] = 0
        BASE["wout0"] = BASE["win0"] + 16 * WIN_U // 2
        BASE["up"] = BASE["wout0"] + 16 * WOUT_U // 2
        BASE["down"] = BASE["up"] + 32 * UP_U // 2
        BASE["win1"] = BASE["down"] + 16 * DOWN_U // 2
        BASE["wout1"] = BASE["win1"] + 16 * WIN_U // 2
        PHASES = [("win0", U_WIN[0], WIN_U), ("wout0", U_WOUT[0], WOUT_U), ("up", U_UP, UP_U),
                  ("down", U_DOWN, DOWN_U), ("win1", U_WIN[1], WIN_U), ("wout1", U_WOUT[1], WOUT_U)]

        def unit_info(u):
            for name, first, n in PHASES:
                if first <= u < first + n:
                    per = 32 if name == "up" else 16
                    return BASE[name] + per * ((u - first) // 2 + 1), DOWN_F if name == "down" else UF
            return None

        @block.scalar
        def _(act):
            links = [0]

            def link(ins):
                links[0] += 1
                ins.then_inc(act_link, 1)
                act.wait_ge(act_link, links[0])

            def split(u, s, loaded=None, n=None):
                if loaded is None:
                    if u >= U_END:
                        return
                    loaded, n = unit_info(u)
                act.wait_ge(raw_loaded[s], loaded)
                if not isinstance(u, int) or u >= 2:
                    act.wait_ge(gemm_done, (u - 1) * 2)
                nc.scalar.activation(w_hi[:, s, 0:n], raw[:, s, 0:n], ACT.Copy).then_inc(hi_done, 1)

            act.sem_inc(proj_read, 4)
            act.sem_inc(ah_done, 1)
            act.sem_inc(e_silu_done, 1)
            act.wait_ge(par_ready, 2)
            nc.scalar.activation(silu_c[:], par2[:, R_C:R_C + K], ACT.Silu).then_inc(silu_ready, 1)
            link(nc.scalar.activation(small[:, 0], par2[:, R_LAM:R_LAM + 2 * J], ACT.Abs))
            nc.scalar.activation(small[:, 1], small[:, 0], ACT.Exp, scale=-1.0).then_inc(decay_step, 1)

            def square(n):
                act.wait_ge(x_upd, n + 1)
                if n >= 1:
                    act.wait_ge(ssq_acc, n)
                nc.scalar.activation(tmp_b[:], xT[:, n % K], ACT.Square).then_inc(sq_done, 1)

            for k in range(K):
                act.wait_ge(xt_turned, k + 1)
                nc.scalar.activation(xT[:, k], banks[:, k % 4], ACT.Copy).then_inc(x_upd, 1)
                square(k)
            split(0, 0)
            split(1, 1)

            def norm(nth, stat):
                act.wait_ge(stat_done, stat + 1)
                nc.scalar.activation(rstd[:], banks[:, 6 - stat % 2], ACT.Sqrt, bias=eps[:]).then_inc(stat_read, 1)
                act.wait_ge(mods_ready, nth + 1)

                def modulate(k):
                    act.wait_ge(xr_ready, K * nth + k + 1)
                    nc.scalar.activation(hf[:, k], hf[:, k], ACT.Identity, bias=mods[:, nth, k:k + 1],
                                         scale=mod_gain[:, nth, k:k + 1]).then_inc(hf_done, 1)

                modulate(0)
                for k in range(K):
                    if k + 1 < K:
                        modulate(k + 1)
                    act.wait_ge(hf_done, K * nth + k + 1)
                    nc.scalar.activation(h_hi[:, k], hf[:, k], ACT.Copy).then_inc(hh_done, 1)

            def mixer(l):
                u0 = U_WIN[l]

                def evacuate(u, i):
                    q, j = u // 2, 2 * (u % 2) + i
                    act.wait_ge(gemm_done, 2 * (u0 + u) + 1 + i)
                    ps = banks[:, j]
                    if q == 0:
                        nc.scalar.activation(xpad[:, j, LT - 1:LT - 1 + T], ps, ACT.Copy).then_inc(xpad_ready, 1)
                        act.wait_ge(xpad_ready, J * l + j + 1)
                        act.sem_inc(proj_read, 1)
                    elif q == 1:
                        nc.scalar.activation(gel[:, j], ps, ACT.Gelu_apprx_tanh).then_inc(proj_read, 1)
                    elif q == 2:
                        nc.scalar.activation(bsc[:, j], ps, ACT.Copy).then_inc(proj_read, 1)
                    elif q == 3:
                        act.wait_ge(xc_ready, J * (l + 1))
                        nc.scalar.activation(csc[:, j], ps, ACT.Copy).then_inc(proj_read, 1)

                def gates(pair):
                    for b in range(2):
                        j = 2 * pair + b
                        n = 8 * l + 2 * j
                        if pair:
                            act.wait_ge(scan_done, J * l + b + 1)
                        act.wait_ge(gate_done, n + 1)
                        nc.scalar.activation(tr[:, b], banks[:, 4], ACT.Sigmoid,
                                             bias=par2[:, R_BA + J * l + j:R_BA + J * l + j + 1]).then_inc(gate_read, 1)
                        act.wait_ge(gate_done, n + 2)
                        nc.scalar.activation(ti[:, b], banks[:, 5], ACT.Sigmoid,
                                             bias=par2[:, R_BI + J * l + j:R_BI + J * l + j + 1]).then_inc(gate_read, 1)
                    act.wait_ge(gate_read, 8 * l + 4 * pair + 4)
                    if pair == 0 and l == 0:
                        act.wait_ge(decay_ready, 1)
                    for b in range(2):
                        col = J * l + 2 * pair + b
                        nc.scalar.activation(tt[:, b], tr[:, b], ACT.Tanh, scale=decay[:, 0, col:col + 1]).then_inc(ta_ready, 1)
                        nc.scalar.activation(ta[:, b], tr[:, b], ACT.Exp, scale=decay[:, 1, col:col + 1]).then_inc(ta_ready, 1)

                def roots(pair):
                    for b in range(2):
                        act.wait_ge(v_ready, J * l + 2 * pair + b + 1)
                        nc.scalar.activation(tt[:, b], tt[:, b], ACT.Sqrt).then_inc(s_ready, 1)

                def group_squares(y, half, j):
                    n = 8 * l + 4 * half + j
                    act.wait_ge(y_ready, n + 1 if half else 8 * l + J)
                    if j >= 2:
                        act.wait_ge(stat_done, stat_of(l, 1 + 4 * half + j - 2) + 1)
                    elif half:
                        act.wait_ge(stat_done, stat_of(l, 1 + 2 + j) + 1)
                    nc.scalar.activation(tt[:, j % 2], y[:, j], ACT.Square).then_inc(ysq_done, 1)

                def group_root(half, j):
                    st = stat_of(l, 1 + 4 * half + j)
                    act.wait_ge(stat_done, st + 1)
                    if j >= 2:
                        act.wait_ge(yn_done, 8 * l + 4 * half + j - 1)
                    elif half:
                        act.wait_ge(yn_done, 8 * l + 2 + j + 1)
                    nc.scalar.activation(ta[:, j % 2], banks[:, 6 - st % 2], ACT.Sqrt, bias=eps[:]).then_inc(stat_read, 1)

                def group_hi(y, half, j):
                    n = 8 * l + 4 * half + j
                    act.wait_ge(yn_done, n + 1)
                    nc.scalar.activation(y_hi[:, 4 * half + j], y[:, j], ACT.Copy).then_inc(yh_done, 1)

                for u in range(WIN_U):
                    for i in range(2):
                        if u // 2 < 4:
                            evacuate(u, i)
                    split(u0 + u + 2, u % 2)
                    if u == 3:
                        gates(0)
                    if u == 4:
                        roots(0)
                    if u == 5:
                        gates(1)
                    if u == 6:
                        roots(1)
                    if u == 7:
                        for j in range(J):
                            group_squares(xc, 0, j)
                            group_root(0, j)
                        for j in range(J):
                            group_hi(xc, 0, j)
                for j in range(J):
                    group_squares(bsc, 1, j)
                    group_root(1, j)
                for j in range(J):
                    group_hi(bsc, 1, j)
                n0 = 8 + 16 * l
                for u in range(WOUT_U):
                    for i in range(2):
                        square(n0 + 2 * u + i)
                    split(U_WOUT[l] + u + 2, u % 2)

            def hidden(g, s, ahead):
                n = g * 2 + s
                act.wait_ge(gemm_done, (n + U_UP) * 2 + 1)
                act.wait_ge(prod_done, n + 1)
                nc.scalar.activation(tmp_a[:], banks[:, 2 * s], ACT.Silu).then_inc(silu_done, 1)
                act.wait_ge(prod_done, n + 2)
                nc.scalar.activation(block_of(act_hi, n), tmp_b[:],
                                     ACT.Copy).then_inc(ah_done, 1)
                if ahead is None:
                    split(n + (U_UP + 2), s, BASE["up"] + 32 * (g + 2), UF)
                else:
                    split(ahead, s)

            norm(0, 0)
            mixer(0)
            norm(1, stat_of(0, 9))
            with act.Fori(0, UP_U // 2 - 1) as g:
                for s in range(2):
                    hidden(g, s, None)
            for s in range(2):
                hidden(UP_U // 2 - 1, s, U_DOWN + s)

            def down(m, bank, last):
                for s in range(2):
                    if last:
                        split(U_WIN[1] + s, s)
                    else:
                        split(m * 2 + (U_DOWN + 2 + s), s, m * 16 + (BASE["down"] + 32), DOWN_F)
                act.wait_ge(x_upd, m + (16 + 1))
                act.wait_ge(ssq_acc, m + 16)
                nc.scalar.activation(tmp_b[:], block_of(xT, m), ACT.Square).then_inc(sq_done, 1)

            with act.Fori(0, K // 2 - 1) as mm:
                for i in range(2):
                    down(mm * 2 + i, i, False)
            for i in range(2):
                down(K - 2 + i, i, i == 1)
            norm(2, stat_of(1, 0))
            mixer(1)

            act.wait_ge(stat_done, stat_of(1, 9) + 1)
            nc.scalar.activation(rstd3[:], banks[:, 6 - stat_of(1, 9) % 2], ACT.Sqrt, bias=eps[:]).then_inc(stat_read, 1)
            act.wait_ge(mods_ready, 4)
            for k in range(K):
                act.wait_ge(xr_ready, 3 * K + k + 1)
                nc.scalar.activation(hf3[:, k], hf3[:, k], ACT.Identity, bias=mods[:, 3, k:k + 1],
                                     scale=mod_gain[:, 3, k:k + 1]).then_inc(hf_done, 1)
            act.wait_ge(diff_ready, 1)
            nc.scalar.activation(rt[:, 13, 0, 0:TT], rt[:, 12, 0, 0:TT], ACT.Exp).then_inc(diff_exp, 1)
            for which, t in enumerate((h_tok, x_tok)):
                for n in range(2 * TT):
                    m = 2 * TT * which + n
                    act.wait_ge(tok_turned, m + 1)
                    nc.scalar.activation(t[:, n // 2, 512 * (n % 2):512 * (n % 2) + 512], banks[:, TOK_BANKS[n % 4]],
                                         ACT.Copy).then_inc(tok_read, 1)

            def ht_split(i):
                for n in range(4):
                    bank = (4, 5, 0, 1)[n]
                    act.wait_ge(ht_turned, i * 4 + (n + 1))
                    nc.scalar.activation(ht_hi[:, 4 * (n % 2):4 * (n % 2) + 4, P * (n // 2):P * (n // 2) + P],
                                         banks[:, bank].rearrange("p (k n) -> p k n", k=4), ACT.Copy).then_inc(ht_hi_done, 1)

            def y_copy(n):
                for b in range(4):
                    ins = nc.scalar.activation(y_rows[:, b // 2, 512 * (b % 2):512 * (b % 2) + 512],
                                               banks[:, (6, 7, 2, 3)[b]], ACT.Copy)
                ins.then_inc(y_read, 1)

            def e_split(i, j):
                n = K * EC if j < 2 * EG else (W2_CUT[j - 2 * EG + 1] - W2_CUT[j - 2 * EG]) * D
                act.wait_ge(e_loaded[j % RAWS], i * (16 * EU // RAWS) + 16 * (j // RAWS + 1))
                act.wait_ge(e_used, i * EU + (j + 1))
                nc.scalar.activation(e_hi[:, j % 2, 0:n], e_raw[:, j % RAWS, 0:n], ACT.Copy).then_inc(e_hi_done, 1)

            def trip(i, tiles):
                def at_split(g):
                    f0, f1 = WHOLE[g], WHOLE[g + 1]
                    act.wait_ge(at_turned, i * EG + (g + 1))
                    for a in range(tiles):
                        ins = nc.scalar.activation(at_hi[:, f0:f1, P * a:P * a + P],
                                                   banks[:, 4 + a, 0:P * (f1 - f0)].rearrange("p (f n) -> p f n", n=P),
                                                   ACT.Copy)
                    ins.then_inc(at_hi_done, 1)

                e_split(i, 0)
                e_split(i, 1)
                act.wait_ge(e_used, i * EU + 2)
                y_copy(i)
                for j in range(EU - 2):
                    g = j // 2
                    if j < 2 * EG and j % 2 == 0:
                        act.wait_ge(e_used, i * EU + (j + 3))
                        act.wait_ge(hid_done, i * EG + (g + 1))
                        nc.scalar.activation(e_silu[:, 0:tiles], banks[:, 0:tiles, 0:EC], ACT.Silu).then_inc(e_silu_done, 1)
                    e_split(i, j + 2)
                    if j in (3, 5, 7):
                        at_split((j - 3) // 2)
                    if j == 8:
                        at_split(3)
                act.wait_ge(y_free, i + 1)
                ht_split(i + 1)

            ht_split(0)
            trips = act.value_load(table[0:1, 3, 0:1], min_val=1, max_val=MAX_TRIPS)
            with act.Fori(0, trips) as i:
                two = act.value_load(table[0:1, 2, bass.ds(i, 1)], min_val=0, max_val=1)
                with act.If(two > 0):
                    trip(i, 2)
                with act.Else():
                    trip(i, 1)
                act.nop()
            act.wait_ge(e_used, trips * EU + 2)
            y_copy(trips)
            for which, t in enumerate((gate_row, gain_row)):
                for b in range(2):
                    act.wait_ge(row_done, 2 * which + b + 1)
                    nc.scalar.activation(t[:, 512 * b:512 * b + 512], banks[:, 2 * which + b], ACT.Copy).then_inc(row_ready, 1)
            for a in range(TT):
                act.wait_ge(xo_ready, a + 1)
                nc.scalar.activation(mix[:, a % 2], x_tok[:, a], ACT.Square, accum_out=sums[:, 0, a:a + 1]).then_inc(osum_ready, 1)
                act.wait_ge(osum_ready, a + 1)
                nc.scalar.activation(sums[:, 1, a:a + 1], sums[:, 0, a:a + 1], ACT.Sqrt, bias=eps[:],
                                     scale=1.0 / D).then_inc(oroot_ready, 1)

        @block.vector
        def _(dve):
            links = [0]

            def link(ins):
                links[0] += 1
                ins.then_inc(vec_link, 1)
                dve.wait_ge(vec_link, links[0])

            def split(u, s, n=None):
                if n is None:
                    if u >= U_END:
                        return
                    n = unit_info(u)[1]
                dve.wait_ge(hi_done, u + 1)
                nc.vector.tensor_tensor(w_lo[:, s, 0:n], raw[:, s, 0:n], w_hi[:, s, 0:n].bitcast(F32),
                                        ALU.subtract).then_inc(lo_done, 1)

            def mod_group(n):
                dve.wait_ge(mod_mm, n + 1)
                for h in range(2):
                    dve.wait_ge(mod_loaded[h], n * 16 + 16)
                    for k in range(KH):
                        i = KH * h + k
                        scalar = silu_c[:, i:i + 1]
                        if i == 0:
                            ins = nc.vector.tensor_scalar(mod_acc[:], mod_buf[:, h, k], scalar, None, ALU.mult)
                        else:
                            dve.wait_ge(mod_step, n * 8 + i)
                            ins = nc.vector.scalar_tensor_tensor(out=mod_acc[:], in0=mod_buf[:, h, k], scalar=scalar,
                                                                 in1=mod_acc[:], op0=ALU.mult, op1=ALU.add)
                        ins.then_inc(mod_step, 1)

            def mod_finish(m):
                dve.wait_ge(mod_mm, MG * (m + 1) + 1)
                link(nc.vector.tensor_tensor(mods[:, m], banks[:, MODS_BANK, 24 * m:24 * m + 24],
                                             par1[:, 24 * m:24 * m + 24], ALU.add))
                gain = 96 + (2 * K if m % 2 else 0) + K * (m // 2)
                nc.vector.scalar_tensor_tensor(out=mod_gain[:, m], in0=mods[:, m, K:2 * K], scalar=1.0,
                                               in1=par1[:, gain:gain + K], op0=ALU.add,
                                               op1=ALU.mult).then_inc(mods_ready, 1)

            def add_square(n):
                dve.wait_ge(sq_done, n + 1)
                if n % K == 0:
                    nc.vector.tensor_copy(tmp_a[:], tmp_b[:]).then_inc(ssq_acc, 1)
                else:
                    dve.wait_ge(ssq_acc, n)
                    nc.vector.tensor_tensor(tmp_a[:], tmp_a[:], tmp_b[:], ALU.add).then_inc(ssq_acc, 1)

            def norm(nth, stat):
                dve.wait_ge(stat_read, stat + 1)
                nc.vector.reciprocal(rstd[:], rstd[:]).then_inc(rstd_ready, 1)
                dve.wait_ge(rstd_ready, nth + 1)
                for k in range(K + 2):
                    if k < K:
                        nc.vector.tensor_tensor(hf[:, k], xT[:, k], rstd[:], ALU.mult).then_inc(xr_ready, 1)
                    if k >= 2:
                        dve.wait_ge(hh_done, K * nth + k - 1)
                        nc.vector.tensor_tensor(h_lo[:, k - 2], hf[:, k - 2], h_hi[:, k - 2].bitcast(F32),
                                                ALU.subtract).then_inc(hl_done, 1)

            def residual(n, m, bank, nth, count):
                dve.wait_ge(gemm_done, count)
                xm = block_of(xT, m)
                gate = mods[:, nth, bass.ds(m + 2 * K, 1)]
                nc.vector.scalar_tensor_tensor(out=xm, in0=banks[:, bank], scalar=gate, in1=xm,
                                               op0=ALU.mult, op1=ALU.add).then_inc(x_upd, 1)
                dve.wait_ge(x_upd, n + 1)
                dve.sem_inc(res_read, 1)

            dve.sem_inc(res_read, 4)
            dve.sem_inc(pair_read, 2)
            for first in (prod_done, al_done, hid_done, at_lo_done):
                dve.sem_inc(first, 1)
            dve.wait_ge(rows_turned, 1)
            nc.vector.tensor_copy(par1[:], banks[:, 4, 0:PT1R]).then_inc(par_ready, 1)
            dve.wait_ge(rows_turned, 2)
            nc.vector.tensor_copy(par2[:], banks[:, 5, 0:R_END]).then_inc(par_ready, 1)
            for k in range(K):
                add_square(k)
            dve.wait_ge(silu_ready, 1)
            split(0, 0)
            split(1, 1)
            with dve.Fori(0, MG) as g:
                mod_group(g)
            dve.wait_ge(decay_step, 1)
            z, w, w2, acc, low = (small[:, i] for i in (1, 2, 3, 4, 5))
            link(nc.vector.tensor_scalar(w, z, 2.0, None, ALU.add))
            link(nc.vector.reciprocal(w, w))
            link(nc.vector.tensor_tensor(w, w, z, ALU.mult))
            link(nc.vector.tensor_tensor(w2, w, w, ALU.mult))
            link(nc.vector.tensor_scalar(acc, w2, 1.0 / 19, 1.0 / 17, ALU.mult, ALU.add))
            for odd in range(15, 0, -2):
                link(nc.vector.tensor_tensor(acc, acc, w2, ALU.mult))
                link(nc.vector.tensor_scalar(acc, acc, 1.0 / odd, None, ALU.add))
            link(nc.vector.tensor_tensor(acc, acc, w, ALU.mult))
            link(nc.vector.tensor_scalar(low, par2[:, R_LAM:R_LAM + 2 * J], -1.0, 0.0, ALU.mult, ALU.max))
            link(nc.vector.scalar_tensor_tensor(out=acc, in0=acc, scalar=2.0, in1=low, op0=ALU.mult, op1=ALU.add))
            nc.vector.tensor_scalar(decay[:, 1], acc, -LRU_C, None, ALU.mult)
            nc.vector.tensor_scalar(decay[:, 0], acc, LRU_C, None, ALU.mult).then_inc(decay_ready, 1)

            def mixer(l):
                u0 = U_WIN[l]
                m_next = 2 * l + 1

                def conv_lru(j):
                    dve.wait_ge(xpad_ready, J * l + j + 1)
                    w = [par2[:, R_CW + 4 * J * l + J * t + j:R_CW + 4 * J * l + J * t + j + 1] for t in range(LT)]
                    b = par2[:, R_CB + J * l + j:R_CB + J * l + j + 1]
                    link(nc.vector.tensor_scalar(xc[:, j], xpad[:, j, LT - 1:LT - 1 + T], w[LT - 1], b, ALU.mult, ALU.add))
                    for t in range(LT - 1):
                        ins = nc.vector.scalar_tensor_tensor(out=xc[:, j], in0=xpad[:, j, t:t + T], scalar=w[t],
                                                             in1=xc[:, j], op0=ALU.mult, op1=ALU.add)
                        if t < LT - 2:
                            link(ins)
                    ins.then_inc(xc_ready, 1)

                def to_v(pair):
                    for b in range(2):
                        dve.wait_ge(ta_ready, 2 * (J * l + 2 * pair + b) + 2)
                        link(nc.vector.tensor_scalar(tr[:, b], tt[:, b], 1.0, None, ALU.add))
                        link(nc.vector.reciprocal(tr[:, b], tr[:, b]))
                        nc.vector.scalar_tensor_tensor(out=tt[:, b], in0=tt[:, b], scalar=2.0, in1=tr[:, b],
                                                       op0=ALU.mult, op1=ALU.mult).then_inc(v_ready, 1)
                        link(nc.vector.tensor_tensor(ti[:, b], ti[:, b], xc[:, 2 * pair + b], ALU.mult))

                def scans(pair):
                    for b in range(2):
                        j = 2 * pair + b
                        dve.wait_ge(s_ready, J * l + j + 1)
                        link(nc.vector.tensor_tensor(ti[:, b], ti[:, b], tt[:, b], ALU.mult))
                        nc.vector.tensor_tensor_scan(xc[:, j], ta[:, b], ti[:, b], 0.0, ALU.mult,
                                                     ALU.add).then_inc(scan_done, 1)
                        dve.wait_ge(scan_done, J * l + j + 1)
                        nc.vector.tensor_tensor(xc[:, j], xc[:, j], gel[:, j], ALU.mult).then_inc(y_ready, 1)

                def gated_conv(j):
                    dve.wait_ge(gemm_done, 2 * (u0 + 8 + j // 2) + 1 + j % 2)
                    link(nc.vector.tensor_tensor(cxpad[:, j % 2, ST - 1:CXW], banks[:, j], csc[:, j], ALU.mult))
                    dve.sem_inc(proj_read, 1)
                    w = [par2[:, R_SW + ST * J * l + J * t + j:R_SW + ST * J * l + J * t + j + 1] for t in range(ST)]
                    link(nc.vector.tensor_scalar(ti[:, j % 2], cxpad[:, j % 2, ST - 1:CXW], w[ST - 1], None, ALU.mult))
                    for t in range(ST - 1):
                        link(nc.vector.scalar_tensor_tensor(out=ti[:, j % 2], in0=cxpad[:, j % 2, t:t + T], scalar=w[t],
                                                            in1=ti[:, j % 2], op0=ALU.mult, op1=ALU.add))
                    nc.vector.tensor_tensor(bsc[:, j], bsc[:, j], ti[:, j % 2], ALU.mult).then_inc(y_ready, 1)

                def group_norm(y, half, j):
                    st = stat_of(l, 1 + 4 * half + j)
                    gain = par2[:, (R_GS if half else R_GL) + J * l + j:(R_GS if half else R_GL) + J * l + j + 1]
                    dve.wait_ge(stat_read, st + 1)
                    link(nc.vector.reciprocal(ta[:, j % 2], ta[:, j % 2]))
                    dve.wait_ge(ysq_done, 8 * l + 4 * half + j + 1)
                    nc.vector.scalar_tensor_tensor(out=y[:, j], in0=y[:, j], scalar=gain, in1=ta[:, j % 2],
                                                   op0=ALU.mult, op1=ALU.mult).then_inc(yn_done, 1)

                def group_lo(y, half, j):
                    dve.wait_ge(yh_done, 8 * l + 4 * half + j + 1)
                    nc.vector.tensor_tensor(y_lo[:, 4 * half + j], y[:, j], y_hi[:, 4 * half + j].bitcast(F32),
                                            ALU.subtract).then_inc(yl_done, 1)

                mod_group(MG * m_next)
                for u in range(WIN_U):
                    if u == 9:
                        gated_conv(0)
                        gated_conv(1)
                    split(u0 + u + 2, u % 2)
                    if u == 0:
                        dve.wait_ge(pad_ready, 2 * l + 2)
                        conv_lru(0)
                        conv_lru(1)
                    if u == 1:
                        conv_lru(2)
                        conv_lru(3)
                    if u == 3:
                        to_v(0)
                    if u == 4:
                        scans(0)
                    if u == 5:
                        to_v(1)
                    if u == 6:
                        scans(1)
                    if u == 7:
                        for j in range(J):
                            group_norm(xc, 0, j)
                        for j in range(J):
                            group_lo(xc, 0, j)
                    if u % 2 == 0:
                        mod_group(MG * m_next + 1 + u // 2)
                gated_conv(2)
                gated_conv(3)
                for j in range(J):
                    group_norm(bsc, 1, j)
                for j in range(J):
                    group_lo(bsc, 1, j)
                n0 = 8 + 16 * l
                for u in range(WOUT_U):
                    for i in range(2):
                        n = n0 + 2 * u + i
                        residual(n, 2 * u + i, (2 * u + i) % 4, 2 * l, 2 * (U_WOUT[l] + u) + 1 + i)
                        if i == 1:
                            split(U_WOUT[l] + u + 2, u % 2)
                        add_square(n)
                    if u % 2 == 0:
                        mod_group(MG * m_next + 6 + u // 2)
                mod_finish(m_next)

            def hidden(g, s, ahead):
                n = g * 2 + s
                dve.wait_ge(gemm_done, (n + U_UP) * 2 + 2)
                dve.wait_ge(silu_done, n + 1)
                dve.wait_ge(ah_done, n + 1)
                dve.wait_ge(al_done, n + 1)
                nc.vector.tensor_tensor(tmp_b[:], banks[:, 2 * s + 1], tmp_a[:], ALU.mult).then_inc(prod_done, 1)
                dve.wait_ge(prod_done, n + 2)
                dve.sem_inc(pair_read, 1)
                dve.wait_ge(ah_done, n + 2)
                nc.vector.tensor_tensor(block_of(act_lo, n), tmp_b[:],
                                        block_of(act_hi, n).bitcast(F32),
                                        ALU.subtract).then_inc(al_done, 1)
                if ahead is None:
                    split(n + (U_UP + 2), s, UF)
                else:
                    split(ahead, s)

            mod_finish(0)
            norm(0, 0)
            mixer(0)
            norm(1, stat_of(0, 9))
            with dve.Fori(0, MG) as g:
                hidden(g, 0, None)
                mod_group(g + 2 * MG)
                hidden(g, 1, None)
            with dve.Fori(MG, UP_U // 2 - 1) as g:
                hidden(g, 0, None)
                hidden(g, 1, None)
            for s in range(2):
                hidden(UP_U // 2 - 1, s, U_DOWN + s)
            mod_finish(2)
            link(nc.vector.memset(tmp_a[:], 0.0))

            def down(m, bank, last):
                for s in range(2):
                    if last:
                        split(U_WIN[1] + s, s)
                    else:
                        split(m * 2 + (U_DOWN + 2 + s), s, DOWN_F)
                residual(m + 16, m, bank, 1, m * 4 + (2 * U_DOWN + 4))
                dve.wait_ge(sq_done, m + 17)
                dve.wait_ge(ssq_acc, m + 16)
                nc.vector.tensor_tensor(tmp_a[:], tmp_a[:], tmp_b[:], ALU.add).then_inc(ssq_acc, 1)

            with dve.Fori(0, K // 2 - 1) as mm:
                for i in range(2):
                    down(mm * 2 + i, i, False)
            for i in range(2):
                down(K - 2 + i, i, i == 1)
            norm(2, stat_of(1, 0))
            mixer(1)

            dve.wait_ge(stat_read, stat_of(1, 9) + 1)
            nc.vector.reciprocal(rstd3[:], rstd3[:]).then_inc(rstd_ready, 1)
            dve.wait_ge(rstd_ready, 4)
            for k in range(K):
                nc.vector.tensor_tensor(hf3[:, k], xT[:, k], rstd3[:], ALU.mult).then_inc(xr_ready, 1)
            dve.wait_ge(iota_ready, 1)
            link(nc.vector.tensor_copy(iota_f[:], iota_i[:]))
            logits, best, best_i, m1, m2, mask, pre, tot, slot = (rt[:, n] for n in range(9))
            dve.wait_ge(logits_done, 1)
            dve.wait_ge(rw_loaded, 32)
            for a in range(TT):
                link(nc.vector.tensor_tensor(logits[:, a], banks[:, 0, E * a:E * a + E], rb[:], ALU.add))
            for a in range(TT):
                link(nc.vector.max(best[:, a], logits[:, a]))
            for a in range(TT):
                link(nc.vector.max_index(rt_u[:, a], best[:, a], logits[:, a]))
            link(nc.vector.tensor_copy(best_i, rt_u[:]))
            for a in range(TT):
                for m, n in ((m1, 0), (m2, 1)):
                    link(nc.vector.tensor_scalar(m[:, a], iota_f[:, 0:E], best_i[:, a, n:n + 1], None, ALU.is_equal))
            nc.vector.tensor_tensor(mask, m1, m2, ALU.add).then_inc(mask_ready, 1)
            diff, e2 = rt[:, 12, 0, 0:TT], rt[:, 13, 0, 0:TT]
            nc.vector.tensor_tensor(diff, best[:, :, 1], best[:, :, 0], ALU.subtract).then_inc(diff_ready, 1)
            dve.wait_ge(count_done, 1)
            link(nc.vector.tensor_copy(pre, banks[:, 5, 0:TT * E].rearrange("p (a e) -> p a e", a=TT)))
            link(nc.vector.tensor_copy(tot, banks[:, 5, TT * E:2 * TT * E].rearrange("p (a e) -> p a e", a=TT)))
            count, tiles_n, trips_n, tile_c, trip_c, one8, tile0, trip0, run = (ex[:, n] for n in range(9))
            link(nc.vector.tensor_tensor(count, tot[:, 0], tot[:, 1], ALU.add))
            for a in range(2, TT):
                link(nc.vector.tensor_tensor(count, count, tot[:, a], ALU.add))
            link(nc.vector.memset(one8, 1.0))
            link(nc.vector.tensor_scalar(tiles_n, count, 0.0, None, ALU.is_gt))
            for n in range(1, TT):
                link(nc.vector.scalar_tensor_tensor(out=tiles_n, in0=count, scalar=float(P * n), in1=tiles_n,
                                                    op0=ALU.is_gt, op1=ALU.add))
            link(nc.vector.tensor_scalar(trips_n, count, 0.0, None, ALU.is_gt))
            for n in range(1, TT // 2):
                link(nc.vector.scalar_tensor_tensor(out=trips_n, in0=count, scalar=float(2 * P * n), in1=trips_n,
                                                    op0=ALU.is_gt, op1=ALU.add))
            link(nc.vector.tensor_tensor_scan(tile_c, one8, tiles_n, 0.0, ALU.mult, ALU.add))
            link(nc.vector.tensor_tensor_scan(trip_c, one8, trips_n, 0.0, ALU.mult, ALU.add))
            link(nc.vector.tensor_tensor(tile0, tile_c, tiles_n, ALU.subtract))
            link(nc.vector.tensor_tensor(trip0, trip_c, trips_n, ALU.subtract))
            link(nc.vector.tensor_scalar(run, tile0, float(P), None, ALU.mult))
            for a in range(TT):
                link(nc.vector.tensor_tensor(slot[:, a], pre[:, a], run, ALU.add))
                if a < TT - 1:
                    link(nc.vector.tensor_tensor(run, run, tot[:, a], ALU.add))
            for which, m in enumerate((m1, m2)):
                link(nc.vector.tensor_tensor(rt[:, 9 + which], m, slot, ALU.mult))
                link(nc.vector.tensor_reduce(rt[:, 11, which, 0:TT], rt[:, 9 + which], AX.X, ALU.add))
                ins = nc.vector.tensor_copy(slots_i[:, which], rt[:, 11, which, 0:TT])
                if which == 0:
                    link(ins)
            ins.then_inc(slots_ready, 1)
            expert, first, after, one, ge0, ge1 = (tb[:, n] for n in range(6))
            number = iota_f[:, 0:TR]
            link(nc.vector.memset(tb[:, 0:3], 0.0))
            link(nc.vector.scalar_tensor_tensor(out=run, in0=trip0, scalar=-2.0, in1=tile0, op0=ALU.mult, op1=ALU.add))
            for e in range(E):
                link(nc.vector.tensor_scalar(ge0, number, trip0[:, e:e + 1], None, ALU.is_ge))
                link(nc.vector.tensor_scalar(ge1, number, trip_c[:, e:e + 1], None, ALU.is_ge))
                link(nc.vector.tensor_tensor(expert, expert, ge1, ALU.add))
                link(nc.vector.tensor_tensor(one, ge0, ge1, ALU.subtract))
                link(nc.vector.scalar_tensor_tensor(out=first, in0=one, scalar=run[:, e:e + 1], in1=first,
                                                    op0=ALU.mult, op1=ALU.add))
                link(nc.vector.scalar_tensor_tensor(out=after, in0=one, scalar=tile_c[:, e:e + 1], in1=after,
                                                    op0=ALU.mult, op1=ALU.add))
            link(nc.vector.scalar_tensor_tensor(out=first, in0=number, scalar=2.0, in1=first, op0=ALU.mult, op1=ALU.add))
            link(nc.vector.tensor_tensor(one, after, first, ALU.subtract))
            link(nc.vector.tensor_scalar(one, one, 2.0, None, ALU.is_ge))
            link(nc.vector.tensor_scalar(expert, expert, float(E - 1), None, ALU.min))
            link(nc.vector.tensor_scalar(first, first, float(MAX_TILES - 1), None, ALU.min))
            link(nc.vector.tensor_copy(table[:, 0], expert))
            link(nc.vector.tensor_copy(table[:, 1], first))
            link(nc.vector.tensor_copy(table[:, 2], one))
            nc.vector.tensor_copy(table[:, 3, 0:1], trip_c[:, E - 1:E]).then_inc(table_ready, 1)
            dve.wait_ge(diff_exp, 1)
            link(nc.vector.tensor_scalar(pick_w[:, 0], e2, 1.0, None, ALU.add))
            link(nc.vector.reciprocal(pick_w[:, 0], pick_w[:, 0]))
            link(nc.vector.tensor_tensor(pick_w[:, 1], pick_w[:, 0], e2, ALU.mult))

            def ht_split(i):
                for n in range(4):
                    bank = (4, 5, 0, 1)[n]
                    part = (slice(None), slice(4 * (n % 2), 4 * (n % 2) + 4), slice(P * (n // 2), P * (n // 2) + P))
                    dve.wait_ge(ht_hi_done, i * 4 + (n + 1))
                    nc.vector.tensor_tensor(ht_lo[part], banks[:, bank].rearrange("p (k n) -> p k n", k=4),
                                            ht_hi[part].bitcast(F32), ALU.subtract).then_inc(ht_lo_done, 1)

            def e_split(i, j):
                n = K * EC if j < 2 * EG else (W2_CUT[j - 2 * EG + 1] - W2_CUT[j - 2 * EG]) * D
                dve.wait_ge(e_hi_done, i * EU + (j + 1))
                nc.vector.tensor_tensor(e_lo[:, j % 2, 0:n], e_raw[:, j % RAWS, 0:n], e_hi[:, j % 2, 0:n].bitcast(F32),
                                        ALU.subtract).then_inc(e_lo_done, 1)

            def trip(i, tiles):
                def at_split(g):
                    f0, f1 = WHOLE[g], WHOLE[g + 1]
                    dve.wait_ge(at_hi_done, i * EG + (g + 1))
                    for a in range(tiles):
                        part = (slice(None), slice(f0, f1), slice(P * a, P * a + P))
                        ins = nc.vector.tensor_tensor(at_lo[part],
                                                      banks[:, 4 + a, 0:P * (f1 - f0)].rearrange("p (f n) -> p f n", n=P),
                                                      at_hi[part].bitcast(F32), ALU.subtract)
                    ins.then_inc(at_lo_done, 1)

                e_split(i, 0)
                e_split(i, 1)
                for j in range(EU - 2):
                    g = j // 2
                    e_split(i, j + 2)
                    if j < 2 * EG and j % 2 == 1:
                        dve.wait_ge(e_used, i * EU + (j + 3))
                        dve.wait_ge(e_silu_done, i * EG + (g + 2))
                        nc.vector.tensor_tensor(hid[:, 0:tiles, EC * g:EC * g + EC], banks[:, 2:2 + tiles, 0:EC],
                                                e_silu[:, 0:tiles], ALU.mult).then_inc(hid_done, 1)
                    if j in (3, 5, 7):
                        at_split((j - 3) // 2)
                    if j == 8:
                        at_split(3)
                ht_split(i + 1)

            dve.sem_inc(e_lo_done, RAWS)
            ht_split(0)
            trips = dve.value_load(table[0:1, 3, 0:1], min_val=1, max_val=MAX_TRIPS)
            with dve.Fori(0, trips) as i:
                two = dve.value_load(table[0:1, 2, bass.ds(i, 1)], min_val=0, max_val=1)
                with dve.If(two > 0):
                    trip(i, 2)
                with dve.Else():
                    trip(i, 1)
                dve.nop()

            dve.wait_ge(e_lo_done, trips * EU + RAWS)
            for k in range(K):
                nc.vector.tensor_scalar(diag[:, 0, k], ident[:], mods[:, 3, 2 * K + k:2 * K + k + 1], None,
                                        ALU.mult).then_inc(diag_ready, 1)
            for k in range(K):
                nc.vector.tensor_scalar(diag[:, 1, k], ident[:], par2[:, R_FN + k:R_FN + k + 1], None,
                                        ALU.mult).then_inc(diag_ready, 1)
            def last_norm(a):
                dve.wait_ge(oroot_ready, a + 1)
                link(nc.vector.reciprocal(sums[:, 2, a:a + 1], sums[:, 1, a:a + 1]))
                if a == 0:
                    dve.wait_ge(row_ready, 4)
                nc.vector.scalar_tensor_tensor(out=mix[:, a % 2], in0=x_tok[:, a], scalar=sums[:, 2, a:a + 1],
                                               in1=gain_row[:], op0=ALU.mult, op1=ALU.mult).then_inc(o_ready, 1)

            for a in range(TT):
                got = picked[:, a % 2]
                dve.wait_ge(picked_in[a % 2], 32 * (a // 2 + 1))
                link(nc.vector.tensor_scalar(got[:, 0], got[:, 0], pick_w[:, 0, a:a + 1], None, ALU.mult))
                link(nc.vector.scalar_tensor_tensor(out=got[:, 0], in0=got[:, 1], scalar=pick_w[:, 1, a:a + 1],
                                                    in1=got[:, 0], op0=ALU.mult, op1=ALU.add))
                if a == 0:
                    dve.wait_ge(row_ready, 2)
                nc.vector.tensor_tensor(got[:, 0], got[:, 0], gate_row[:], ALU.mult).then_inc(mix_done, 1)
                dve.wait_ge(mix_done, a + 1)
                if a >= 2:
                    dve.wait_ge(out_stored[a % 2], 16 * (a // 2))
                nc.vector.tensor_tensor(x_tok[:, a], x_tok[:, a], got[:, 0], ALU.add).then_inc(xo_ready, 1)
                last_norm(a)

        @block.tensor
        def _(pe):
            def product(ps, hi, lo, x_hi, x_lo, start, stop):
                nc.tensor.matmul(ps, hi, x_hi, start=start, stop=False)
                nc.tensor.matmul(ps, hi, x_lo, start=False, stop=False)
                return nc.tensor.matmul(ps, lo, x_hi, start=False, stop=stop)

            def mod_sum(n):
                pe.wait_ge(mod_step, n * 8 + 8)
                for b in range(MC // P):
                    last = nc.tensor.matmul(banks[:, MODS_BANK, bass.ds(n * 3 + b, 1)], mod_acc[:, b * P:(b + 1) * P],
                                            ones[:], start=True, stop=True)
                last.then_inc(mod_mm, 1)

            def stat(st, matrix, values):
                if st >= 2:
                    pe.wait_ge(stat_read, st - 1)
                nc.tensor.matmul(banks[:, 6 - st % 2], matrix, values, start=True, stop=True).then_inc(stat_done, 1)

            def unit_of_two(u, s, x_hi, x_lo, bank, credit):
                pe.wait_ge(lo_done, u + 1)
                for i in range(2):
                    pe.wait_ge(*credit(i))
                    for k in range(K):
                        cols = slice(2 * P * k + P * i, 2 * P * k + P * i + P)
                        last = product(banks[:, bank + i], w_hi[:, s, cols], w_lo[:, s, cols], x_hi[:, k], x_lo[:, k],
                                       k == 0, k == K - 1)
                    last.then_inc(gemm_done, 1)

            pe.sem_inc(mod_mm, 1)
            pe.wait_ge(const_ready, 11)
            pe.wait_ge(rows_loaded, 16 * 16)
            nc.tensor.transpose(banks[:, 4, 0:PT1R], rows[0:PT1R, 0, :], ident[0:PT1R, 0:PT1R]).then_inc(rows_turned, 1)
            nc.tensor.transpose(banks[:, 5, 0:R_END], rows[0:R_END, 1, :], ident[0:R_END, 0:R_END]).then_inc(rows_turned, 1)
            pe.wait_ge(x_loaded, 16)
            for k in range(K):
                if k >= 4:
                    pe.wait_ge(x_upd, k - 3)
                for a in range(TT):
                    last = nc.tensor.transpose(banks[:, k % 4, a * P:(a + 1) * P], xrow[:, a, k * P:(k + 1) * P], ident[:])
                last.then_inc(xt_turned, 1)

            def norm(nth, st):
                pe.wait_ge(ssq_acc, K * (nth + 1))
                stat(st, mean_all[:], tmp_a[:])

            def mixer(l):
                u0, m_next = U_WIN[l], 2 * l + 1
                norm(2 * l, stat_of(l, 0))
                if l == 0:
                    with pe.Fori(0, MG) as g:
                        mod_sum(g)
                mod_sum(MG * m_next)
                pe.wait_ge(hl_done, K * (2 * l + 1))

                def trip(q):
                    for s in range(2):
                        unit_of_two(q * 2 + (u0 + s), s, h_hi, h_lo, 2 * s,
                                    lambda i: (proj_read, q * 4 + (20 * l + 2 * s + i + 1)))
                    mod_sum(q + (MG * m_next + 1))

                def gates(pair):
                    pe.wait_ge(gw_loaded, 64 * (l + 1))
                    for b in range(2):
                        j = 2 * pair + b
                        pe.wait_ge(xc_ready, J * l + j + 1)
                        for g in range(2):
                            n = 8 * l + 2 * j + g
                            if n >= 2:
                                pe.wait_ge(gate_read, n - 1)
                            nc.tensor.matmul(banks[:, 4 + g], gate_w[:, g, j], xc[:, j], start=True,
                                             stop=True).then_inc(gate_done, 1)

                def group_stats(half, j):
                    pe.wait_ge(ysq_done, 8 * l + 4 * half + j + 1)
                    stat(stat_of(l, 1 + 4 * half + j), mean_head[:], tt[:, j % 2])

                with pe.Fori(0, 2) as q:
                    trip(q)
                gates(0)
                trip(2)
                gates(1)
                trip(3)
                pe.wait_ge(gate_read, 8 * (l + 1))
                for j in range(J):
                    group_stats(0, j)
                trip(4)
                for j in range(J):
                    group_stats(1, j)
                pe.wait_ge(yl_done, 8 * (l + 1))
                with pe.Fori(0, WOUT_U // 2) as q:
                    for s in range(2):
                        unit_of_two(q * 2 + (U_WOUT[l] + s), s, y_hi, y_lo, 2 * s,
                                    lambda i: (res_read, q * 4 + (16 * l + 2 * s + i + 1)))
                    mod_sum(q + (MG * m_next + 6))

            def up(n, s):
                pe.wait_ge(lo_done, n + (U_UP + 1))
                pe.wait_ge(pair_read, n + 1)
                for w in range(2):
                    for k in range(K):
                        cols = slice(P * (K * w + k), P * (K * w + k) + P)
                        last = product(banks[:, 2 * s + w], w_hi[:, s, cols], w_lo[:, s, cols], h_hi[:, k], h_lo[:, k],
                                       k == 0, k == K - 1)
                    last.then_inc(gemm_done, 1)

            mixer(0)
            norm(1, stat_of(0, 9))
            pe.wait_ge(hl_done, K * 2)
            with pe.Fori(0, MG) as g:
                for s in range(2):
                    up(g * 2 + s, s)
                mod_sum(g + 2 * MG)
            with pe.Fori(MG, UP_U // 2) as g:
                for s in range(2):
                    up(g * 2 + s, s)
            pe.wait_ge(al_done, FB + 1)
            with pe.Fori(0, K // 2) as mm:
                for i in range(2):
                    pe.wait_ge(res_read, mm * 2 + (8 + i + 3))
                    for h in range(2):
                        pe.wait_ge(lo_done, mm * 4 + (U_DOWN + 2 * i + h + 1))
                        for f in range(FH):
                            cols = slice(P * f, P * f + P)
                            last = product(banks[:, i], w_hi[:, h, cols], w_lo[:, h, cols], act_hi[:, h * FH + f],
                                           act_lo[:, h * FH + f], h == 0 and f == 0, h == 1 and f == FH - 1)
                        last.then_inc(gemm_done, 2)
            mixer(1)

            norm(3, stat_of(1, 9))
            pe.wait_ge(hf_done, 4 * K)
            pe.wait_ge(rw_loaded, 32)
            for a in range(TT):
                for k in range(K):
                    last = nc.tensor.matmul(banks[:, 0, E * a:E * a + E], hf3[:, k, P * a:P * a + P], rw[:, k],
                                            start=(k == 0), stop=(k == K - 1))
            last.then_inc(logits_done, 1)

            def token_major(src, first, n):
                m = first + n
                if m >= 4:
                    pe.wait_ge(tok_read, m - 3)
                for q in range(4):
                    last = nc.tensor.transpose(banks[:, TOK_BANKS[n % 4], P * q:P * q + P],
                                               src[:, 4 * (n % 2) + q, P * (n // 2):P * (n // 2) + P], ident[:])
                last.then_inc(tok_turned, 1)

            for n in range(4):
                token_major(hf3, 0, n)
            pe.wait_ge(mask_ready, 1)
            mask = rt[:, 5].rearrange("p a e -> p (a e)")
            nc.tensor.matmul(banks[:, 5, 0:TT * E], before[:], mask, start=True, stop=True)
            nc.tensor.matmul(banks[:, 5, TT * E:2 * TT * E], ones_all[:], mask, start=True, stop=True).then_inc(count_done, 1)
            for n in range(4, 2 * TT):
                token_major(hf3, 0, n)
            for n in range(2 * TT):
                token_major(xT, 2 * TT, n)

            def turn_rows(i):
                pe.wait_ge(rows_in, i * 16 + 16)
                for n in range(4):
                    for q in range(4):
                        k = 4 * (n % 2) + q
                        last = nc.tensor.transpose(banks[:, (4, 5, 0, 1)[n], P * q:P * q + P],
                                                   h_rows[:, n // 2, P * k:P * k + P], ident[:])
                    last.then_inc(ht_turned, 1)

            def trip(i, tiles):
                def turn_hidden(g):
                    pe.wait_ge(hid_done, i * EG + (g + 2))
                    pe.wait_ge(at_lo_done, i * EG + (g + 1))
                    for a in range(tiles):
                        for q, f in enumerate(range(WHOLE[g], WHOLE[g + 1])):
                            last = nc.tensor.transpose(banks[:, 4 + a, P * q:P * q + P], hid[:, a, P * f:P * f + P], ident[:])
                    last.then_inc(at_turned, 1)

                pe.wait_ge(ht_lo_done, i * 4 + 4)
                for j in range(EU):
                    s = j % 2
                    pe.wait_ge(e_lo_done, i * EU + (j + 1 + RAWS))
                    if j < 2 * EG:
                        g, w = j // 2, j % 2
                        if w == 0:
                            pe.wait_ge(e_silu_done, i * EG + (g + 1))
                        else:
                            pe.wait_ge(hid_done, i * EG + (g + 1))
                            if g == 0:
                                pe.wait_ge(y_read, i + 1)
                        for a in range(tiles):
                            for k in range(K):
                                cols = slice(EC * k, EC * k + EC)
                                part = (slice(None), k, slice(P * a, P * a + P))
                                last = product(banks[:, 2 * w + a, 0:EC], ht_hi[part], ht_lo[part], e_hi[:, s, cols],
                                               e_lo[:, s, cols], k == 0, k == K - 1)
                    else:
                        if j == 2 * EG:
                            pe.wait_ge(y_read, i + 1)
                        f0, f1 = W2_CUT[j - 2 * EG], W2_CUT[j - 2 * EG + 1]
                        pe.wait_ge(at_lo_done, i * EG + (4 if j < 10 else 5))
                        for a in range(tiles):
                            for half in range(2):
                                for f in range(f0, f1):
                                    cols = slice(D * (f - f0) + 512 * half, D * (f - f0) + 512 * half + 512)
                                    part = (slice(None), f, slice(P * a, P * a + P))
                                    last = product(banks[:, (6, 2)[a] + half], at_hi[part], at_lo[part], e_hi[:, s, cols],
                                                   e_lo[:, s, cols], f == 0, f == FEB - 1)
                    last.then_inc(e_used, 1)
                    if j in (3, 5, 7):
                        turn_hidden((j - 3) // 2)
                    if j == 8:
                        turn_hidden(3)
                    if j == 9:
                        pe.wait_ge(at_lo_done, i * EG + (EG + 1))
                        turn_rows(i + 1)

            pe.sem_inc(e_used, 2)
            pe.wait_ge(sorted_stored, 16 * 2 * TT)
            pe.wait_ge(tok_read, 4 * TT)
            pe.wait_ge(table_ready, 1)
            turn_rows(0)
            trips = pe.value_load(table[0:1, 3, 0:1], min_val=1, max_val=MAX_TRIPS)
            with pe.Fori(0, trips) as i:
                two = pe.value_load(table[0:1, 2, bass.ds(i, 1)], min_val=0, max_val=1)
                with pe.If(two > 0):
                    trip(i, 2)
                with pe.Else():
                    trip(i, 1)
                pe.nop()
            pe.wait_ge(y_read, trips + 1)
            for which in range(2):
                for k in range(K):
                    pe.wait_ge(diag_ready, K * which + k + 1)
                    last = nc.tensor.matmul(banks[:, 2 * which + k // 4, P * (k % 4):P * (k % 4) + P], ones_all[:],
                                            diag[:, which, k], start=True, stop=True)
                    if k % 4 == 3:
                        last.then_inc(row_done, 1)
    return None


INPUTS = ["x", "c", "mix_norm", "mix_mod_w", "mix_mod_b", "w_in", "lru_conv_w", "lru_conv_b", "lru_wa", "lru_ba",
          "lru_wi", "lru_bi", "lru_lambda", "sc_conv_w", "gn_lru", "gn_sc", "w_out", "ffn_norm", "ffn_mod_w",
          "ffn_mod_b", "dense_w1", "dense_w3", "dense_w2", "router_w", "router_b", "exp_w1", "exp_w3", "exp_w2",
          "final_norm"]


def kernel(**inputs):
    import numpy as np
    import concourse.bacc as bacc
    from concourse.bass_utils import run_bass_kernel_spmd

    nc = bacc.Bacc("TRN2", target_bir_lowering=False, num_devices=1)
    arrays = {f"in_{n}": np.ascontiguousarray(inputs[n]) for n in INPUTS}
    args = {n: nc.dram_tensor(f"in_{n}", arrays[f"in_{n}"].shape, F32, kind="ExternalInput").ap() for n in INPUTS}
    out = nc.dram_tensor("out", arrays["in_x"].shape, F32, kind="ExternalOutput")
    trunk_kernel(nc, out=out.ap(), **args)
    result = run_bass_kernel_spmd(nc, [arrays], core_ids=[0])
    return result.results[0]["out"]
```

```python
from contextlib import ExitStack

import concourse.bass as bass
from concourse import mybir

F32 = mybir.dt.float32
F32R = mybir.dt.float32r
I32 = mybir.dt.int32
U32 = mybir.dt.uint32
ALU = mybir.AluOpType
ACT = mybir.ActivationFunctionType
AX = mybir.AxisListType

P = 128
EPS = 1e-6
LRU_C = 8.0


def trunk_kernel(nc, x, c, mix_norm, mix_mod_w, mix_mod_b, w_in, lru_conv_w, lru_conv_b, lru_wa, lru_ba,
                 lru_wi, lru_bi, lru_lambda, sc_conv_w, gn_lru, gn_sc, w_out, ffn_norm, ffn_mod_w,
                 ffn_mod_b, dense_w1, dense_w3, dense_w2, router_w, router_b, exp_w1, exp_w3, exp_w2,
                 final_norm, out):
    _, T, D = x.shape
    DEPTH = w_in.shape[0]
    K = D // P
    TT = T // P
    DL = lru_conv_w.shape[2]
    J = DL // P
    LT, ST = lru_conv_w.shape[1], sc_conv_w.shape[1]
    HD = lru_wa.shape[2]
    FF = dense_w1.shape[2]
    FB = FF // P
    assert T == 512 and K == 8 and J == 4 and HD * 2 == P and DEPTH == 2 and FB == 22

    E = router_w.shape[2]
    FE = exp_w1.shape[3]
    FEB = FE // P
    EG = 4
    EC = FE // EG
    assert E == 8 and FE % P == 0 and FE % EG == 0 and EC <= 512 and D == 1024
    MAX_TILES = 2 * T // P + E - 1
    MIN_TILES = 2 * T // P
    MAX_TRIPS = 2 * T // (2 * P) + E - 1
    TR = MAX_TRIPS + 1
    W2_CUT = [0, 3, 6, 9, FEB]
    WHOLE = [0] + [(g + 1) * EC // P for g in range(EG)]
    EU = 2 * EG + len(W2_CUT) - 1
    EUF = max(K * EC, 3 * D)
    RAWS = 4
    assert EU % RAWS == 0 and EU % 2 == 0 and max(b - a for a, b in zip(WHOLE, WHOLE[1:])) * P <= 512

    UF = 2048
    WIN_U = w_in.shape[2] // (2 * P)
    WOUT_U = D // (2 * P)
    UP_U = FB
    DOWN_U = 2 * K
    U_WIN, U_WOUT = [0, 0], [0, 0]
    U_WOUT[0] = WIN_U
    U_UP = U_WOUT[0] + WOUT_U
    U_DOWN = U_UP + UP_U
    U_WIN[1] = U_DOWN + DOWN_U
    U_WOUT[1] = U_WIN[1] + WIN_U
    U_END = U_WOUT[1] + WOUT_U
    MC = 3 * P
    MG = 3 * D // MC
    KH = K // 2

    with ExitStack() as ctx:
        def sem(name):
            return ctx.enter_context(nc.semaphore(name))

        top = [-(-nc.sbuf_base // 32) * 32]

        def at(name, shape, dt, offset):
            return nc.alloc_sbuf_tensor_at(name, shape, dt, offset=offset)

        def place(name, shape, dt=F32):
            size = 4
            for n in shape[1:]:
                size *= n
            t = at(name, shape, dt, top[0])
            top[0] += -(-size // 32) * 32
            assert top[0] <= nc.sbuf_usable_end, (name, top[0])
            return t

        ident = place("ident", [P, P])
        spread = place("spread", [P, J, P])
        GR = 2 * J
        head_sel = place("head_sel", [P, 2 * GR])
        PT1R = 4 * 24 + 4 * K
        par1 = place("par1", [P, PT1R])
        R_CW, R_CB, R_BA, R_BI, R_LAM, R_SW, R_GL, R_GS, R_C, R_FN, R_END = (
            0, 32, 40, 48, 56, 64, 88, 96, 104, 112, 120)
        par2 = place("par2", [P, R_END])
        eps = place("eps", [P, 1])
        ones = place("ones", [P, 1])
        silu_c = place("silu_c", [P, K])
        ones_all = place("ones_all", [P, P])
        before = place("before", [P, P])
        rw = place("rw", [P, K, E])
        rb = place("rb", [P, E])
        iota_i = place("iota_i", [P, 16], I32)
        iota_f = place("iota_f", [P, 16])
        pick_w = place("pick_w", [P, 2, TT])
        slots_i = place("slots_i", [P, 2, TT], U32)
        table = place("table", [P, 4, TR], I32)
        decay = place("decay", [P, 2, 2 * J])
        small = place("small", [P, 6, 2 * J])
        mods = place("mods", [P, 4, 24])
        mod_gain = place("mod_gain", [P, 4, K])
        tmp_a = place("tmp_a", [P, T])
        tmp_b = place("tmp_b", [P, T])
        xT = place("xT", [P, K, T])
        dense_at = top[0]
        h_hi = place("h_hi", [P, K, T], F32R)
        h_lo = place("h_lo", [P, K, T], F32R)
        mod_acc = place("mod_acc", [P, MC])
        mod_buf = place("mod_buf", [P, 2, KH, MC])
        raw = place("raw", [P, 2, UF])
        w_hi = place("w_hi", [P, 2, UF], F32R)
        w_lo = place("w_lo", [P, 2, UF], F32R)
        area = top[0]
        act_hi = place("act_hi", [P, FB, T], F32R)
        act_lo = place("act_lo", [P, FB, T], F32R)
        top[0] = area
        y_hi = place("y_hi", [P, K, T], F32R)
        y_lo = place("y_lo", [P, K, T], F32R)
        gate_w = place("gate_w", [P, 2, J, P])
        XPW = LT - 1 + T
        xpad = place("xpad", [P, J, XPW + 1])
        xc = place("xc", [P, J, T])
        gel = place("gel", [P, J, T])
        bsc = place("bsc", [P, J, T])
        tr = place("tr", [P, 2, T])
        ti = place("ti", [P, 2, T])
        tt = place("tt", [P, 2, T])
        ta = place("ta", [P, 2, T])
        CXW = ST - 1 + T
        cxpad = place("cxpad", [P, 2, CXW])
        csc = at("csc", [P, J, T], F32, area + 2 * 4 * K * T + 4 * 2 * J * P)
        hf = at("hf", [P, K, T], F32, area + 2 * 4 * K * T + 4 * 2 * J * P)
        rstd = tmp_b
        xrow = at("xrow", [P, TT, D], F32, area)
        rows = at("rows", [P, 2, P], F32, dense_at + 2 * 4 * K * MC)
        first_at = area + 4 * TT * D
        mod_first = [at(f"mod_first{g}", [P, K, MC], F32,
                        dense_at + 4 * K * MC * g if g < 2 else first_at + 4 * K * MC * (g - 2)) for g in range(MG)]
        assert 2 * 4 * K * MC + 4 * 2 * P <= 2 * 4 * K * T and first_at + 4 * K * MC * (MG - 2) <= nc.sbuf_usable_end

        ZT = 2 * KH * MC // D
        ZEROS = -(-(MAX_TILES + 1) // ZT) + -(-(MAX_TILES + 1 - MIN_TILES) // ZT)
        top[0] = dense_at
        x_tok = place("x_tok", [P, TT, D])
        ht_hi = place("ht_hi", [P, K, 2 * P], F32R)
        ht_lo = place("ht_lo", [P, K, 2 * P], F32R)
        e_raw = place("e_raw", [P, RAWS, EUF])
        e_hi = place("e_hi", [P, 2, EUF], F32R)
        e_lo = place("e_lo", [P, 2, EUF], F32R)
        at_at = top[0]
        at_hi = place("at_hi", [P, FEB, 2 * P], F32R)
        at_lo = place("at_lo", [P, FEB, 2 * P], F32R)
        rows_at = top[0]
        h_rows = place("h_rows", [P, 2, D])
        hid = place("hid", [P, 2, FE])
        e_silu = place("e_silu", [P, 2, EC])
        y_rows = place("y_rows", [P, 2, D])
        hf3 = at("hf3", [P, K, T], F32, at_at)
        h_tok = at("h_tok", [P, TT, D], F32, rows_at)
        rstd3 = at("rstd3", [P, T], F32, at_at + 4 * K * T)
        route_at = at_at + 4 * K * T + 4 * T
        rt = at("rt", [P, 16, TT, E], F32, route_at)
        rt_u = at("rt_u", [P, TT, E], U32, route_at + 4 * 16 * TT * E)
        ex = at("ex", [P, 16, E], F32, route_at + 4 * 17 * TT * E)
        tb = at("tb", [P, 8, TR], F32, route_at + 4 * 17 * TT * E + 4 * 16 * E)
        raw_at = dense_at + 4 * TT * D + 2 * 4 * K * 2 * P
        picked = at("picked", [P, 2, 2, D], F32, raw_at)
        gate_row = at("gate_row", [P, D], F32, raw_at + 16 * D)
        gain_row = at("gain_row", [P, D], F32, raw_at + 20 * D)
        diag = at("diag", [P, 2, K, P], F32, raw_at + 24 * D)
        mix = at("mix", [P, 2, D], F32, raw_at + 32 * D)
        sums = at("sums", [P, 3, TT], F32, raw_at + 40 * D)

        h_sorted = nc.dram_tensor("h_sorted", ((MAX_TILES + 1) * P, D), F32)
        y_sorted = nc.dram_tensor("y_sorted", ((MAX_TILES + 1) * P, D), F32)

        banks = ctx.enter_context(nc.psum_tensor("banks", [P, 8, 512], F32))
        MODS_BANK = 7
        STAT_BANK = 6
        GROUP_BANK = 5
        SPREAD_BANKS = (4, 6)
        TOK_BANKS = (1, 2, 3, 7)

        const_ready = sem("const_ready")
        x_loaded = sem("x_loaded")
        rows_loaded = sem("rows_loaded")
        rows_turned = sem("rows_turned")
        par_ready = sem("par_ready")
        vec_link = sem("vec_link")
        act_link = sem("act_link")
        silu_ready = sem("silu_ready")
        decay_step = sem("decay_step")
        decay_ready = sem("decay_ready")
        xt_turned = sem("xt_turned")
        xt_read = sem("xt_read")
        raw_loaded = [sem("raw_loaded0"), sem("raw_loaded1")]
        hi_done = sem("hi_done")
        lo_done = sem("lo_done")
        gemm_done = sem("gemm_done")
        proj_read = sem("proj_read")
        res_read = sem("res_read")
        pair_read = sem("pair_read")
        mod_loaded = [sem("mod_loaded0"), sem("mod_loaded1")]
        mod_first_in = [sem(f"mod_first_in{g}") for g in range(MG)]
        mod_step = sem("mod_step")
        mod_part = sem("mod_part")
        mod_mm = sem("mod_mm")
        mods_ready = sem("mods_ready")
        x_upd = sem("x_upd")
        sq_done = sem("sq_done")
        ssq_acc = sem("ssq_acc")
        stat_done = sem("stat_done")
        stat_read = sem("stat_read")
        rstd_ready = sem("rstd_ready")
        xr_ready = sem("xr_ready")
        hf_done = sem("hf_done")
        hh_done = sem("hh_done")
        hl_done = sem("hl_done")
        gw_zero = sem("gw_zero")
        gw_loaded = sem("gw_loaded")
        xpad_ready = sem("xpad_ready")
        pad_ready = sem("pad_ready")
        xc_ready = sem("xc_ready")
        gate_done = sem("gate_done")
        gate_read = sem("gate_read")
        ta_ready = sem("ta_ready")
        v_ready = sem("v_ready")
        s_ready = sem("s_ready")
        scan_done = sem("scan_done")
        y_ready = sem("y_ready")
        ysq_done = sem("ysq_done")
        gsum_done = sem("gsum_done")
        groot_done = sem("groot_done")
        grstd_done = sem("grstd_done")
        gspread_done = sem("gspread_done")
        yn_done = sem("yn_done")
        yh_done = sem("yh_done")
        yl_done = sem("yl_done")
        silu_done = sem("silu_done")
        prod_done = sem("prod_done")
        ah_done = sem("ah_done")
        al_done = sem("al_done")
        out_stored = [sem("out_stored0"), sem("out_stored1")]
        rw_loaded = sem("rw_loaded")
        iota_ready = sem("iota_ready")
        zeros_ready = sem("zeros_ready")
        zeros_stored = sem("zeros_stored")
        logits_done = sem("logits_done")
        tok_turned = sem("tok_turned")
        tok_read = sem("tok_read")
        mask_ready = sem("mask_ready")
        diff_ready = sem("diff_ready")
        diff_exp = sem("diff_exp")
        count_done = sem("count_done")
        slots_ready = sem("slots_ready")
        table_ready = sem("table_ready")
        sorted_stored = sem("sorted_stored")
        rows_in = sem("rows_in")
        ht_turned = sem("ht_turned")
        ht_hi_done = sem("ht_hi_done")
        ht_lo_done = sem("ht_lo_done")
        e_loaded = [sem(f"e_loaded{i}") for i in range(RAWS)]
        e_hi_done = sem("e_hi_done")
        e_lo_done = sem("e_lo_done")
        e_used = sem("e_used")
        e_silu_done = sem("e_silu_done")
        hid_done = sem("hid_done")
        at_turned = sem("at_turned")
        at_hi_done = sem("at_hi_done")
        at_lo_done = sem("at_lo_done")
        y_read = sem("y_read")
        y_stored = sem("y_stored")
        y_free = sem("y_free")
        trips_over = sem("trips_over")
        diag_ready = sem("diag_ready")
        row_done = sem("row_done")
        row_ready = sem("row_ready")
        picked_in = [sem("picked_in0"), sem("picked_in1")]
        mix_done = sem("mix_done")
        xo_ready = sem("xo_ready")
        osum_ready = sem("osum_ready")
        oroot_ready = sem("oroot_ready")
        o_ready = sem("o_ready")

        win_v = [w_in[l].rearrange("(k p) n -> p k n", p=P) for l in range(2)]
        wout_v = [w_out[l].rearrange("(k p) n -> p k n", p=P) for l in range(2)]
        w1_v = dense_w1[0].rearrange("(k p) n -> p k n", p=P)
        w3_v = dense_w3[0].rearrange("(k p) n -> p k n", p=P)
        w2_v = dense_w2[0].rearrange("(h f p) n -> p h f n", p=P, h=2)
        mod_w = [mix_mod_w[0], ffn_mod_w[0], mix_mod_w[1], ffn_mod_w[1]]
        mod_b = [mix_mod_b[0], ffn_mod_b[0], mix_mod_b[1], ffn_mod_b[1]]
        e1_v = exp_w1[0].rearrange("e (k p) n -> e p k n", p=P)
        e3_v = exp_w3[0].rearrange("e (k p) n -> e p k n", p=P)
        e2_v = exp_w2[0].rearrange("e (f p) n -> e p f n", p=P)
        hs_v = h_sorted.ap().rearrange("(t p) d -> p t d", p=P)
        ys_v = y_sorted.ap().rearrange("(t p) d -> p t d", p=P)
        FH = FB // 2
        DOWN_F = FH * P

        def k_of(t, s, n=K):
            return t[:, s, 0:n * (UF // K if n == K else P)].rearrange("p (k n) -> p k n", k=n)

        def block_of(t, n):
            return t[:, bass.ds(n, 1), :].rearrange("p a t -> p (a t)")

        block = ctx.enter_context(nc.Block())

        @block.sync
        def _(sp):
            sp.dma_start(rows[0:24, 0, :], mod_b[0].rearrange("(r q) -> r q", q=P)).then_inc(rows_loaded, 16)
            for m in range(1, 4):
                sp.dma_start(rows[24 * m:24 * m + 24, 0, :],
                             mod_b[m].rearrange("(r q) -> r q", q=P)).then_inc(rows_loaded, 16)
            sp.dma_start(rows[96:96 + 2 * K, 0, :],
                         mix_norm.rearrange("l (r q) -> (l r) q", q=P)).then_inc(rows_loaded, 16)
            sp.dma_start(rows[96 + 2 * K:96 + 4 * K, 0, :],
                         ffn_norm.rearrange("l (r q) -> (l r) q", q=P)).then_inc(rows_loaded, 16)
            for at_row, src in ((R_CW, lru_conv_w.rearrange("l t (r q) -> (l t r) q", q=P)),
                                (R_CB, lru_conv_b.rearrange("l (r q) -> (l r) q", q=P)),
                                (R_BA, lru_ba.rearrange("l (r h) q -> (l r) (h q)", h=2)),
                                (R_BI, lru_bi.rearrange("l (r h) q -> (l r) (h q)", h=2)),
                                (R_LAM, lru_lambda.rearrange("l (r q) -> (l r) q", q=P)),
                                (R_SW, sc_conv_w.rearrange("l t (r q) -> (l t r) q", q=P)),
                                (R_GL, gn_lru.rearrange("l (r q) -> (l r) q", q=P)),
                                (R_GS, gn_sc.rearrange("l (r q) -> (l r) q", q=P)),
                                (R_C, c.rearrange("b (r q) -> (b r) q", q=P)),
                                (R_FN, final_norm.rearrange("(r q) -> r q", q=P))):
                sp.dma_start(rows[at_row:at_row + src.shape[0], 1, :], src).then_inc(rows_loaded, 16)
            sp.dma_start(xrow[:], x[0].rearrange("(a p) d -> p a d", p=P)).then_inc(x_loaded, 16)

            def first_loads(groups):
                view = mod_w[0].rearrange("(k p) n -> p k n", p=P)
                for g in groups:
                    sp.dma_start(mod_first[g][:], view[:, :, g * MC:(g + 1) * MC]).then_inc(mod_first_in[g], 16)

            def free(u):
                if not isinstance(u, int) or u >= 2:
                    sp.wait_ge(lo_done, u - 1)

            def load_cols(view, col, s, u):
                free(u)
                sp.dma_start(k_of(raw, s), view[:, :, bass.ds(col, 2 * P)]).then_inc(raw_loaded[s], 16)

            def mixer_loads(l):
                if l == 0:
                    first_loads(range(MG // 2))
                for s in range(2):
                    load_cols(win_v[l], 2 * P * s, s, U_WIN[l] + s)
                if l == 0:
                    first_loads(range(MG // 2, MG))
                with sp.Fori(1, WIN_U // 2) as q:
                    for s in range(2):
                        load_cols(win_v[l], q * 4 * P + 2 * P * s, s, q * 2 + (U_WIN[l] + s))
                with sp.Fori(0, WOUT_U // 2) as q:
                    for s in range(2):
                        load_cols(wout_v[l], q * 4 * P + 2 * P * s, s, q * 2 + (U_WOUT[l] + s))

            mixer_loads(0)
            with sp.Fori(0, UP_U // 2) as g:
                for s in range(2):
                    free(g * 2 + (U_UP + s))
                    pair = raw[:, s, :].rearrange("p (w k n) -> p w k n", w=2, k=K)
                    for w, view in enumerate((w1_v, w3_v)):
                        sp.dma_start(pair[:, w], view[:, :, bass.ds(g * 2 * P + P * s, P)]).then_inc(raw_loaded[s], 16)
            with sp.Fori(0, K) as m:
                for s in range(2):
                    free(m * 2 + (U_DOWN + s))
                    sp.dma_start(raw[:, s, 0:DOWN_F].rearrange("p (f n) -> p f n", f=FH),
                                 w2_v[:, s, :, bass.ds(m * P, P)]).then_inc(raw_loaded[s], 16)
            mixer_loads(1)

            sp.wait_ge(table_ready, 1)
            sp.wait_ge(zeros_stored, 16 * ZEROS)
            trips = sp.value_load(table[0:1, 3, 0:1], min_val=1, max_val=MAX_TRIPS)
            with sp.Fori(0, trips) as i:
                e = sp.value_load(table[0:1, 0, bass.ds(i, 1)], min_val=0, max_val=E - 1)
                for j in range(EU):
                    sp.wait_ge(e_lo_done, i * EU + (j + 1))
                    if j < 2 * EG:
                        view = e1_v if j % 2 == 0 else e3_v
                        src = view[bass.ds(e, 1), :, :, EC * (j // 2):EC * (j // 2 + 1)].rearrange("e p k n -> p (e k) n")
                        dst = e_raw[:, j % RAWS, 0:K * EC].rearrange("p (k n) -> p k n", k=K)
                    else:
                        f0, f1 = W2_CUT[j - 2 * EG], W2_CUT[j - 2 * EG + 1]
                        src = e2_v[bass.ds(e, 1), :, f0:f1, :].rearrange("e p f n -> p (e f) n")
                        dst = e_raw[:, j % RAWS, 0:(f1 - f0) * D].rearrange("p (f n) -> p f n", n=D)
                    sp.dma_start(dst, src).then_inc(e_loaded[j % RAWS], 16)
            for a in range(TT):
                sp.wait_ge(o_ready, a + 1)
                sp.dma_start(out[0, a * P:(a + 1) * P, :], mix[:, a % 2]).then_inc(out_stored[a % 2], 16)
            for n in range(2):
                sp.wait_ge(out_stored[n], 16 * TT // 2)

        @block.gpsimd
        def _(pool):
            made = [0]

            def make(ins):
                made[0] += 1
                ins.then_inc(const_ready, 1)
                pool.wait_ge(const_ready, made[0])

            make(nc.gpsimd.memset(spread[:], 1.0))
            flat = spread[:].rearrange("r j p -> r (j p)")
            make(nc.gpsimd.affine_select(out=flat, in_=flat, compare_op=ALU.is_ge, fill=0.0, base=0,
                                         pattern=[[1, J * P]], channel_multiplier=-HD))
            make(nc.gpsimd.affine_select(out=flat, in_=flat, compare_op=ALU.is_ge, fill=0.0, base=HD - 1,
                                         pattern=[[-1, J * P]], channel_multiplier=HD))
            make(nc.gpsimd.memset(ident[:], 0.0))
            make(nc.gpsimd.affine_select(out=ident[:], in_=ident[:], compare_op=ALU.not_equal, fill=1.0, base=0,
                                         pattern=[[-1, P]], channel_multiplier=1))
            make(nc.gpsimd.memset(head_sel[:], 0.0))
            for h in range(2):
                part = slice(HD * h, HD * h + HD)
                make(nc.gpsimd.memset(head_sel[part, GR - 2 + h:GR - 1 + h], 1.0 / HD))
            make(nc.gpsimd.memset(eps[:], EPS))
            make(nc.gpsimd.memset(ones[:], 1.0))
            make(nc.gpsimd.memset(ones_all[:], 1.0))
            make(nc.gpsimd.memset(before[:], 1.0))
            make(nc.gpsimd.affine_select(out=before[:], in_=before[:], compare_op=ALU.is_gt, fill=0.0, base=0,
                                         pattern=[[1, P]], channel_multiplier=-1))
            nc.gpsimd.iota(iota_i[:], pattern=[[1, 16]], base=0, channel_multiplier=0).then_inc(iota_ready, 1)
            pool.dma_start(rw[:], router_w[0].rearrange("(k p) e -> p k e", p=P)).then_inc(rw_loaded, 16)
            pool.dma_start(rb[:], router_b[0:1, :].partition_broadcast(P)).then_inc(rw_loaded, 16)

            def mod_load(m, g, h):
                view = mod_w[m].rearrange("(h k p) n -> p h k n", p=P, h=2)
                pool.dma_start(mod_buf[:, h], view[:, h, :, bass.ds(g * MC, MC)]).then_inc(mod_loaded[h], 16)

            def mod_group(n, following):
                q = n - MG
                steps = [0]

                def step(ins):
                    steps[0] += 1
                    ins.then_inc(mod_part, 1)
                    pool.wait_ge(mod_part, q * 7 + steps[0])

                for h in range(2):
                    part = mod_buf[:, h]
                    scalars = silu_c[:, KH * h:KH * h + KH].unsqueeze(2).to_broadcast([P, KH, MC])
                    pool.wait_ge(mod_loaded[h], q * 16 + 16)
                    step(nc.gpsimd.tensor_tensor(part, part, scalars, ALU.mult))
                    step(nc.gpsimd.tensor_tensor(part[:, 0:2], part[:, 0:2], part[:, 2:4], ALU.add))
                    if h == 0:
                        pool.wait_ge(mod_mm, n + 1)
                        step(nc.gpsimd.tensor_tensor(mod_acc[:], part[:, 0], part[:, 1], ALU.add))
                    else:
                        step(nc.gpsimd.tensor_tensor(part[:, 0], part[:, 0], part[:, 1], ALU.add))
                        step(nc.gpsimd.tensor_tensor(mod_acc[:], mod_acc[:], part[:, 0], ALU.add))
                    following(h)

            def mod_groups(m, first, last):
                end = min(last, MG - 1)
                if end - first == 1:
                    mod_group(MG * m + first, lambda h: mod_load(m, first + 1, h))
                else:
                    with pool.Fori(first, end) as g:
                        mod_group(g + MG * m, lambda h: mod_load(m, g + 1, h))
                if last == MG:
                    mod_group(MG * m + MG - 1, (lambda h: mod_load(m + 1, 0, h)) if m < 3 else (lambda h: None))

            def gate_loads(l):
                if l:
                    pool.wait_ge(gemm_done, 2 * U_WIN[1])
                    pool.wait_ge(hl_done, K * 3)
                else:
                    pool.wait_ge(mods_ready, 1)
                nc.gpsimd.memset(gate_w[:], 0.0).then_inc(gw_zero, 1)
                pool.wait_ge(gw_zero, l + 1)
                for g, w in enumerate((lru_wa, lru_wi)):
                    v = w[l].rearrange("(j h) i o -> h i j o", h=2)
                    for h in range(2):
                        part = slice(HD * h, HD * h + HD)
                        pool.dma_start(gate_w[part, g, :, part], v[h]).then_inc(gw_loaded, 16)

            def pads(l):
                pool.wait_ge(hl_done, K * (2 * l + 1))
                nc.gpsimd.memset(xpad[:, :, 0:LT - 1], 0.0).then_inc(pad_ready, 1)
                pool.wait_ge(pad_ready, 2 * l + 1)
                nc.gpsimd.memset(cxpad[:, :, 0:ST - 1], 0.0).then_inc(pad_ready, 1)
                pool.wait_ge(pad_ready, 2 * l + 2)

            for h in range(2):
                mod_load(1, 0, h)
            pool.wait_ge(silu_ready, 1)
            for l in range(2):
                mod_groups(2 * l + 1, 0, 1)
                gate_loads(l)
                pads(l)
                mod_groups(2 * l + 1, 1, MG)
                if l == 0:
                    mod_groups(2, 0, MG)

            nc.gpsimd.memset(mod_buf[:], 0.0).then_inc(zeros_ready, 1)
            pool.wait_ge(zeros_ready, 1)
            zeros = mod_buf[:].rearrange("p h k n -> p (h k n)")
            for view, t0 in ((hs_v, 0), (ys_v, MIN_TILES)):
                for t in range(t0, MAX_TILES + 1, ZT):
                    n = min(ZT, MAX_TILES + 1 - t)
                    pool.dma_start(view[:, t:t + n, :], zeros[:, 0:n * D].rearrange("p (t d) -> p t d", t=n)
                                   ).then_inc(zeros_stored, 16)
            pool.wait_ge(zeros_stored, 16 * ZEROS)
            pool.wait_ge(slots_ready, 1)
            pool.wait_ge(tok_read, 2 * TT)
            for a in range(TT):
                for which in range(2):
                    pool.indirect_dma_start(
                        out=h_sorted.ap(), out_offset=bass.IndirectOffsetOnAxis(ap=slots_i[:, which, a:a + 1], axis=0),
                        in_=h_tok[:, a, :], in_offset=None).then_inc(sorted_stored, 16)
            pool.wait_ge(sorted_stored, 16 * 2 * TT)
            pool.wait_ge(table_ready, 1)

            def load_rows(i):
                t0 = pool.value_load(table[0:1, 1, bass.ds(i, 1)], min_val=0, max_val=MAX_TILES - 1)
                pool.dma_start(h_rows[:], hs_v[:, bass.ds(t0, 2), :]).then_inc(rows_in, 16)

            pool.sem_inc(y_free, 1)
            load_rows(0)
            trips = pool.value_load(table[0:1, 3, 0:1], min_val=1, max_val=MAX_TRIPS)
            with pool.Fori(0, trips) as i:
                pool.wait_ge(ht_turned, i * 4 + 4)
                load_rows(i + 1)
                pool.wait_ge(y_read, i + 2)
                t0 = pool.value_load(table[0:1, 1, bass.ds(i, 1)], min_val=0, max_val=MAX_TILES - 1)
                two = pool.value_load(table[0:1, 2, bass.ds(i, 1)], min_val=0, max_val=1)
                with pool.If(two > 0):
                    pool.dma_start(ys_v[:, bass.ds(t0, 2), :], y_rows[:]).then_inc(y_stored, 16)
                with pool.Else():
                    pool.dma_start(ys_v[:, bass.ds(t0, 1), :], y_rows[:, 0:1]).then_inc(y_stored, 16)
                pool.nop()
                pool.wait_ge(y_stored, i * 16 + 16)
                pool.sem_inc(y_free, 1)
            pool.wait_ge(rows_in, trips * 16 + 16)
            pool.sem_inc(trips_over, 1)
            pool.wait_ge(trips_over, 1)
            for a in range(TT):
                if a >= 2:
                    pool.wait_ge(xo_ready, a - 1)
                for which in range(2):
                    pool.indirect_dma_start(
                        out=picked[:, a % 2, which, :], out_offset=None, in_=y_sorted.ap(),
                        in_offset=bass.IndirectOffsetOnAxis(ap=slots_i[:, which, a:a + 1], axis=0)
                    ).then_inc(picked_in[a % 2], 16)

        BASE = {}
        BASE["win0"] = 0
        BASE["wout0"] = BASE["win0"] + 16 * WIN_U // 2
        BASE["up"] = BASE["wout0"] + 16 * WOUT_U // 2
        BASE["down"] = BASE["up"] + 32 * UP_U // 2
        BASE["win1"] = BASE["down"] + 16 * DOWN_U // 2
        BASE["wout1"] = BASE["win1"] + 16 * WIN_U // 2
        PHASES = [("win0", U_WIN[0], WIN_U), ("wout0", U_WOUT[0], WOUT_U), ("up", U_UP, UP_U),
                  ("down", U_DOWN, DOWN_U), ("win1", U_WIN[1], WIN_U), ("wout1", U_WOUT[1], WOUT_U)]

        def unit_info(u):
            for name, first, n in PHASES:
                if first <= u < first + n:
                    per = 32 if name == "up" else 16
                    return BASE[name] + per * ((u - first) // 2 + 1), DOWN_F if name == "down" else UF
            return None

        @block.scalar
        def _(act):
            links = [0]

            def link(ins):
                links[0] += 1
                ins.then_inc(act_link, 1)
                act.wait_ge(act_link, links[0])

            def split(u, s, loaded=None, n=None):
                if loaded is None:
                    if u >= U_END:
                        return
                    loaded, n = unit_info(u)
                act.wait_ge(raw_loaded[s], loaded)
                if not isinstance(u, int) or u >= 2:
                    act.wait_ge(gemm_done, (u - 1) * 2)
                nc.scalar.activation(w_hi[:, s, 0:n], raw[:, s, 0:n], ACT.Copy).then_inc(hi_done, 1)

            act.sem_inc(proj_read, 4)
            act.sem_inc(ah_done, 1)
            act.sem_inc(e_silu_done, 1)
            act.wait_ge(par_ready, 2)
            nc.scalar.activation(silu_c[:], par2[:, R_C:R_C + K], ACT.Silu).then_inc(silu_ready, 1)
            link(nc.scalar.activation(small[:, 0], par2[:, R_LAM:R_LAM + 2 * J], ACT.Abs))
            nc.scalar.activation(small[:, 1], small[:, 0], ACT.Exp, scale=-1.0).then_inc(decay_step, 1)

            def square(n):
                act.wait_ge(x_upd, n + 1)
                if n >= 1:
                    act.wait_ge(ssq_acc, n)
                nc.scalar.activation(tmp_b[:], xT[:, n % K], ACT.Square).then_inc(sq_done, 1)

            for k in range(K):
                act.wait_ge(xt_turned, k + 1)
                nc.scalar.activation(xT[:, k], banks[:, k % 4], ACT.Copy).then_inc(x_upd, 1)
                square(k)
            split(0, 0)
            split(1, 1)

            def norm(nth):
                act.wait_ge(stat_done, nth + 1)
                nc.scalar.activation(rstd[:], banks[:, STAT_BANK], ACT.Sqrt, bias=eps[:],
                                     scale=1.0 / D).then_inc(stat_read, 1)
                act.wait_ge(mods_ready, nth + 1)

                def modulate(k):
                    act.wait_ge(xr_ready, K * nth + k + 1)
                    nc.scalar.activation(hf[:, k], hf[:, k], ACT.Identity, bias=mods[:, nth, k:k + 1],
                                         scale=mod_gain[:, nth, k:k + 1]).then_inc(hf_done, 1)

                modulate(0)
                for k in range(K):
                    if k + 1 < K:
                        modulate(k + 1)
                    act.wait_ge(hf_done, K * nth + k + 1)
                    nc.scalar.activation(h_hi[:, k], hf[:, k], ACT.Copy).then_inc(hh_done, 1)

            def mixer(l):
                u0 = U_WIN[l]

                def evacuate(u, i):
                    q, j = u // 2, 2 * (u % 2) + i
                    act.wait_ge(gemm_done, 2 * (u0 + u) + 1 + i)
                    ps = banks[:, j]
                    if q == 0:
                        nc.scalar.activation(xpad[:, j, LT - 1:LT - 1 + T], ps, ACT.Copy).then_inc(xpad_ready, 1)
                        act.wait_ge(xpad_ready, J * l + j + 1)
                        act.sem_inc(proj_read, 1)
                    elif q == 1:
                        nc.scalar.activation(gel[:, j], ps, ACT.Gelu_apprx_tanh).then_inc(proj_read, 1)
                    elif q == 2:
                        nc.scalar.activation(bsc[:, j], ps, ACT.Copy).then_inc(proj_read, 1)
                    elif q == 3:
                        act.wait_ge(xc_ready, J * (l + 1))
                        nc.scalar.activation(csc[:, j], ps, ACT.Copy).then_inc(proj_read, 1)

                def gates(pair):
                    for b in range(2):
                        j = 2 * pair + b
                        n = 8 * l + 2 * j
                        if pair:
                            act.wait_ge(scan_done, J * l + b + 1)
                        act.wait_ge(gate_done, n + 1)
                        nc.scalar.activation(tr[:, b], banks[:, 4], ACT.Sigmoid,
                                             bias=par2[:, R_BA + J * l + j:R_BA + J * l + j + 1]).then_inc(gate_read, 1)
                        act.wait_ge(gate_done, n + 2)
                        nc.scalar.activation(ti[:, b], banks[:, 5], ACT.Sigmoid,
                                             bias=par2[:, R_BI + J * l + j:R_BI + J * l + j + 1]).then_inc(gate_read, 1)
                    act.wait_ge(gate_read, 8 * l + 4 * pair + 4)
                    if pair == 0 and l == 0:
                        act.wait_ge(decay_ready, 1)
                    for b in range(2):
                        col = J * l + 2 * pair + b
                        nc.scalar.activation(tt[:, b], tr[:, b], ACT.Tanh, scale=decay[:, 0, col:col + 1]).then_inc(ta_ready, 1)
                        nc.scalar.activation(ta[:, b], tr[:, b], ACT.Exp, scale=decay[:, 1, col:col + 1]).then_inc(ta_ready, 1)

                def roots(pair):
                    for b in range(2):
                        act.wait_ge(v_ready, J * l + 2 * pair + b + 1)
                        nc.scalar.activation(tt[:, b], tt[:, b], ACT.Sqrt).then_inc(s_ready, 1)

                def group_roots(y, half):
                    for j in range(J):
                        n = 8 * l + 4 * half + j
                        act.wait_ge(y_ready, n + 1 if half else 8 * l + J)
                        if half or j >= 2:
                            act.wait_ge(gsum_done, n - 1)
                        nc.scalar.activation(tt[:, j % 2], y[:, j], ACT.Square).then_inc(ysq_done, 1)
                    act.wait_ge(gsum_done, 8 * l + 4 * half + J)
                    if half:
                        act.wait_ge(yn_done, 8 * l + J)
                    nc.scalar.activation(ta[0:GR, 0], banks[0:GR, GROUP_BANK], ACT.Sqrt,
                                         bias=eps[0:GR]).then_inc(groot_done, 1)

                def group_hi(y, half, j):
                    n = 8 * l + 4 * half + j
                    act.wait_ge(yn_done, n + 1)
                    nc.scalar.activation(y_hi[:, 4 * half + j], y[:, j], ACT.Copy).then_inc(yh_done, 1)

                for u in range(WIN_U):
                    for i in range(2):
                        if u // 2 < 4:
                            evacuate(u, i)
                    split(u0 + u + 2, u % 2)
                    if u == 3:
                        gates(0)
                    if u == 4:
                        roots(0)
                    if u == 5:
                        gates(1)
                    if u == 6:
                        roots(1)
                    if u == 7:
                        group_roots(xc, 0)
                        for j in range(J):
                            group_hi(xc, 0, j)
                group_roots(bsc, 1)
                for j in range(J):
                    group_hi(bsc, 1, j)
                n0 = 8 + 16 * l
                for u in range(WOUT_U):
                    for i in range(2):
                        square(n0 + 2 * u + i)
                    split(U_WOUT[l] + u + 2, u % 2)

            def hidden(g, s, ahead):
                n = g * 2 + s
                act.wait_ge(gemm_done, (n + U_UP) * 2 + 1)
                act.wait_ge(prod_done, n + 1)
                nc.scalar.activation(tmp_a[:], banks[:, 2 * s], ACT.Silu).then_inc(silu_done, 1)
                act.wait_ge(prod_done, n + 2)
                nc.scalar.activation(block_of(act_hi, n), tmp_b[:],
                                     ACT.Copy).then_inc(ah_done, 1)
                if ahead is None:
                    split(n + (U_UP + 2), s, BASE["up"] + 32 * (g + 2), UF)
                else:
                    split(ahead, s)

            norm(0)
            mixer(0)
            norm(1)
            with act.Fori(0, UP_U // 2 - 1) as g:
                for s in range(2):
                    hidden(g, s, None)
            for s in range(2):
                hidden(UP_U // 2 - 1, s, U_DOWN + s)

            def down(m, bank, last):
                for s in range(2):
                    if last:
                        split(U_WIN[1] + s, s)
                    else:
                        split(m * 2 + (U_DOWN + 2 + s), s, m * 16 + (BASE["down"] + 32), DOWN_F)
                act.wait_ge(x_upd, m + (16 + 1))
                act.wait_ge(ssq_acc, m + 16)
                nc.scalar.activation(tmp_b[:], block_of(xT, m), ACT.Square).then_inc(sq_done, 1)

            with act.Fori(0, K // 2 - 1) as mm:
                for i in range(2):
                    down(mm * 2 + i, i, False)
            for i in range(2):
                down(K - 2 + i, i, i == 1)
            norm(2)
            mixer(1)

            act.wait_ge(stat_done, 4)
            nc.scalar.activation(rstd3[:], banks[:, STAT_BANK], ACT.Sqrt, bias=eps[:],
                                     scale=1.0 / D).then_inc(stat_read, 1)
            act.wait_ge(mods_ready, 4)
            for k in range(K):
                act.wait_ge(xr_ready, 3 * K + k + 1)
                nc.scalar.activation(hf3[:, k], hf3[:, k], ACT.Identity, bias=mods[:, 3, k:k + 1],
                                     scale=mod_gain[:, 3, k:k + 1]).then_inc(hf_done, 1)
            act.wait_ge(diff_ready, 1)
            nc.scalar.activation(rt[:, 13, 0, 0:TT], rt[:, 12, 0, 0:TT], ACT.Exp).then_inc(diff_exp, 1)
            for which, t in enumerate((h_tok, x_tok)):
                for n in range(2 * TT):
                    m = 2 * TT * which + n
                    act.wait_ge(tok_turned, m + 1)
                    nc.scalar.activation(t[:, n // 2, 512 * (n % 2):512 * (n % 2) + 512], banks[:, TOK_BANKS[n % 4]],
                                         ACT.Copy).then_inc(tok_read, 1)

            def ht_split(i):
                for n in range(4):
                    bank = (4, 5, 0, 1)[n]
                    act.wait_ge(ht_turned, i * 4 + (n + 1))
                    nc.scalar.activation(ht_hi[:, 4 * (n % 2):4 * (n % 2) + 4, P * (n // 2):P * (n // 2) + P],
                                         banks[:, bank].rearrange("p (k n) -> p k n", k=4), ACT.Copy).then_inc(ht_hi_done, 1)

            def y_copy(n):
                for b in range(4):
                    ins = nc.scalar.activation(y_rows[:, b // 2, 512 * (b % 2):512 * (b % 2) + 512],
                                               banks[:, (6, 7, 2, 3)[b]], ACT.Copy)
                ins.then_inc(y_read, 1)

            def e_split(i, j):
                n = K * EC if j < 2 * EG else (W2_CUT[j - 2 * EG + 1] - W2_CUT[j - 2 * EG]) * D
                act.wait_ge(e_loaded[j % RAWS], i * (16 * EU // RAWS) + 16 * (j // RAWS + 1))
                act.wait_ge(e_used, i * EU + (j + 1))
                nc.scalar.activation(e_hi[:, j % 2, 0:n], e_raw[:, j % RAWS, 0:n], ACT.Copy).then_inc(e_hi_done, 1)

            def trip(i, tiles):
                def at_split(g):
                    f0, f1 = WHOLE[g], WHOLE[g + 1]
                    act.wait_ge(at_turned, i * EG + (g + 1))
                    for a in range(tiles):
                        ins = nc.scalar.activation(at_hi[:, f0:f1, P * a:P * a + P],
                                                   banks[:, 4 + a, 0:P * (f1 - f0)].rearrange("p (f n) -> p f n", n=P),
                                                   ACT.Copy)
                    ins.then_inc(at_hi_done, 1)

                e_split(i, 0)
                e_split(i, 1)
                act.wait_ge(e_used, i * EU + 2)
                y_copy(i)
                for j in range(EU - 2):
                    g = j // 2
                    if j < 2 * EG and j % 2 == 0:
                        act.wait_ge(e_used, i * EU + (j + 3))
                        act.wait_ge(hid_done, i * EG + (g + 1))
                        nc.scalar.activation(e_silu[:, 0:tiles], banks[:, 0:tiles, 0:EC], ACT.Silu).then_inc(e_silu_done, 1)
                    e_split(i, j + 2)
                    if j in (3, 5, 7):
                        at_split((j - 3) // 2)
                    if j == 8:
                        at_split(3)
                act.wait_ge(y_free, i + 1)
                ht_split(i + 1)

            ht_split(0)
            trips = act.value_load(table[0:1, 3, 0:1], min_val=1, max_val=MAX_TRIPS)
            with act.Fori(0, trips) as i:
                two = act.value_load(table[0:1, 2, bass.ds(i, 1)], min_val=0, max_val=1)
                with act.If(two > 0):
                    trip(i, 2)
                with act.Else():
                    trip(i, 1)
                act.nop()
            act.wait_ge(e_used, trips * EU + 2)
            y_copy(trips)
            for which, t in enumerate((gate_row, gain_row)):
                for b in range(2):
                    act.wait_ge(row_done, 2 * which + b + 1)
                    nc.scalar.activation(t[:, 512 * b:512 * b + 512], banks[:, 2 * which + b], ACT.Copy).then_inc(row_ready, 1)
            for a in range(TT):
                act.wait_ge(xo_ready, a + 1)
                nc.scalar.activation(mix[:, a % 2], x_tok[:, a], ACT.Square, accum_out=sums[:, 0, a:a + 1]).then_inc(osum_ready, 1)
                act.wait_ge(osum_ready, a + 1)
                nc.scalar.activation(sums[:, 1, a:a + 1], sums[:, 0, a:a + 1], ACT.Sqrt, bias=eps[:],
                                     scale=1.0 / D).then_inc(oroot_ready, 1)

        @block.vector
        def _(dve):
            links = [0]

            def link(ins):
                links[0] += 1
                ins.then_inc(vec_link, 1)
                dve.wait_ge(vec_link, links[0])

            def split(u, s, n=None):
                if n is None:
                    if u >= U_END:
                        return
                    n = unit_info(u)[1]
                dve.wait_ge(hi_done, u + 1)
                nc.vector.tensor_tensor(w_lo[:, s, 0:n], raw[:, s, 0:n], w_hi[:, s, 0:n].bitcast(F32),
                                        ALU.subtract).then_inc(lo_done, 1)

            def mod_group(n):
                dve.wait_ge(mod_mm, n + 1)
                dve.wait_ge(mod_first_in[n], 16)
                for k in range(K):
                    scalar = silu_c[:, k:k + 1]
                    if k == 0:
                        ins = nc.vector.tensor_scalar(mod_acc[:], mod_first[n][:, k], scalar, None, ALU.mult)
                    else:
                        dve.wait_ge(mod_step, n * K + k)
                        ins = nc.vector.scalar_tensor_tensor(out=mod_acc[:], in0=mod_first[n][:, k], scalar=scalar,
                                                             in1=mod_acc[:], op0=ALU.mult, op1=ALU.add)
                    ins.then_inc(mod_step, 1)

            def mod_finish(m):
                dve.wait_ge(mod_mm, MG * (m + 1) + 1)
                link(nc.vector.tensor_tensor(mods[:, m], banks[:, MODS_BANK, 24 * m:24 * m + 24],
                                             par1[:, 24 * m:24 * m + 24], ALU.add))
                gain = 96 + (2 * K if m % 2 else 0) + K * (m // 2)
                nc.vector.scalar_tensor_tensor(out=mod_gain[:, m], in0=mods[:, m, K:2 * K], scalar=1.0,
                                               in1=par1[:, gain:gain + K], op0=ALU.add,
                                               op1=ALU.mult).then_inc(mods_ready, 1)

            def add_square(n):
                dve.wait_ge(sq_done, n + 1)
                if n % K == 0:
                    nc.vector.tensor_copy(tmp_a[:], tmp_b[:]).then_inc(ssq_acc, 1)
                else:
                    dve.wait_ge(ssq_acc, n)
                    nc.vector.tensor_tensor(tmp_a[:], tmp_a[:], tmp_b[:], ALU.add).then_inc(ssq_acc, 1)

            def norm(nth):
                dve.wait_ge(stat_read, nth + 1)
                nc.vector.reciprocal(rstd[:], rstd[:]).then_inc(rstd_ready, 1)
                dve.wait_ge(rstd_ready, nth + 1)
                for k in range(K + 2):
                    if k < K:
                        nc.vector.tensor_tensor(hf[:, k], xT[:, k], rstd[:], ALU.mult).then_inc(xr_ready, 1)
                    if k >= 2:
                        dve.wait_ge(hh_done, K * nth + k - 1)
                        nc.vector.tensor_tensor(h_lo[:, k - 2], hf[:, k - 2], h_hi[:, k - 2].bitcast(F32),
                                                ALU.subtract).then_inc(hl_done, 1)

            def residual(n, m, bank, nth, count):
                dve.wait_ge(gemm_done, count)
                xm = block_of(xT, m)
                gate = mods[:, nth, bass.ds(m + 2 * K, 1)]
                nc.vector.scalar_tensor_tensor(out=xm, in0=banks[:, bank], scalar=gate, in1=xm,
                                               op0=ALU.mult, op1=ALU.add).then_inc(x_upd, 1)
                dve.wait_ge(x_upd, n + 1)
                dve.sem_inc(res_read, 1)

            dve.sem_inc(res_read, 4)
            dve.sem_inc(pair_read, 2)
            for first in (prod_done, al_done, hid_done, at_lo_done):
                dve.sem_inc(first, 1)
            dve.wait_ge(rows_turned, 1)
            nc.vector.tensor_copy(par1[:], banks[:, 4, 0:PT1R]).then_inc(par_ready, 1)
            dve.wait_ge(rows_turned, 2)
            nc.vector.tensor_copy(par2[:], banks[:, 5, 0:R_END]).then_inc(par_ready, 1)
            for k in range(K):
                add_square(k)
            dve.wait_ge(silu_ready, 1)
            for g in range(MG):
                mod_group(g)
                if g >= MG - 3 and g < MG - 1:
                    split(g - (MG - 3), g - (MG - 3))
            def decays():
                dve.wait_ge(decay_step, 1)
                z, w, w2, acc, low = (small[:, i] for i in (1, 2, 3, 4, 5))
                link(nc.vector.tensor_scalar(w, z, 2.0, None, ALU.add))
                link(nc.vector.reciprocal(w, w))
                link(nc.vector.tensor_tensor(w, w, z, ALU.mult))
                link(nc.vector.tensor_tensor(w2, w, w, ALU.mult))
                link(nc.vector.tensor_scalar(acc, w2, 1.0 / 19, 1.0 / 17, ALU.mult, ALU.add))
                for odd in range(15, 0, -2):
                    link(nc.vector.tensor_tensor(acc, acc, w2, ALU.mult))
                    link(nc.vector.tensor_scalar(acc, acc, 1.0 / odd, None, ALU.add))
                link(nc.vector.tensor_tensor(acc, acc, w, ALU.mult))
                link(nc.vector.tensor_scalar(low, par2[:, R_LAM:R_LAM + 2 * J], -1.0, 0.0, ALU.mult, ALU.max))
                link(nc.vector.scalar_tensor_tensor(out=acc, in0=acc, scalar=2.0, in1=low, op0=ALU.mult, op1=ALU.add))
                nc.vector.tensor_scalar(decay[:, 1], acc, -LRU_C, None, ALU.mult)
                nc.vector.tensor_scalar(decay[:, 0], acc, LRU_C, None, ALU.mult).then_inc(decay_ready, 1)

            def mixer(l):
                u0 = U_WIN[l]
                m_next = 2 * l + 1

                def conv_lru(j):
                    dve.wait_ge(xpad_ready, J * l + j + 1)
                    w = [par2[:, R_CW + 4 * J * l + J * t + j:R_CW + 4 * J * l + J * t + j + 1] for t in range(LT)]
                    b = par2[:, R_CB + J * l + j:R_CB + J * l + j + 1]
                    link(nc.vector.tensor_scalar(xc[:, j], xpad[:, j, LT - 1:LT - 1 + T], w[LT - 1], b, ALU.mult, ALU.add))
                    for t in range(LT - 1):
                        ins = nc.vector.scalar_tensor_tensor(out=xc[:, j], in0=xpad[:, j, t:t + T], scalar=w[t],
                                                             in1=xc[:, j], op0=ALU.mult, op1=ALU.add)
                        if t < LT - 2:
                            link(ins)
                    ins.then_inc(xc_ready, 1)

                def to_v(pair):
                    for b in range(2):
                        dve.wait_ge(ta_ready, 2 * (J * l + 2 * pair + b) + 2)
                        link(nc.vector.tensor_scalar(tr[:, b], tt[:, b], 1.0, None, ALU.add))
                        link(nc.vector.reciprocal(tr[:, b], tr[:, b]))
                        nc.vector.scalar_tensor_tensor(out=tt[:, b], in0=tt[:, b], scalar=2.0, in1=tr[:, b],
                                                       op0=ALU.mult, op1=ALU.mult).then_inc(v_ready, 1)
                        link(nc.vector.tensor_tensor(ti[:, b], ti[:, b], xc[:, 2 * pair + b], ALU.mult))

                def scans(pair):
                    for b in range(2):
                        j = 2 * pair + b
                        dve.wait_ge(s_ready, J * l + j + 1)
                        link(nc.vector.tensor_tensor(ti[:, b], ti[:, b], tt[:, b], ALU.mult))
                        nc.vector.tensor_tensor_scan(xc[:, j], ta[:, b], ti[:, b], 0.0, ALU.mult,
                                                     ALU.add).then_inc(scan_done, 1)
                        dve.wait_ge(scan_done, J * l + j + 1)
                        nc.vector.tensor_tensor(xc[:, j], xc[:, j], gel[:, j], ALU.mult).then_inc(y_ready, 1)

                def gated_conv(j):
                    dve.wait_ge(gemm_done, 2 * (u0 + 8 + j // 2) + 1 + j % 2)
                    link(nc.vector.tensor_tensor(cxpad[:, j % 2, ST - 1:CXW], banks[:, j], csc[:, j], ALU.mult))
                    dve.sem_inc(proj_read, 1)
                    w = [par2[:, R_SW + ST * J * l + J * t + j:R_SW + ST * J * l + J * t + j + 1] for t in range(ST)]
                    link(nc.vector.tensor_scalar(ti[:, j % 2], cxpad[:, j % 2, ST - 1:CXW], w[ST - 1], None, ALU.mult))
                    for t in range(ST - 1):
                        link(nc.vector.scalar_tensor_tensor(out=ti[:, j % 2], in0=cxpad[:, j % 2, t:t + T], scalar=w[t],
                                                            in1=ti[:, j % 2], op0=ALU.mult, op1=ALU.add))
                    nc.vector.tensor_tensor(bsc[:, j], bsc[:, j], ti[:, j % 2], ALU.mult).then_inc(y_ready, 1)

                def group_norm(y, half):
                    dve.wait_ge(groot_done, 2 * l + half + 1)
                    nc.vector.reciprocal(ta[0:GR, 0], ta[0:GR, 0]).then_inc(grstd_done, 1)
                    for j in range(J):
                        col = (R_GS if half else R_GL) + J * l + j
                        dve.wait_ge(gspread_done, 8 * l + 4 * half + j + 1)
                        nc.vector.scalar_tensor_tensor(out=y[:, j], in0=y[:, j], scalar=par2[:, col:col + 1],
                                                       in1=banks[:, SPREAD_BANKS[j % 2]], op0=ALU.mult,
                                                       op1=ALU.mult).then_inc(yn_done, 1)

                def group_lo(y, half, j):
                    dve.wait_ge(yh_done, 8 * l + 4 * half + j + 1)
                    nc.vector.tensor_tensor(y_lo[:, 4 * half + j], y[:, j], y_hi[:, 4 * half + j].bitcast(F32),
                                            ALU.subtract).then_inc(yl_done, 1)

                for u in range(WIN_U):
                    if u == 9:
                        gated_conv(0)
                        gated_conv(1)
                    split(u0 + u + 2, u % 2)
                    if u == 0:
                        dve.wait_ge(pad_ready, 2 * l + 2)
                        conv_lru(0)
                        conv_lru(1)
                    if u == 1:
                        conv_lru(2)
                        conv_lru(3)
                    if u == 3:
                        to_v(0)
                    if u == 4:
                        scans(0)
                    if u == 5:
                        to_v(1)
                    if u == 6:
                        scans(1)
                    if u == 7:
                        group_norm(xc, 0)
                        for j in range(J):
                            group_lo(xc, 0, j)
                gated_conv(2)
                gated_conv(3)
                group_norm(bsc, 1)
                for j in range(J):
                    group_lo(bsc, 1, j)
                n0 = 8 + 16 * l
                for u in range(WOUT_U):
                    for i in range(2):
                        n = n0 + 2 * u + i
                        residual(n, 2 * u + i, (2 * u + i) % 4, 2 * l, 2 * (U_WOUT[l] + u) + 1 + i)
                        if i == 1:
                            split(U_WOUT[l] + u + 2, u % 2)
                        add_square(n)
                mod_finish(m_next)

            def hidden(g, s, ahead):
                n = g * 2 + s
                dve.wait_ge(gemm_done, (n + U_UP) * 2 + 2)
                dve.wait_ge(silu_done, n + 1)
                dve.wait_ge(ah_done, n + 1)
                dve.wait_ge(al_done, n + 1)
                nc.vector.tensor_tensor(tmp_b[:], banks[:, 2 * s + 1], tmp_a[:], ALU.mult).then_inc(prod_done, 1)
                dve.wait_ge(prod_done, n + 2)
                dve.sem_inc(pair_read, 1)
                dve.wait_ge(ah_done, n + 2)
                nc.vector.tensor_tensor(block_of(act_lo, n), tmp_b[:],
                                        block_of(act_hi, n).bitcast(F32),
                                        ALU.subtract).then_inc(al_done, 1)
                if ahead is None:
                    split(n + (U_UP + 2), s, UF)
                else:
                    split(ahead, s)

            mod_finish(0)
            norm(0)
            decays()
            mixer(0)
            norm(1)
            with dve.Fori(0, UP_U // 2 - 1) as g:
                hidden(g, 0, None)
                hidden(g, 1, None)
            for s in range(2):
                hidden(UP_U // 2 - 1, s, U_DOWN + s)
            mod_finish(2)
            link(nc.vector.memset(tmp_a[:], 0.0))

            def down(m, bank, last):
                for s in range(2):
                    if last:
                        split(U_WIN[1] + s, s)
                    else:
                        split(m * 2 + (U_DOWN + 2 + s), s, DOWN_F)
                residual(m + 16, m, bank, 1, m * 4 + (2 * U_DOWN + 4))
                dve.wait_ge(sq_done, m + 17)
                dve.wait_ge(ssq_acc, m + 16)
                nc.vector.tensor_tensor(tmp_a[:], tmp_a[:], tmp_b[:], ALU.add).then_inc(ssq_acc, 1)

            with dve.Fori(0, K // 2 - 1) as mm:
                for i in range(2):
                    down(mm * 2 + i, i, False)
            for i in range(2):
                down(K - 2 + i, i, i == 1)
            norm(2)
            mixer(1)

            dve.wait_ge(stat_read, 4)
            nc.vector.reciprocal(rstd3[:], rstd3[:]).then_inc(rstd_ready, 1)
            dve.wait_ge(rstd_ready, 4)
            for k in range(K):
                nc.vector.tensor_tensor(hf3[:, k], xT[:, k], rstd3[:], ALU.mult).then_inc(xr_ready, 1)
            dve.wait_ge(iota_ready, 1)
            link(nc.vector.tensor_copy(iota_f[:], iota_i[:]))
            logits, best, best_i, m1, m2, mask, pre, tot, slot = (rt[:, n] for n in range(9))
            dve.wait_ge(logits_done, 1)
            dve.wait_ge(rw_loaded, 32)
            for a in range(TT):
                link(nc.vector.tensor_tensor(logits[:, a], banks[:, 0, E * a:E * a + E], rb[:], ALU.add))
            for a in range(TT):
                link(nc.vector.max(best[:, a], logits[:, a]))
            for a in range(TT):
                link(nc.vector.max_index(rt_u[:, a], best[:, a], logits[:, a]))
            link(nc.vector.tensor_copy(best_i, rt_u[:]))
            for a in range(TT):
                for m, n in ((m1, 0), (m2, 1)):
                    link(nc.vector.tensor_scalar(m[:, a], iota_f[:, 0:E], best_i[:, a, n:n + 1], None, ALU.is_equal))
            nc.vector.tensor_tensor(mask, m1, m2, ALU.add).then_inc(mask_ready, 1)
            diff, e2 = rt[:, 12, 0, 0:TT], rt[:, 13, 0, 0:TT]
            nc.vector.tensor_tensor(diff, best[:, :, 1], best[:, :, 0], ALU.subtract).then_inc(diff_ready, 1)
            dve.wait_ge(count_done, 1)
            link(nc.vector.tensor_copy(pre, banks[:, 5, 0:TT * E].rearrange("p (a e) -> p a e", a=TT)))
            link(nc.vector.tensor_copy(tot, banks[:, 5, TT * E:2 * TT * E].rearrange("p (a e) -> p a e", a=TT)))
            count, tiles_n, trips_n, tile_c, trip_c, one8, tile0, trip0, run = (ex[:, n] for n in range(9))
            link(nc.vector.tensor_tensor(count, tot[:, 0], tot[:, 1], ALU.add))
            for a in range(2, TT):
                link(nc.vector.tensor_tensor(count, count, tot[:, a], ALU.add))
            link(nc.vector.memset(one8, 1.0))
            link(nc.vector.tensor_scalar(tiles_n, count, 0.0, None, ALU.is_gt))
            for n in range(1, TT):
                link(nc.vector.scalar_tensor_tensor(out=tiles_n, in0=count, scalar=float(P * n), in1=tiles_n,
                                                    op0=ALU.is_gt, op1=ALU.add))
            link(nc.vector.tensor_scalar(trips_n, count, 0.0, None, ALU.is_gt))
            for n in range(1, TT // 2):
                link(nc.vector.scalar_tensor_tensor(out=trips_n, in0=count, scalar=float(2 * P * n), in1=trips_n,
                                                    op0=ALU.is_gt, op1=ALU.add))
            link(nc.vector.tensor_tensor_scan(tile_c, one8, tiles_n, 0.0, ALU.mult, ALU.add))
            link(nc.vector.tensor_tensor_scan(trip_c, one8, trips_n, 0.0, ALU.mult, ALU.add))
            link(nc.vector.tensor_tensor(tile0, tile_c, tiles_n, ALU.subtract))
            link(nc.vector.tensor_tensor(trip0, trip_c, trips_n, ALU.subtract))
            link(nc.vector.tensor_scalar(run, tile0, float(P), None, ALU.mult))
            for a in range(TT):
                link(nc.vector.tensor_tensor(slot[:, a], pre[:, a], run, ALU.add))
                if a < TT - 1:
                    link(nc.vector.tensor_tensor(run, run, tot[:, a], ALU.add))
            for which, m in enumerate((m1, m2)):
                link(nc.vector.tensor_tensor(rt[:, 9 + which], m, slot, ALU.mult))
                link(nc.vector.tensor_reduce(rt[:, 11, which, 0:TT], rt[:, 9 + which], AX.X, ALU.add))
                ins = nc.vector.tensor_copy(slots_i[:, which], rt[:, 11, which, 0:TT])
                if which == 0:
                    link(ins)
            ins.then_inc(slots_ready, 1)
            expert, first, after, one, ge0, ge1 = (tb[:, n] for n in range(6))
            number = iota_f[:, 0:TR]
            link(nc.vector.memset(tb[:, 0:3], 0.0))
            link(nc.vector.scalar_tensor_tensor(out=run, in0=trip0, scalar=-2.0, in1=tile0, op0=ALU.mult, op1=ALU.add))
            for e in range(E):
                link(nc.vector.tensor_scalar(ge0, number, trip0[:, e:e + 1], None, ALU.is_ge))
                link(nc.vector.tensor_scalar(ge1, number, trip_c[:, e:e + 1], None, ALU.is_ge))
                link(nc.vector.tensor_tensor(expert, expert, ge1, ALU.add))
                link(nc.vector.tensor_tensor(one, ge0, ge1, ALU.subtract))
                link(nc.vector.scalar_tensor_tensor(out=first, in0=one, scalar=run[:, e:e + 1], in1=first,
                                                    op0=ALU.mult, op1=ALU.add))
                link(nc.vector.scalar_tensor_tensor(out=after, in0=one, scalar=tile_c[:, e:e + 1], in1=after,
                                                    op0=ALU.mult, op1=ALU.add))
            link(nc.vector.scalar_tensor_tensor(out=first, in0=number, scalar=2.0, in1=first, op0=ALU.mult, op1=ALU.add))
            link(nc.vector.tensor_tensor(one, after, first, ALU.subtract))
            link(nc.vector.tensor_scalar(one, one, 2.0, None, ALU.is_ge))
            link(nc.vector.tensor_scalar(expert, expert, float(E - 1), None, ALU.min))
            link(nc.vector.tensor_scalar(first, first, float(MAX_TILES - 1), None, ALU.min))
            link(nc.vector.tensor_copy(table[:, 0], expert))
            link(nc.vector.tensor_copy(table[:, 1], first))
            link(nc.vector.tensor_copy(table[:, 2], one))
            nc.vector.tensor_copy(table[:, 3, 0:1], trip_c[:, E - 1:E]).then_inc(table_ready, 1)
            dve.wait_ge(diff_exp, 1)
            link(nc.vector.tensor_scalar(pick_w[:, 0], e2, 1.0, None, ALU.add))
            link(nc.vector.reciprocal(pick_w[:, 0], pick_w[:, 0]))
            link(nc.vector.tensor_tensor(pick_w[:, 1], pick_w[:, 0], e2, ALU.mult))

            def ht_split(i):
                for n in range(4):
                    bank = (4, 5, 0, 1)[n]
                    part = (slice(None), slice(4 * (n % 2), 4 * (n % 2) + 4), slice(P * (n // 2), P * (n // 2) + P))
                    dve.wait_ge(ht_hi_done, i * 4 + (n + 1))
                    nc.vector.tensor_tensor(ht_lo[part], banks[:, bank].rearrange("p (k n) -> p k n", k=4),
                                            ht_hi[part].bitcast(F32), ALU.subtract).then_inc(ht_lo_done, 1)

            def e_split(i, j):
                n = K * EC if j < 2 * EG else (W2_CUT[j - 2 * EG + 1] - W2_CUT[j - 2 * EG]) * D
                dve.wait_ge(e_hi_done, i * EU + (j + 1))
                nc.vector.tensor_tensor(e_lo[:, j % 2, 0:n], e_raw[:, j % RAWS, 0:n], e_hi[:, j % 2, 0:n].bitcast(F32),
                                        ALU.subtract).then_inc(e_lo_done, 1)

            def trip(i, tiles):
                def at_split(g):
                    f0, f1 = WHOLE[g], WHOLE[g + 1]
                    dve.wait_ge(at_hi_done, i * EG + (g + 1))
                    for a in range(tiles):
                        part = (slice(None), slice(f0, f1), slice(P * a, P * a + P))
                        ins = nc.vector.tensor_tensor(at_lo[part],
                                                      banks[:, 4 + a, 0:P * (f1 - f0)].rearrange("p (f n) -> p f n", n=P),
                                                      at_hi[part].bitcast(F32), ALU.subtract)
                    ins.then_inc(at_lo_done, 1)

                e_split(i, 0)
                e_split(i, 1)
                for j in range(EU - 2):
                    g = j // 2
                    if j < 2 * EG and j % 2 == 1:
                        dve.wait_ge(e_used, i * EU + (j + 3))
                        dve.wait_ge(e_silu_done, i * EG + (g + 2))
                        nc.vector.tensor_tensor(hid[:, 0:tiles, EC * g:EC * g + EC], banks[:, 2:2 + tiles, 0:EC],
                                                e_silu[:, 0:tiles], ALU.mult).then_inc(hid_done, 1)
                    e_split(i, j + 2)
                    if j in (3, 5, 7):
                        at_split((j - 3) // 2)
                    if j == 8:
                        at_split(3)
                ht_split(i + 1)

            dve.sem_inc(e_lo_done, RAWS)
            ht_split(0)
            trips = dve.value_load(table[0:1, 3, 0:1], min_val=1, max_val=MAX_TRIPS)
            with dve.Fori(0, trips) as i:
                two = dve.value_load(table[0:1, 2, bass.ds(i, 1)], min_val=0, max_val=1)
                with dve.If(two > 0):
                    trip(i, 2)
                with dve.Else():
                    trip(i, 1)
                dve.nop()

            dve.wait_ge(e_lo_done, trips * EU + RAWS)
            for k in range(K):
                nc.vector.tensor_scalar(diag[:, 0, k], ident[:], mods[:, 3, 2 * K + k:2 * K + k + 1], None,
                                        ALU.mult).then_inc(diag_ready, 1)
            for k in range(K):
                nc.vector.tensor_scalar(diag[:, 1, k], ident[:], par2[:, R_FN + k:R_FN + k + 1], None,
                                        ALU.mult).then_inc(diag_ready, 1)
            def last_norm(a):
                dve.wait_ge(oroot_ready, a + 1)
                link(nc.vector.reciprocal(sums[:, 2, a:a + 1], sums[:, 1, a:a + 1]))
                if a == 0:
                    dve.wait_ge(row_ready, 4)
                nc.vector.scalar_tensor_tensor(out=mix[:, a % 2], in0=x_tok[:, a], scalar=sums[:, 2, a:a + 1],
                                               in1=gain_row[:], op0=ALU.mult, op1=ALU.mult).then_inc(o_ready, 1)

            for a in range(TT):
                got = picked[:, a % 2]
                dve.wait_ge(picked_in[a % 2], 32 * (a // 2 + 1))
                link(nc.vector.tensor_scalar(got[:, 0], got[:, 0], pick_w[:, 0, a:a + 1], None, ALU.mult))
                link(nc.vector.scalar_tensor_tensor(out=got[:, 0], in0=got[:, 1], scalar=pick_w[:, 1, a:a + 1],
                                                    in1=got[:, 0], op0=ALU.mult, op1=ALU.add))
                if a == 0:
                    dve.wait_ge(row_ready, 2)
                nc.vector.tensor_tensor(got[:, 0], got[:, 0], gate_row[:], ALU.mult).then_inc(mix_done, 1)
                dve.wait_ge(mix_done, a + 1)
                if a >= 2:
                    dve.wait_ge(out_stored[a % 2], 16 * (a // 2))
                nc.vector.tensor_tensor(x_tok[:, a], x_tok[:, a], got[:, 0], ALU.add).then_inc(xo_ready, 1)
                last_norm(a)

        @block.tensor
        def _(pe):
            def product(ps, hi, lo, x_hi, x_lo, start, stop):
                nc.tensor.matmul(ps, hi, x_hi, start=start, stop=False)
                nc.tensor.matmul(ps, hi, x_lo, start=False, stop=False)
                return nc.tensor.matmul(ps, lo, x_hi, start=False, stop=stop)

            def mod_sum(n):
                if isinstance(n, int) and n < MG:
                    pe.wait_ge(mod_step, n * K + K)
                else:
                    pe.wait_ge(mod_part, (n - MG) * 7 + 7)
                for b in range(MC // P):
                    last = nc.tensor.matmul(banks[:, MODS_BANK, bass.ds(n * 3 + b, 1)], mod_acc[:, b * P:(b + 1) * P],
                                            ones[:], start=True, stop=True)
                last.then_inc(mod_mm, 1)

            def unit_of_two(u, s, x_hi, x_lo, bank, credit, chunks=None, between=None):
                pe.wait_ge(lo_done, u + 1)

                def step(i, k):
                    cols = slice(2 * P * k + P * i, 2 * P * k + P * i + P)
                    last = product(banks[:, bank + i], w_hi[:, s, cols], w_lo[:, s, cols], x_hi[:, k], x_lo[:, k],
                                   k == 0, k == K - 1)
                    if k == K - 1:
                        last.then_inc(gemm_done, 1)

                if chunks is None:
                    for i in range(2):
                        pe.wait_ge(*credit(i))
                        for k in range(K):
                            step(i, k)
                else:
                    for i in range(2):
                        pe.wait_ge(*credit(i))
                    for k in range(K):
                        if between is not None and k == J:
                            between()
                        pe.wait_ge(chunks[0], chunks[1] + k + 1)
                        for i in range(2):
                            step(i, k)

            pe.sem_inc(mod_mm, 1)
            pe.wait_ge(const_ready, 13)
            pe.wait_ge(rows_loaded, 16 * 16)
            nc.tensor.transpose(banks[:, 4, 0:PT1R], rows[0:PT1R, 0, :], ident[0:PT1R, 0:PT1R]).then_inc(rows_turned, 1)
            nc.tensor.transpose(banks[:, 5, 0:R_END], rows[0:R_END, 1, :], ident[0:R_END, 0:R_END]).then_inc(rows_turned, 1)
            pe.wait_ge(x_loaded, 16)
            for k in range(K):
                if k >= 4:
                    pe.wait_ge(x_upd, k - 3)
                for a in range(TT):
                    last = nc.tensor.transpose(banks[:, k % 4, a * P:(a + 1) * P], xrow[:, a, k * P:(k + 1) * P], ident[:])
                last.then_inc(xt_turned, 1)

            def norm(nth):
                pe.wait_ge(ssq_acc, K * (nth + 1))
                nc.tensor.matmul(banks[:, STAT_BANK], ones_all[:], tmp_a[:], start=True, stop=True).then_inc(stat_done, 1)

            def mixer(l):
                u0, m_next = U_WIN[l], 2 * l + 1
                norm(2 * l)
                if l == 0:
                    for g in range(MG):
                        mod_sum(g)

                def trip(q, between=None):
                    for s in range(2):
                        if s and between is not None:
                            between()
                        unit_of_two(q * 2 + (u0 + s), s, h_hi, h_lo, 2 * s,
                                    lambda i: (proj_read, q * 4 + (20 * l + 2 * s + i + 1)),
                                    None if s else (hl_done, K * (2 * l)))
                        if s == 0:
                            mod_sum(q + MG * m_next)

                def gates(pair):
                    pe.wait_ge(gw_loaded, 64 * (l + 1))
                    for b in range(2):
                        j = 2 * pair + b
                        pe.wait_ge(xc_ready, J * l + j + 1)
                        for g in range(2):
                            n = 8 * l + 2 * j + g
                            if n >= 2:
                                pe.wait_ge(gate_read, n - 1)
                            nc.tensor.matmul(banks[:, 4 + g], gate_w[:, g, j], xc[:, j], start=True,
                                             stop=True).then_inc(gate_done, 1)

                def group_sums(half):
                    for j in range(J):
                        pe.wait_ge(ysq_done, 8 * l + 4 * half + j + 1)
                        nc.tensor.matmul(banks[0:GR, GROUP_BANK], head_sel[:, GR - 2 - 2 * j:2 * GR - 2 - 2 * j],
                                         tt[:, j % 2], start=(j == 0), stop=(j == J - 1)).then_inc(gsum_done, 1)

                def group_spread(half):
                    pe.wait_ge(grstd_done, 2 * l + half + 1)
                    for j in range(J):
                        if j >= 2 or half:
                            pe.wait_ge(yn_done, 8 * l + 4 * half + j - 1)
                        nc.tensor.matmul(banks[:, SPREAD_BANKS[j % 2]],
                                         spread[0:GR, j],
                                         ta[0:GR, 0], start=True, stop=True).then_inc(gspread_done, 1)

                with pe.Fori(0, 2) as q:
                    trip(q)
                gates(0)
                trip(2)
                gates(1)
                trip(3)
                pe.wait_ge(gate_read, 8 * (l + 1))
                group_sums(0)
                trip(4, lambda: group_spread(0))
                mod_sum(MG * m_next + 5)
                group_sums(1)
                for q in range(WOUT_U // 2):
                    for s in range(2):
                        unit_of_two(q * 2 + (U_WOUT[l] + s), s, y_hi, y_lo, 2 * s,
                                    lambda i: (res_read, q * 4 + (16 * l + 2 * s + i + 1)),
                                    (yl_done, 8 * l) if q == s == 0 else None,
                                    lambda: group_spread(1))
                    mod_sum(q + (MG * m_next + 6))

            def up(n, s):
                pe.wait_ge(lo_done, n + (U_UP + 1))
                pe.wait_ge(pair_read, n + 1)
                for w in range(2):
                    for k in range(K):
                        if s == w == 0:
                            pe.wait_ge(hl_done, K + k + 1)
                        cols = slice(P * (K * w + k), P * (K * w + k) + P)
                        last = product(banks[:, 2 * s + w], w_hi[:, s, cols], w_lo[:, s, cols], h_hi[:, k], h_lo[:, k],
                                       k == 0, k == K - 1)
                    last.then_inc(gemm_done, 1)

            mixer(0)
            norm(1)
            with pe.Fori(0, MG) as g:
                for s in range(2):
                    up(g * 2 + s, s)
                mod_sum(g + 2 * MG)
            with pe.Fori(MG, UP_U // 2) as g:
                for s in range(2):
                    up(g * 2 + s, s)
            pe.wait_ge(al_done, FB + 1)
            with pe.Fori(0, K // 2) as mm:
                for i in range(2):
                    pe.wait_ge(res_read, mm * 2 + (8 + i + 3))
                    for h in range(2):
                        pe.wait_ge(lo_done, mm * 4 + (U_DOWN + 2 * i + h + 1))
                        for f in range(FH):
                            cols = slice(P * f, P * f + P)
                            last = product(banks[:, i], w_hi[:, h, cols], w_lo[:, h, cols], act_hi[:, h * FH + f],
                                           act_lo[:, h * FH + f], h == 0 and f == 0, h == 1 and f == FH - 1)
                        last.then_inc(gemm_done, 2)
            mixer(1)

            norm(3)
            pe.wait_ge(hf_done, 4 * K)
            pe.wait_ge(rw_loaded, 32)
            for a in range(TT):
                for k in range(K):
                    last = nc.tensor.matmul(banks[:, 0, E * a:E * a + E], hf3[:, k, P * a:P * a + P], rw[:, k],
                                            start=(k == 0), stop=(k == K - 1))
            last.then_inc(logits_done, 1)

            def token_major(src, first, n):
                m = first + n
                if m >= 4:
                    pe.wait_ge(tok_read, m - 3)
                for q in range(4):
                    last = nc.tensor.transpose(banks[:, TOK_BANKS[n % 4], P * q:P * q + P],
                                               src[:, 4 * (n % 2) + q, P * (n // 2):P * (n // 2) + P], ident[:])
                last.then_inc(tok_turned, 1)

            for n in range(4):
                token_major(hf3, 0, n)
            pe.wait_ge(mask_ready, 1)
            mask = rt[:, 5].rearrange("p a e -> p (a e)")
            nc.tensor.matmul(banks[:, 5, 0:TT * E], before[:], mask, start=True, stop=True)
            nc.tensor.matmul(banks[:, 5, TT * E:2 * TT * E], ones_all[:], mask, start=True, stop=True).then_inc(count_done, 1)
            for n in range(4, 2 * TT):
                token_major(hf3, 0, n)
            for n in range(2 * TT):
                token_major(xT, 2 * TT, n)

            def turn_rows(i):
                pe.wait_ge(rows_in, i * 16 + 16)
                for n in range(4):
                    for q in range(4):
                        k = 4 * (n % 2) + q
                        last = nc.tensor.transpose(banks[:, (4, 5, 0, 1)[n], P * q:P * q + P],
                                                   h_rows[:, n // 2, P * k:P * k + P], ident[:])
                    last.then_inc(ht_turned, 1)

            def trip(i, tiles):
                def turn_hidden(g):
                    pe.wait_ge(hid_done, i * EG + (g + 2))
                    pe.wait_ge(at_lo_done, i * EG + (g + 1))
                    for a in range(tiles):
                        for q, f in enumerate(range(WHOLE[g], WHOLE[g + 1])):
                            last = nc.tensor.transpose(banks[:, 4 + a, P * q:P * q + P], hid[:, a, P * f:P * f + P], ident[:])
                    last.then_inc(at_turned, 1)

                pe.wait_ge(ht_lo_done, i * 4 + 4)
                for j in range(EU):
                    s = j % 2
                    pe.wait_ge(e_lo_done, i * EU + (j + 1 + RAWS))
                    if j < 2 * EG:
                        g, w = j // 2, j % 2
                        if w == 0:
                            pe.wait_ge(e_silu_done, i * EG + (g + 1))
                        else:
                            pe.wait_ge(hid_done, i * EG + (g + 1))
                            if g == 0:
                                pe.wait_ge(y_read, i + 1)
                        for a in range(tiles):
                            for k in range(K):
                                cols = slice(EC * k, EC * k + EC)
                                part = (slice(None), k, slice(P * a, P * a + P))
                                last = product(banks[:, 2 * w + a, 0:EC], ht_hi[part], ht_lo[part], e_hi[:, s, cols],
                                               e_lo[:, s, cols], k == 0, k == K - 1)
                    else:
                        if j == 2 * EG:
                            pe.wait_ge(y_read, i + 1)
                        f0, f1 = W2_CUT[j - 2 * EG], W2_CUT[j - 2 * EG + 1]
                        whole = min(g for g in range(EG + 1) if WHOLE[g] >= f1)
                        pe.wait_ge(at_lo_done, i * EG + (whole + 1))
                        for a in range(tiles):
                            if j == 2 * EG and a == 1:
                                pe.wait_ge(hid_done, i * EG + (EG + 1))
                            for half in range(2):
                                for f in range(f0, f1):
                                    cols = slice(D * (f - f0) + 512 * half, D * (f - f0) + 512 * half + 512)
                                    part = (slice(None), f, slice(P * a, P * a + P))
                                    last = product(banks[:, (6, 2)[a] + half], at_hi[part], at_lo[part], e_hi[:, s, cols],
                                                   e_lo[:, s, cols], f == 0, f == FEB - 1)
                    last.then_inc(e_used, 1)
                    if j in (3, 5, 7):
                        turn_hidden((j - 3) // 2)
                    if j == 8:
                        turn_hidden(3)
                    if j == 9:
                        pe.wait_ge(at_lo_done, i * EG + (EG + 1))
                        turn_rows(i + 1)

            pe.sem_inc(e_used, 2)
            pe.wait_ge(sorted_stored, 16 * 2 * TT)
            pe.wait_ge(tok_read, 4 * TT)
            pe.wait_ge(table_ready, 1)
            turn_rows(0)
            trips = pe.value_load(table[0:1, 3, 0:1], min_val=1, max_val=MAX_TRIPS)
            with pe.Fori(0, trips) as i:
                two = pe.value_load(table[0:1, 2, bass.ds(i, 1)], min_val=0, max_val=1)
                with pe.If(two > 0):
                    trip(i, 2)
                with pe.Else():
                    trip(i, 1)
                pe.nop()
            pe.wait_ge(y_read, trips + 1)
            for which in range(2):
                for k in range(K):
                    pe.wait_ge(diag_ready, K * which + k + 1)
                    last = nc.tensor.matmul(banks[:, 2 * which + k // 4, P * (k % 4):P * (k % 4) + P], ones_all[:],
                                            diag[:, which, k], start=True, stop=True)
                    if k % 4 == 3:
                        last.then_inc(row_done, 1)
    return None


INPUTS = ["x", "c", "mix_norm", "mix_mod_w", "mix_mod_b", "w_in", "lru_conv_w", "lru_conv_b", "lru_wa", "lru_ba",
          "lru_wi", "lru_bi", "lru_lambda", "sc_conv_w", "gn_lru", "gn_sc", "w_out", "ffn_norm", "ffn_mod_w",
          "ffn_mod_b", "dense_w1", "dense_w3", "dense_w2", "router_w", "router_b", "exp_w1", "exp_w3", "exp_w2",
          "final_norm"]


def kernel(**inputs):
    import numpy as np
    import concourse.bacc as bacc
    from concourse.bass_utils import run_bass_kernel_spmd

    nc = bacc.Bacc("TRN2", target_bir_lowering=False, num_devices=1)
    arrays = {f"in_{n}": np.ascontiguousarray(inputs[n]) for n in INPUTS}
    args = {n: nc.dram_tensor(f"in_{n}", arrays[f"in_{n}"].shape, F32, kind="ExternalInput").ap() for n in INPUTS}
    out = nc.dram_tensor("out", arrays["in_x"].shape, F32, kind="ExternalOutput")
    trunk_kernel(nc, out=out.ap(), **args)
    result = run_bass_kernel_spmd(nc, [arrays], core_ids=[0])
    return result.results[0]["out"]
```

```python
from contextlib import ExitStack

import concourse.bass as bass
from concourse import mybir

F32 = mybir.dt.float32
F32R = mybir.dt.float32r
I32 = mybir.dt.int32
U32 = mybir.dt.uint32
ALU = mybir.AluOpType
ACT = mybir.ActivationFunctionType
AX = mybir.AxisListType

P = 128
EPS = 1e-6
LRU_C = 8.0


def trunk_kernel(nc, x, c, mix_norm, mix_mod_w, mix_mod_b, w_in, lru_conv_w, lru_conv_b, lru_wa, lru_ba,
                 lru_wi, lru_bi, lru_lambda, sc_conv_w, gn_lru, gn_sc, w_out, ffn_norm, ffn_mod_w,
                 ffn_mod_b, dense_w1, dense_w3, dense_w2, router_w, router_b, exp_w1, exp_w3, exp_w2,
                 final_norm, out):
    _, T, D = x.shape
    DEPTH = w_in.shape[0]
    K = D // P
    TT = T // P
    DL = lru_conv_w.shape[2]
    J = DL // P
    LT, ST = lru_conv_w.shape[1], sc_conv_w.shape[1]
    HD = lru_wa.shape[2]
    FF = dense_w1.shape[2]
    FB = FF // P
    assert T == 512 and K == 8 and J == 4 and HD * 2 == P and DEPTH == 2 and FB == 22

    E = router_w.shape[2]
    FE = exp_w1.shape[3]
    FEB = FE // P
    EG = 4
    EC = FE // EG
    assert E == 8 and FE % P == 0 and FE % EG == 0 and EC <= 512 and D == 1024
    MAX_TILES = 2 * T // P + E - 1
    MIN_TILES = 2 * T // P
    MAX_TRIPS = 2 * T // (2 * P) + E - 1
    TR = MAX_TRIPS + 1
    W2_CUT = [0, 3, 6, 9, FEB]
    WHOLE = [0] + [(g + 1) * EC // P for g in range(EG)]
    EU = 2 * EG + len(W2_CUT) - 1
    EUF = max(K * EC, 3 * D)
    RAWS = 4
    AHEAD = 2
    assert EU % RAWS == 0 and EU % 2 == 0 and max(b - a for a, b in zip(WHOLE, WHOLE[1:])) * P <= 512

    UF = 2048
    WIN_U = w_in.shape[2] // (2 * P)
    WOUT_U = D // (2 * P)
    UP_U = FB
    DOWN_U = 2 * K
    U_WIN, U_WOUT = [0, 0], [0, 0]
    U_WOUT[0] = WIN_U
    U_UP = U_WOUT[0] + WOUT_U
    U_DOWN = U_UP + UP_U
    U_WIN[1] = U_DOWN + DOWN_U
    U_WOUT[1] = U_WIN[1] + WIN_U
    U_END = U_WOUT[1] + WOUT_U
    MC = 3 * P
    MG = 3 * D // MC
    KH = K // 2

    with ExitStack() as ctx:
        def sem(name):
            return ctx.enter_context(nc.semaphore(name))

        top = [-(-nc.sbuf_base // 32) * 32]

        def at(name, shape, dt, offset):
            return nc.alloc_sbuf_tensor_at(name, shape, dt, offset=offset)

        def place(name, shape, dt=F32):
            size = 4
            for n in shape[1:]:
                size *= n
            t = at(name, shape, dt, top[0])
            top[0] += -(-size // 32) * 32
            assert top[0] <= nc.sbuf_usable_end, (name, top[0])
            return t

        ident = place("ident", [P, P])
        spread = place("spread", [P, J, P])
        GR = 2 * J
        head_sel = place("head_sel", [P, 2 * GR])
        PT1R = 4 * 24 + 4 * K
        par1 = place("par1", [P, PT1R])
        R_CW, R_CB, R_BA, R_BI, R_LAM, R_SW, R_GL, R_GS, R_C, R_FN, R_END = (
            0, 32, 40, 48, 56, 64, 88, 96, 104, 112, 120)
        par2 = place("par2", [P, R_END])
        eps = place("eps", [P, 1])
        ones = place("ones", [P, 1])
        silu_c = place("silu_c", [P, K])
        ones_all = place("ones_all", [P, P])
        before = place("before", [P, P])
        rw = place("rw", [P, K, E])
        rb = place("rb", [P, 1])
        iota_i = place("iota_i", [P, 16], I32)
        iota_f = place("iota_f", [P, 16])
        pick_w = place("pick_w", [P, 2, TT])
        slots_i = place("slots_i", [P, 2, TT], U32)
        table = place("table", [P, 4, TR], I32)
        decay = place("decay", [P, 2, 2 * J])
        small = place("small", [P, 6, 2 * J])
        rstd = place("rstd", [P, TT])
        mods = place("mods", [P, 4, 24])
        mod_gain = place("mod_gain", [P, 4, K])
        tmp_a = place("tmp_a", [P, T])
        tmp_b = place("tmp_b", [P, T])
        xT = place("xT", [P, K, T])
        dense_at = top[0]
        h_hi = place("h_hi", [P, K, T], F32R)
        h_lo = place("h_lo", [P, K, T], F32R)
        mod_acc = place("mod_acc", [P, MC])
        mod_buf = place("mod_buf", [P, 2, KH, MC])
        raw = place("raw", [P, 2, UF])
        w_hi = place("w_hi", [P, 2, UF], F32R)
        w_lo = place("w_lo", [P, 2, UF], F32R)
        area = top[0]
        act_hi = place("act_hi", [P, FB, T], F32R)
        act_lo = place("act_lo", [P, FB, T], F32R)
        top[0] = area
        y_hi = place("y_hi", [P, K, T], F32R)
        y_lo = place("y_lo", [P, K, T], F32R)
        gate_w = place("gate_w", [P, 2, J, P])
        XPW = LT - 1 + T
        xpad = place("xpad", [P, J, XPW + 1])
        xc = place("xc", [P, J, T])
        gel = place("gel", [P, J, T])
        bsc = place("bsc", [P, J, T])
        tr = place("tr", [P, 2, T])
        ti = place("ti", [P, 2, T])
        tt = place("tt", [P, 2, T])
        ta = place("ta", [P, 2, T])
        CXW = ST - 1 + T
        cxpad = place("cxpad", [P, 2, CXW])
        csc = at("csc", [P, J, T], F32, area + 2 * 4 * K * T + 4 * 2 * J * P)
        hf = at("hf", [P, K, T], F32, area + 2 * 4 * K * T + 4 * 2 * J * P)
        diag_rstd = tmp_b
        xrow = at("xrow", [P, TT, D], F32, area)
        rows = at("rows", [P, 2, P], F32, dense_at + 2 * 4 * K * MC)
        first_at = area + 4 * TT * D
        mod_first = [at(f"mod_first{g}", [P, K, MC], F32,
                        dense_at + 4 * K * MC * g if g < 2 else first_at + 4 * K * MC * (g - 2)) for g in range(MG)]
        mod_acc1 = at("mod_acc1", [P, 3, MC], F32, dense_at + 2 * 4 * K * MC + 4 * 2 * P)
        first_acc = [(mod_acc[:], mod_acc1[:, 0]), (mod_acc1[:, 1], mod_acc1[:, 2])]
        assert 2 * 4 * K * MC + 4 * 2 * P + 4 * 3 * MC <= 2 * 4 * K * T and first_at + 4 * K * MC * (MG - 2) <= nc.sbuf_usable_end

        ZEROS = 4 * MG
        assert 2 * (MAX_TILES + 1 - MIN_TILES) % MG == 0 and 2 * (MAX_TILES + 1) % MG == 0 and GR <= HD
        top[0] = dense_at
        x_tok = place("x_tok", [P, TT, D])
        ht_hi = place("ht_hi", [P, K, 2 * P], F32R)
        ht_lo = place("ht_lo", [P, K, 2 * P], F32R)
        e_raw = place("e_raw", [P, RAWS, EUF])
        e_lo = at("e_lo", [P, RAWS, EUF], F32R, top[0] - 4 * RAWS * EUF)
        e_hi = place("e_hi", [P, RAWS, EUF], F32R)
        at_at = top[0]
        at_hi = place("at_hi", [P, FEB, 2 * P], F32R)
        at_lo = place("at_lo", [P, FEB, 2 * P], F32R)
        rows_at = top[0]
        h_rows = place("h_rows", [P, 2, D])
        hid = place("hid", [P, 2, FE])
        e_silu = place("e_silu", [P, 2, EC])
        y_rows = place("y_rows", [P, 2, D])
        hf3 = at("hf3", [P, K, T], F32, at_at)
        h_tok = at("h_tok", [P, TT, D], F32, rows_at)
        route_at = at_at + 4 * K * T + 4 * T
        rt = at("rt", [P, 16, TT, E], F32, route_at)
        lg = tmp_a
        LOGIT_BANK = 4
        rt_u = at("rt_u", [P, TT, E], U32, route_at + 4 * 16 * TT * E)
        ex = at("ex", [P, 16, E], F32, route_at + 4 * 17 * TT * E)
        tb = at("tb", [P, 8, TR], F32, route_at + 4 * 17 * TT * E + 4 * 16 * E)
        tv = at("tv", [P, 4, TR, E], F32, rows_at + 4 * TT * D)
        raw_at = dense_at + 4 * TT * D + 2 * 4 * K * 2 * P
        picked = at("picked", [P, TT, 2, D], F32, raw_at)
        gate_row = at("gate_row", [P, D], F32, raw_at + 32 * D)
        gain_row = at("gain_row", [P, D], F32, raw_at + 36 * D)
        diag = at("diag", [P, 2, K, P], F32, raw_at + 40 * D)
        mix = at("mix", [P, TT, D], F32, raw_at + 48 * D)
        sums = at("sums", [P, 3, TT], F32, raw_at + 64 * D)
        assert 66 * D <= 2 * 4 * RAWS * EUF

        h_sorted = nc.dram_tensor("h_sorted", ((MAX_TILES + 1) * P, D), F32)
        y_sorted = nc.dram_tensor("y_sorted", ((MAX_TILES + 1) * P, D), F32)

        banks = ctx.enter_context(nc.psum_tensor("banks", [P, 8, 512], F32))
        MODS_BANK = 7
        STAT_BANK = 6
        GATE_BANKS = (4, 5, 6)
        GROUP_BANK = 5
        SPREAD_BANKS = (4, 6)
        TOK_BANKS = (1, 2, 3, 7)

        const_ready = sem("const_ready")
        x_loaded = sem("x_loaded")
        rows_loaded = sem("rows_loaded")
        rows_turned = sem("rows_turned")
        par_ready = sem("par_ready")
        vec_link = sem("vec_link")
        act_link = sem("act_link")
        silu_ready = sem("silu_ready")
        decay_step = sem("decay_step")
        decay_ready = sem("decay_ready")
        xt_turned = sem("xt_turned")
        raw_loaded = [sem("raw_loaded0"), sem("raw_loaded1")]
        hi_done = sem("hi_done")
        lo_done = sem("lo_done")
        gemm_done = sem("gemm_done")
        proj_read = sem("proj_read")
        res_read = sem("res_read")
        pair_read = sem("pair_read")
        mod_loaded = [sem("mod_loaded0"), sem("mod_loaded1")]
        mod_first_in = [sem(f"mod_first_in{g}") for g in range(MG)]
        mod_step = sem("mod_step")
        mod_part = sem("mod_part")
        mod_mm = sem("mod_mm")
        mods_ready = sem("mods_ready")
        x_upd = sem("x_upd")
        sq_done = sem("sq_done")
        ssq_acc = sem("ssq_acc")
        stat_done = sem("stat_done")
        stat_read = sem("stat_read")
        rstd_ready = sem("rstd_ready")
        rstd_spread = sem("rstd_spread")
        xr_ready = sem("xr_ready")
        hf_done = sem("hf_done")
        hh_done = sem("hh_done")
        hl_done = sem("hl_done")
        gw_zero = sem("gw_zero")
        gw_loaded = sem("gw_loaded")
        xpad_ready = sem("xpad_ready")
        pad_ready = sem("pad_ready")
        xc_ready = sem("xc_ready")
        gate_done = sem("gate_done")
        gate_read = sem("gate_read")
        ta_ready = sem("ta_ready")
        v_ready = sem("v_ready")
        s_ready = sem("s_ready")
        scan_done = sem("scan_done")
        y_ready = sem("y_ready")
        ysq_done = sem("ysq_done")
        gsum_done = sem("gsum_done")
        groot_done = sem("groot_done")
        grstd_done = sem("grstd_done")
        gspread_done = sem("gspread_done")
        yn_done = sem("yn_done")
        yh_done = sem("yh_done")
        yl_done = sem("yl_done")
        silu_done = sem("silu_done")
        prod_done = sem("prod_done")
        ah_done = sem("ah_done")
        al_done = sem("al_done")
        out_stored = sem("out_stored")
        rw_loaded = sem("rw_loaded")
        iota_ready = sem("iota_ready")
        zeros_stored = sem("zeros_stored")
        logits_done = sem("logits_done")
        logits_read = sem("logits_read")
        tok_turned = sem("tok_turned")
        tok_read = sem("tok_read")
        mask_ready = sem("mask_ready")
        diff_ready = sem("diff_ready")
        diff_exp = sem("diff_exp")
        count_done = sem("count_done")
        slots_ready = sem("slots_ready")
        table_ready = sem("table_ready")
        sorted_stored = sem("sorted_stored")
        rows_in = sem("rows_in")
        ht_turned = sem("ht_turned")
        ht_hi_done = sem("ht_hi_done")
        ht_lo_done = sem("ht_lo_done")
        e_loaded = [sem(f"e_loaded{i}") for i in range(RAWS)]
        e_asked = sem("e_asked")
        e_hi_done = sem("e_hi_done")
        e_lo_done = sem("e_lo_done")
        e_used = sem("e_used")
        e_silu_done = sem("e_silu_done")
        hid_done = sem("hid_done")
        at_turned = sem("at_turned")
        at_hi_done = sem("at_hi_done")
        at_lo_done = sem("at_lo_done")
        y_read = sem("y_read")
        y_stored = sem("y_stored")
        y_free = sem("y_free")
        trips_over = sem("trips_over")
        diag_ready = sem("diag_ready")
        row_done = sem("row_done")
        row_ready = sem("row_ready")
        picked_in = [sem(f"picked_in{a}") for a in range(TT)]
        weighed = sem("weighed")
        mix_done = sem("mix_done")
        gated = sem("gated")
        xo_ready = sem("xo_ready")
        table_in = sem("table_in")
        osum_ready = sem("osum_ready")
        oroot_ready = sem("oroot_ready")
        o_ready = sem("o_ready")

        win_v = [w_in[l].rearrange("(k p) n -> p k n", p=P) for l in range(2)]
        wout_v = [w_out[l].rearrange("(k p) n -> p k n", p=P) for l in range(2)]
        w1_v = dense_w1[0].rearrange("(k p) n -> p k n", p=P)
        w3_v = dense_w3[0].rearrange("(k p) n -> p k n", p=P)
        w2_v = dense_w2[0].rearrange("(h f p) n -> p h f n", p=P, h=2)
        mod_w = [mix_mod_w[0], ffn_mod_w[0], mix_mod_w[1], ffn_mod_w[1]]
        mod_b = [mix_mod_b[0], ffn_mod_b[0], mix_mod_b[1], ffn_mod_b[1]]
        e1_v = exp_w1[0].rearrange("e (k p) n -> e p k n", p=P)
        e3_v = exp_w3[0].rearrange("e (k p) n -> e p k n", p=P)
        e2_v = exp_w2[0].rearrange("e (f p) n -> e p f n", p=P)
        hs_v = h_sorted.ap().rearrange("(t p) d -> p t d", p=P)
        ys_v = y_sorted.ap().rearrange("(t p) d -> p t d", p=P)
        FH = FB // 2
        DOWN_F = FH * P

        def k_of(t, s, n=K):
            return t[:, s, 0:n * (UF // K if n == K else P)].rearrange("p (k n) -> p k n", k=n)

        def block_of(t, n):
            return t[:, bass.ds(n, 1), :].rearrange("p a t -> p (a t)")

        block = ctx.enter_context(nc.Block())

        @block.sync
        def _(sp):
            sp.dma_start(xrow[:], x[0].rearrange("(a p) d -> p a d", p=P)).then_inc(x_loaded, 16)

            def first_loads(groups):
                view = mod_w[0].rearrange("(k p) n -> p k n", p=P)
                sp.wait_ge(rows_loaded, 16 * 16)
                for g in groups:
                    sp.dma_start(mod_first[g][:], view[:, :, g * MC:(g + 1) * MC]).then_inc(mod_first_in[g], 16)

            def free(u):
                if not isinstance(u, int) or u >= 2:
                    sp.wait_ge(lo_done, u - 1)

            def load_cols(view, col, s, u):
                free(u)
                sp.dma_start(k_of(raw, s), view[:, :, bass.ds(col, 2 * P)]).then_inc(raw_loaded[s], 16)

            def mixer_loads(l):
                if l == 0:
                    first_loads(range(MG))
                for s in range(2):
                    load_cols(win_v[l], 2 * P * s, s, U_WIN[l] + s)
                with sp.Fori(1, WIN_U // 2) as q:
                    for s in range(2):
                        load_cols(win_v[l], q * 4 * P + 2 * P * s, s, q * 2 + (U_WIN[l] + s))
                with sp.Fori(0, WOUT_U // 2) as q:
                    for s in range(2):
                        load_cols(wout_v[l], q * 4 * P + 2 * P * s, s, q * 2 + (U_WOUT[l] + s))

            mixer_loads(0)
            with sp.Fori(0, UP_U // 2) as g:
                for s in range(2):
                    free(g * 2 + (U_UP + s))
                    pair = raw[:, s, :].rearrange("p (w k n) -> p w k n", w=2, k=K)
                    for w, view in enumerate((w1_v, w3_v)):
                        sp.dma_start(pair[:, w], view[:, :, bass.ds(g * 2 * P + P * s, P)]).then_inc(raw_loaded[s], 16)
            with sp.Fori(0, K) as m:
                for s in range(2):
                    free(m * 2 + (U_DOWN + s))
                    sp.dma_start(raw[:, s, 0:DOWN_F].rearrange("p (f n) -> p f n", f=FH),
                                 w2_v[:, s, :, bass.ds(m * P, P)]).then_inc(raw_loaded[s], 16)
            mixer_loads(1)

            sp.wait_ge(table_ready, 1)
            sp.wait_ge(sorted_stored, 16 * 2 * TT)

            def e_load(e, i, j):
                if j < 2 * EG:
                    view = e1_v if j % 2 == 0 else e3_v
                    src = view[bass.ds(e, 1), :, :, EC * (j // 2):EC * (j // 2 + 1)].rearrange("e p k n -> p (e k) n")
                    dst = e_raw[:, j % RAWS, 0:K * EC].rearrange("p (k n) -> p k n", k=K)
                else:
                    f0, f1 = W2_CUT[j - 2 * EG], W2_CUT[j - 2 * EG + 1]
                    src = e2_v[bass.ds(e, 1), :, f0:f1, :].rearrange("e p f n -> p (e f) n")
                    dst = e_raw[:, j % RAWS, 0:(f1 - f0) * D].rearrange("p (f n) -> p f n", n=D)
                sp.wait_ge(e_used, i * EU + (j + 1))
                sp.sem_inc(e_asked, 1)
                sp.dma_start(dst, src).then_inc(e_loaded[j % RAWS], 16)

            first = sp.value_load(table[0:1, 0, 0:1], min_val=0, max_val=E - 1)
            for j in range(AHEAD):
                e_load(first, 0, j)
            trips = sp.value_load(table[0:1, 3, 0:1], min_val=1, max_val=MAX_TRIPS)
            with sp.Fori(0, trips) as i:
                e = sp.value_load(table[0:1, 0, bass.ds(i, 1)], min_val=0, max_val=E - 1)
                for j in range(AHEAD, EU):
                    e_load(e, i, j)
                following = sp.value_load(table[0:1, 0, bass.ds(i + 1, 1)], min_val=0, max_val=E - 1)
                for j in range(AHEAD):
                    e_load(following, i + 1, j)
            for a in range(TT):
                sp.wait_ge(o_ready, a + 1)
                sp.dma_start(out[0, a * P:(a + 1) * P, :], mix[:, a]).then_inc(out_stored, 16)
            sp.wait_ge(out_stored, 16 * TT)

        @block.gpsimd
        def _(pool):
            made = [0]

            def make(ins):
                made[0] += 1
                ins.then_inc(const_ready, 1)
                pool.wait_ge(const_ready, made[0])

            make(nc.gpsimd.memset(spread[:], 1.0))
            flat = spread[:].rearrange("r j p -> r (j p)")
            make(nc.gpsimd.affine_select(out=flat, in_=flat, compare_op=ALU.is_ge, fill=0.0, base=0,
                                         pattern=[[1, J * P]], channel_multiplier=-HD))
            make(nc.gpsimd.affine_select(out=flat, in_=flat, compare_op=ALU.is_ge, fill=0.0, base=HD - 1,
                                         pattern=[[-1, J * P]], channel_multiplier=HD))
            make(nc.gpsimd.memset(ident[:], 0.0))
            make(nc.gpsimd.affine_select(out=ident[:], in_=ident[:], compare_op=ALU.not_equal, fill=1.0, base=0,
                                         pattern=[[-1, P]], channel_multiplier=1))
            make(nc.gpsimd.memset(head_sel[:], 0.0))
            for h in range(2):
                part = slice(HD * h, HD * h + HD)
                make(nc.gpsimd.memset(head_sel[part, GR - 2 + h:GR - 1 + h], 1.0 / HD))
            make(nc.gpsimd.memset(eps[:], EPS))
            make(nc.gpsimd.memset(ones[:], 1.0))
            make(nc.gpsimd.memset(ones_all[:], 1.0))
            make(nc.gpsimd.memset(before[:], 1.0))
            make(nc.gpsimd.affine_select(out=before[:], in_=before[:], compare_op=ALU.is_gt, fill=0.0, base=0,
                                         pattern=[[1, P]], channel_multiplier=-1))
            nc.gpsimd.iota(iota_i[:], pattern=[[1, 16]], base=0, channel_multiplier=0).then_inc(iota_ready, 1)
            pool.dma_start(rw[:], router_w[0].rearrange("(k p) e -> p k e", p=P)).then_inc(rw_loaded, 16)
            pool.dma_start(rb[0:E, :], router_b.rearrange("l e -> e l")).then_inc(rw_loaded, 16)

            def mod_load(m, g, h):
                view = mod_w[m].rearrange("(h k p) n -> p h k n", p=P, h=2)
                pool.dma_start(mod_buf[:, h], view[:, h, :, bass.ds(g * MC, MC)]).then_inc(mod_loaded[h], 16)

            def mod_group(n, following):
                q = n - MG
                steps = [0]

                def step(ins):
                    steps[0] += 1
                    ins.then_inc(mod_part, 1)
                    pool.wait_ge(mod_part, q * 7 + steps[0])

                for h in range(2):
                    part = mod_buf[:, h]
                    scalars = silu_c[:, KH * h:KH * h + KH].unsqueeze(2).to_broadcast([P, KH, MC])
                    pool.wait_ge(mod_loaded[h], q * 16 + 16)
                    step(nc.gpsimd.tensor_tensor(part, part, scalars, ALU.mult))
                    step(nc.gpsimd.tensor_tensor(part[:, 0:2], part[:, 0:2], part[:, 2:4], ALU.add))
                    if h == 0:
                        pool.wait_ge(mod_mm, n + 1)
                        step(nc.gpsimd.tensor_tensor(mod_acc[:], part[:, 0], part[:, 1], ALU.add))
                    else:
                        step(nc.gpsimd.tensor_tensor(part[:, 0], part[:, 0], part[:, 1], ALU.add))
                        step(nc.gpsimd.tensor_tensor(mod_acc[:], mod_acc[:], part[:, 0], ALU.add))
                    following(h)

            def clear(g):
                for t, first in ((h_sorted, 0), (y_sorted, 2 * MIN_TILES)):
                    n = (2 * (MAX_TILES + 1) - first) // MG
                    view = t.ap().rearrange("(r p) (h n) -> p r h n", p=HD, n=J * P)
                    zeros = spread[HD:2 * HD].rearrange("p j c -> p (j c)").unsqueeze(1)
                    for h in range(2):
                        pool.dma_start(view[:, bass.ds(g * n + first, n), h],
                                       zeros.to_broadcast([HD, n, J * P])).then_inc(zeros_stored, 16)

            def mod_groups(m, first, last):
                end = min(last, MG - 1)
                if end - first == 1:
                    mod_group(MG * m + first, lambda h: mod_load(m, first + 1, h))
                else:
                    with pool.Fori(first, end) as g:
                        mod_group(g + MG * m, lambda h: mod_load(m, g + 1, h))
                        if m == 2:
                            clear(g)
                if last == MG:
                    if m == 2:
                        clear(MG - 1)
                    mod_group(MG * m + MG - 1, (lambda h: mod_load(m + 1, 0, h)) if m < 3 else (lambda h: None))

            def gate_loads(l):
                if l:
                    pool.wait_ge(gemm_done, 2 * U_WIN[1])
                    pool.wait_ge(hl_done, K * 3)
                else:
                    pool.wait_ge(mods_ready, 1)
                nc.gpsimd.memset(gate_w[:], 0.0).then_inc(gw_zero, 1)
                pool.wait_ge(gw_zero, l + 1)
                for g, w in enumerate((lru_wa, lru_wi)):
                    v = w[l].rearrange("(j h) i o -> h i j o", h=2)
                    for h in range(2):
                        part = slice(HD * h, HD * h + HD)
                        pool.dma_start(gate_w[part, g, :, part], v[h]).then_inc(gw_loaded, 16)

            def pads(l):
                pool.wait_ge(hl_done, K * (2 * l + 1))
                nc.gpsimd.memset(xpad[:, :, 0:LT - 1], 0.0).then_inc(pad_ready, 1)
                pool.wait_ge(pad_ready, 2 * l + 1)
                nc.gpsimd.memset(cxpad[:, :, 0:ST - 1], 0.0).then_inc(pad_ready, 1)
                pool.wait_ge(pad_ready, 2 * l + 2)

            pool.wait_ge(silu_ready, 1)
            pool.wait_ge(mod_first_in[MG - 2], 16)
            for h in range(2):
                mod_load(1, 0, h)
            for l in range(2):
                mod_groups(2 * l + 1, 0, 1)
                gate_loads(l)
                pads(l)
                mod_groups(2 * l + 1, 1, MG)
                if l == 0:
                    mod_groups(2, 0, MG)

            pool.wait_ge(zeros_stored, 16 * ZEROS)
            pool.wait_ge(slots_ready, 1)
            pool.wait_ge(tok_read, 2 * TT)
            for a in range(TT):
                for which in range(2):
                    pool.indirect_dma_start(
                        out=h_sorted.ap(), out_offset=bass.IndirectOffsetOnAxis(ap=slots_i[:, which, a:a + 1], axis=0),
                        in_=h_tok[:, a, :], in_offset=None).then_inc(sorted_stored, 16)
            pool.wait_ge(sorted_stored, 16 * 2 * TT)
            pool.wait_ge(table_ready, 1)

            def load_rows(i):
                t0 = pool.value_load(table[0:1, 1, bass.ds(i, 1)], min_val=0, max_val=MAX_TILES - 1)
                pool.dma_start(h_rows[:], hs_v[:, bass.ds(t0, 2), :]).then_inc(rows_in, 16)

            pool.sem_inc(y_free, 1)
            load_rows(0)
            trips = pool.value_load(table[0:1, 3, 0:1], min_val=1, max_val=MAX_TRIPS)
            with pool.Fori(0, trips) as i:
                pool.wait_ge(ht_turned, i * 4 + 4)
                load_rows(i + 1)
                pool.wait_ge(y_read, i + 2)
                t0 = pool.value_load(table[0:1, 1, bass.ds(i, 1)], min_val=0, max_val=MAX_TILES - 1)
                two = pool.value_load(table[0:1, 2, bass.ds(i, 1)], min_val=0, max_val=1)
                with pool.If(two > 0):
                    pool.dma_start(ys_v[:, bass.ds(t0, 2), :], y_rows[:]).then_inc(y_stored, 16)
                with pool.Else():
                    pool.dma_start(ys_v[:, bass.ds(t0, 1), :], y_rows[:, 0:1]).then_inc(y_stored, 16)
                pool.nop()
                pool.wait_ge(y_stored, i * 16 + 16)
                pool.sem_inc(y_free, 1)
            pool.wait_ge(rows_in, trips * 16 + 16)
            pool.nop()
            pool.wait_ge(e_lo_done, trips * EU + AHEAD)
            pool.sem_inc(trips_over, 1)
            pool.wait_ge(trips_over, 1)
            for a in range(TT):
                for which in range(2):
                    pool.indirect_dma_start(
                        out=picked[:, a, which, :], out_offset=None, in_=y_sorted.ap(),
                        in_offset=bass.IndirectOffsetOnAxis(ap=slots_i[:, which, a:a + 1], axis=0)
                    ).then_inc(picked_in[a], 16)
            pool.wait_ge(row_ready, 2)
            for a in range(TT):
                pool.wait_ge(mix_done, a + 1)
                nc.gpsimd.tensor_tensor(picked[:, a, 0], picked[:, a, 0], gate_row[:], ALU.mult).then_inc(gated, 1)

        BASE = {}
        BASE["win0"] = 0
        BASE["wout0"] = BASE["win0"] + 16 * WIN_U // 2
        BASE["up"] = BASE["wout0"] + 16 * WOUT_U // 2
        BASE["down"] = BASE["up"] + 32 * UP_U // 2
        BASE["win1"] = BASE["down"] + 16 * DOWN_U // 2
        BASE["wout1"] = BASE["win1"] + 16 * WIN_U // 2
        PHASES = [("win0", U_WIN[0], WIN_U), ("wout0", U_WOUT[0], WOUT_U), ("up", U_UP, UP_U),
                  ("down", U_DOWN, DOWN_U), ("win1", U_WIN[1], WIN_U), ("wout1", U_WOUT[1], WOUT_U)]

        SECOND = {1: U_UP + 1, 2: U_WIN[1] + 1}

        def unit_info(u):
            for name, first, n in PHASES:
                if first <= u < first + n:
                    per = 32 if name == "up" else 16
                    return BASE[name] + per * ((u - first) // 2 + 1), DOWN_F if name == "down" else UF
            return None

        @block.scalar
        def _(act):
            links = [0]

            def link(ins):
                links[0] += 1
                ins.then_inc(act_link, 1)
                act.wait_ge(act_link, links[0])

            def split(u, s, loaded=None, n=None):
                if loaded is None:
                    if u >= U_END:
                        return
                    loaded, n = unit_info(u)
                act.wait_ge(raw_loaded[s], loaded)
                if not isinstance(u, int) or u >= 2:
                    act.wait_ge(gemm_done, (u - 1) * 2)
                nc.scalar.activation(w_hi[:, s, 0:n], raw[:, s, 0:n], ACT.Copy).then_inc(hi_done, 1)

            for at_row, src in ((R_C, c.rearrange("b (r q) -> (b r) q", q=P)),
                                (R_CW, lru_conv_w.rearrange("l t (r q) -> (l t r) q", q=P)),
                                (R_CB, lru_conv_b.rearrange("l (r q) -> (l r) q", q=P)),
                                (R_BA, lru_ba.rearrange("l (r h) q -> (l r) (h q)", h=2)),
                                (R_BI, lru_bi.rearrange("l (r h) q -> (l r) (h q)", h=2)),
                                (R_LAM, lru_lambda.rearrange("l (r q) -> (l r) q", q=P)),
                                (R_SW, sc_conv_w.rearrange("l t (r q) -> (l t r) q", q=P)),
                                (R_GL, gn_lru.rearrange("l (r q) -> (l r) q", q=P)),
                                (R_GS, gn_sc.rearrange("l (r q) -> (l r) q", q=P)),
                                (R_FN, final_norm.rearrange("(r q) -> r q", q=P))):
                act.dma_start(rows[at_row:at_row + src.shape[0], 1, :], src).then_inc(rows_loaded, 16)
            act.dma_start(rows[0:24, 0, :], mod_b[0].rearrange("(r q) -> r q", q=P)).then_inc(rows_loaded, 16)
            for m in range(1, 4):
                act.dma_start(rows[24 * m:24 * m + 24, 0, :],
                             mod_b[m].rearrange("(r q) -> r q", q=P)).then_inc(rows_loaded, 16)
            act.dma_start(rows[96:96 + 2 * K, 0, :],
                         mix_norm.rearrange("l (r q) -> (l r) q", q=P)).then_inc(rows_loaded, 16)
            act.dma_start(rows[96 + 2 * K:96 + 4 * K, 0, :],
                         ffn_norm.rearrange("l (r q) -> (l r) q", q=P)).then_inc(rows_loaded, 16)
            act.sem_inc(proj_read, 4)
            act.sem_inc(ah_done, 1)
            act.sem_inc(e_silu_done, 1)
            act.wait_ge(par_ready, 2)
            nc.scalar.activation(silu_c[:], par2[:, R_C:R_C + K], ACT.Silu).then_inc(silu_ready, 1)
            link(nc.scalar.activation(small[:, 0], par2[:, R_LAM:R_LAM + 2 * J], ACT.Abs))
            nc.scalar.activation(small[:, 1], small[:, 0], ACT.Exp, scale=-1.0).then_inc(decay_step, 1)

            def square(n):
                act.wait_ge(x_upd, n + 1)
                if n >= 1:
                    act.wait_ge(ssq_acc, n)
                nc.scalar.activation(tmp_b[:], xT[:, n % K], ACT.Square).then_inc(sq_done, 1)

            for k in range(K):
                act.wait_ge(xt_turned, k + 1)
                nc.scalar.activation(xT[:, k], banks[:, k % 4], ACT.Copy).then_inc(x_upd, 1)
                square(k)

            def norm_root(nth):
                act.wait_ge(stat_done, nth + 1)
                nc.scalar.activation(rstd[:], banks[:, STAT_BANK, 0:TT], ACT.Sqrt, bias=eps[:],
                                     scale=1.0 / D).then_inc(stat_read, 1)

            def norm(nth):
                if nth > 0:
                    norm_root(nth)
                    split(SECOND[nth], 1)
                act.wait_ge(mods_ready, nth + 1)

                def modulate(k):
                    act.wait_ge(xr_ready, K * nth + k + 1)
                    nc.scalar.activation(hf[:, k], hf[:, k], ACT.Identity, bias=mods[:, nth, k:k + 1],
                                         scale=mod_gain[:, nth, k:k + 1]).then_inc(hf_done, 1)

                modulate(0)
                for k in range(K):
                    if k + 1 < K:
                        modulate(k + 1)
                    act.wait_ge(hf_done, K * nth + k + 1)
                    nc.scalar.activation(h_hi[:, k], hf[:, k], ACT.Copy).then_inc(hh_done, 1)

            def mixer(l):
                u0 = U_WIN[l]

                def evacuate(u, i):
                    q, j = u // 2, 2 * (u % 2) + i
                    act.wait_ge(gemm_done, 2 * (u0 + u) + 1 + i)
                    ps = banks[:, j]
                    if q == 0:
                        nc.scalar.activation(xpad[:, j, LT - 1:LT - 1 + T], ps, ACT.Copy).then_inc(xpad_ready, 1)
                        act.wait_ge(xpad_ready, J * l + j + 1)
                        act.sem_inc(proj_read, 1)
                    elif q == 1:
                        nc.scalar.activation(gel[:, j], ps, ACT.Gelu_apprx_tanh).then_inc(proj_read, 1)
                    elif q == 2:
                        nc.scalar.activation(bsc[:, j], ps, ACT.Copy).then_inc(proj_read, 1)
                    elif q == 3:
                        act.wait_ge(xc_ready, J * (l + 1))
                        nc.scalar.activation(csc[:, j], ps, ACT.Copy).then_inc(proj_read, 1)

                def gates(pair):
                    for b in range(2):
                        j = 2 * pair + b
                        n = 8 * l + 2 * j
                        if pair:
                            act.wait_ge(scan_done, J * l + b + 1)
                        act.wait_ge(gate_done, n + 1)
                        nc.scalar.activation(tr[:, b], banks[:, GATE_BANKS[n % 3]], ACT.Sigmoid,
                                             bias=par2[:, R_BA + J * l + j:R_BA + J * l + j + 1]).then_inc(gate_read, 1)
                        act.wait_ge(gate_done, n + 2)
                        nc.scalar.activation(ti[:, b], banks[:, GATE_BANKS[(n + 1) % 3]], ACT.Sigmoid,
                                             bias=par2[:, R_BI + J * l + j:R_BI + J * l + j + 1]).then_inc(gate_read, 1)
                    act.wait_ge(gate_read, 8 * l + 4 * pair + 4)
                    if pair == 0 and l == 0:
                        act.wait_ge(decay_ready, 1)
                    for b in range(2):
                        col = J * l + 2 * pair + b
                        nc.scalar.activation(tt[:, b], tr[:, b], ACT.Tanh, scale=decay[:, 0, col:col + 1]).then_inc(ta_ready, 1)
                        nc.scalar.activation(ta[:, b], tr[:, b], ACT.Exp, scale=decay[:, 1, col:col + 1]).then_inc(ta_ready, 1)

                def roots(pair):
                    for b in range(2):
                        act.wait_ge(v_ready, J * l + 2 * pair + b + 1)
                        nc.scalar.activation(tt[:, b], tt[:, b], ACT.Sqrt).then_inc(s_ready, 1)

                def group_roots(y, half):
                    for j in range(J):
                        n = 8 * l + 4 * half + j
                        act.wait_ge(y_ready, n + 1 if half else 8 * l + J)
                        if half or j >= 2:
                            act.wait_ge(gsum_done, n - 1)
                        nc.scalar.activation(tt[:, j % 2], y[:, j], ACT.Square).then_inc(ysq_done, 1)
                    act.wait_ge(gsum_done, 8 * l + 4 * half + J)
                    if half:
                        act.wait_ge(yn_done, 8 * l + J)
                    nc.scalar.activation(ta[0:GR, 0], banks[0:GR, GROUP_BANK], ACT.Sqrt,
                                         bias=eps[0:GR]).then_inc(groot_done, 1)

                def group_hi(y, half, j):
                    n = 8 * l + 4 * half + j
                    act.wait_ge(yn_done, n + 1)
                    nc.scalar.activation(y_hi[:, 4 * half + j], y[:, j], ACT.Copy).then_inc(yh_done, 1)

                for u in range(WIN_U):
                    for i in range(2):
                        if u // 2 < 4:
                            evacuate(u, i)
                    if u in (2, 4):
                        gates(u // 2 - 1)
                    split(u0 + u + 2, u % 2)
                    if u in (3, 5):
                        roots(u // 2 - 1)
                    if u == 7:
                        group_roots(xc, 0)
                        for j in range(J):
                            group_hi(xc, 0, j)
                group_roots(bsc, 1)
                for j in range(J):
                    group_hi(bsc, 1, j)
                n0 = 8 + 16 * l
                for u in range(WOUT_U):
                    for i in range(2):
                        square(n0 + 2 * u + i)
                    if u < WOUT_U - 1:
                        split(U_WOUT[l] + u + 2, u % 2)

            def hidden(g, s, ahead):
                n = g * 2 + s
                act.wait_ge(gemm_done, (n + U_UP) * 2 + 1)
                act.wait_ge(prod_done, n + 1)
                nc.scalar.activation(tmp_a[:], banks[:, 2 * s], ACT.Silu).then_inc(silu_done, 1)
                act.wait_ge(prod_done, n + 2)
                nc.scalar.activation(block_of(act_hi, n), tmp_b[:],
                                     ACT.Copy).then_inc(ah_done, 1)
                if ahead is None:
                    split(n + (U_UP + 2), s, BASE["up"] + 32 * (g + 2), UF)
                else:
                    split(ahead, s)

            norm_root(0)
            split(0, 0)
            split(1, 1)
            norm(0)
            mixer(0)
            norm(1)
            with act.Fori(0, UP_U // 2 - 1) as g:
                for s in range(2):
                    hidden(g, s, None)
            for s in range(2):
                hidden(UP_U // 2 - 1, s, U_DOWN + s)

            def down(m, bank, last):
                for s in range(2):
                    if not last:
                        split(m * 2 + (U_DOWN + 2 + s), s, m * 16 + (BASE["down"] + 32), DOWN_F)
                    elif s == 0:
                        split(U_WIN[1], 0)
                act.wait_ge(x_upd, m + (16 + 1))
                act.wait_ge(ssq_acc, m + 16)
                nc.scalar.activation(tmp_b[:], block_of(xT, m), ACT.Square).then_inc(sq_done, 1)

            with act.Fori(0, K // 2 - 1) as mm:
                for i in range(2):
                    down(mm * 2 + i, i, False)
            for i in range(2):
                down(K - 2 + i, i, i == 1)
            norm(2)
            mixer(1)

            act.wait_ge(stat_done, 4)
            nc.scalar.activation(rstd[:], banks[:, STAT_BANK, 0:TT], ACT.Sqrt, bias=eps[:],
                                 scale=1.0 / D).then_inc(stat_read, 1)
            act.wait_ge(mods_ready, 4)

            def copy_tokens(t, first, n):
                act.wait_ge(tok_turned, first + n + 1)
                nc.scalar.activation(t[:, n // 2, 512 * (n % 2):512 * (n % 2) + 512], banks[:, TOK_BANKS[n % 4]],
                                     ACT.Copy).then_inc(tok_read, 1)

            for k in range(K):
                act.wait_ge(xr_ready, 3 * K + k + 1)
                nc.scalar.activation(hf3[:, k], hf3[:, k], ACT.Identity, bias=mods[:, 3, k:k + 1],
                                     scale=mod_gain[:, 3, k:k + 1]).then_inc(hf_done, 1)
            for n in range(2 * TT):
                if n == TT:
                    act.wait_ge(diff_ready, 1)
                    nc.scalar.activation(rt[:, 13, 0, 0:TT], rt[:, 12, 0, 0:TT], ACT.Exp).then_inc(diff_exp, 1)
                copy_tokens(h_tok, 0, n)
            for n in range(2 * TT):
                copy_tokens(x_tok, 2 * TT, n)

            def ht_split(i):
                for n in range(4):
                    bank = (4, 5, 0, 1)[n]
                    act.wait_ge(ht_turned, i * 4 + (n + 1))
                    nc.scalar.activation(ht_hi[:, 4 * (n % 2):4 * (n % 2) + 4, P * (n // 2):P * (n // 2) + P],
                                         banks[:, bank].rearrange("p (k n) -> p k n", k=4), ACT.Copy).then_inc(ht_hi_done, 1)

            def y_copy():
                for b in range(4):
                    ins = nc.scalar.activation(y_rows[:, b // 2, 512 * (b % 2):512 * (b % 2) + 512],
                                               banks[:, (6, 7, 2, 3)[b]], ACT.Copy)
                ins.then_inc(y_read, 1)

            def e_split(i, j):
                n = K * EC if j < 2 * EG else (W2_CUT[j - 2 * EG + 1] - W2_CUT[j - 2 * EG]) * D
                act.wait_ge(e_loaded[j % RAWS], i * (16 * EU // RAWS) + 16 * (j // RAWS + 1))
                nc.scalar.activation(e_hi[:, j % RAWS, 0:n], e_raw[:, j % RAWS, 0:n], ACT.Copy).then_inc(e_hi_done, 1)

            def trip(i, tiles):
                def at_split(g):
                    f0, f1 = WHOLE[g], WHOLE[g + 1]
                    act.wait_ge(at_turned, i * EG + (g + 1))
                    for a in range(tiles):
                        ins = nc.scalar.activation(at_hi[:, f0:f1, P * a:P * a + P],
                                                   banks[:, 4 + a, 0:P * (f1 - f0)].rearrange("p (f n) -> p f n", n=P),
                                                   ACT.Copy)
                    ins.then_inc(at_hi_done, 1)

                act.wait_ge(e_used, i * EU + RAWS)
                y_copy()
                e_split(i, 2)
                for j in range(2 * EG + 1):
                    g = j // 2
                    if j < 2 * EG and j % 2 == 0:
                        act.wait_ge(e_used, i * EU + (j + 1 + RAWS))
                        act.wait_ge(hid_done, i * EG + (g + 1))
                        nc.scalar.activation(e_silu[:, 0:tiles], banks[:, 0:tiles, 0:EC], ACT.Silu).then_inc(e_silu_done, 1)
                    e_split(i, j + 3)
                    if j in (3, 5, 7):
                        at_split((j - 3) // 2)
                    if j == 8:
                        at_split(3)
                act.wait_ge(y_free, i + 1)
                e_split(i + 1, 0)
                ht_split(i + 1)
                e_split(i + 1, 1)

            for j in range(AHEAD):
                e_split(0, j)
            ht_split(0)
            trips = act.value_load(table[0:1, 3, 0:1], min_val=1, max_val=MAX_TRIPS)
            with act.Fori(0, trips) as i:
                two = act.value_load(table[0:1, 2, bass.ds(i, 1)], min_val=0, max_val=1)
                with act.If(two > 0):
                    trip(i, 2)
                with act.Else():
                    trip(i, 1)
                act.nop()
            act.wait_ge(e_used, trips * EU + RAWS)
            y_copy()
            for which, t in enumerate((gate_row, gain_row)):
                for b in range(2):
                    act.wait_ge(row_done, 2 * which + b + 1)
                    nc.scalar.activation(t[:, 512 * b:512 * b + 512], banks[:, 2 * which + b], ACT.Copy).then_inc(row_ready, 1)

            def weigh(a):
                act.wait_ge(picked_in[a], 32)
                nc.scalar.activation(picked[:, a, 0], picked[:, a, 0], ACT.Identity,
                                     scale=pick_w[:, 0, a:a + 1]).then_inc(weighed, 1)

            def root(a):
                act.wait_ge(xo_ready, a + 1)
                nc.scalar.activation(mix[:, a], x_tok[:, a], ACT.Square, accum_out=sums[:, 0, a:a + 1]).then_inc(osum_ready, 1)
                act.wait_ge(osum_ready, a + 1)
                nc.scalar.activation(sums[:, 1, a:a + 1], sums[:, 0, a:a + 1], ACT.Sqrt, bias=eps[:],
                                     scale=1.0 / D).then_inc(oroot_ready, 1)

            for a in range(TT):
                weigh(a)
                if a == 0:
                    nc.scalar.activation(mix[:, 0, 0:1], eps[:], ACT.Sqrt).then_inc(table_in, 1)
            act.wait_ge(table_in, 1)
            for a in range(TT):
                root(a)

        @block.vector
        def _(dve):
            links = [0]

            def link(ins):
                links[0] += 1
                ins.then_inc(vec_link, 1)
                dve.wait_ge(vec_link, links[0])

            def note(ins):
                links[0] += 1
                ins.then_inc(vec_link, 1)

            def linked():
                dve.wait_ge(vec_link, links[0])

            def split(u, s, n=None):
                if n is None:
                    if u >= U_END:
                        return
                    n = unit_info(u)[1]
                dve.wait_ge(hi_done, u + 1)
                nc.vector.tensor_tensor(w_lo[:, s, 0:n], raw[:, s, 0:n], w_hi[:, s, 0:n].bitcast(F32),
                                        ALU.subtract).then_inc(lo_done, 1)

            def mod_group(n):
                if n >= 2:
                    dve.wait_ge(mod_mm, n)
                dve.wait_ge(mod_first_in[n], 16)
                for k in range(K):
                    scalar = silu_c[:, k:k + 1]
                    acc = first_acc[n % 2][k % 2]
                    if k < 2:
                        ins = nc.vector.tensor_scalar(acc, mod_first[n][:, k], scalar, None, ALU.mult)
                    else:
                        dve.wait_ge(mod_step, n * K + k - 1)
                        ins = nc.vector.scalar_tensor_tensor(out=acc, in0=mod_first[n][:, k], scalar=scalar,
                                                             in1=acc, op0=ALU.mult, op1=ALU.add)
                    ins.then_inc(mod_step, 1)

            def mod_finish(m):
                dve.wait_ge(mod_mm, MG * (m + 1) + 1)
                link(nc.vector.tensor_tensor(mods[:, m], banks[:, MODS_BANK, 24 * m:24 * m + 24],
                                             par1[:, 24 * m:24 * m + 24], ALU.add))
                gain = 96 + (2 * K if m % 2 else 0) + K * (m // 2)
                nc.vector.scalar_tensor_tensor(out=mod_gain[:, m], in0=mods[:, m, K:2 * K], scalar=1.0,
                                               in1=par1[:, gain:gain + K], op0=ALU.add,
                                               op1=ALU.mult).then_inc(mods_ready, 1)

            def add_square(n):
                dve.wait_ge(sq_done, n + 1)
                if n % K == 0:
                    nc.vector.tensor_copy(tmp_a[:], tmp_b[:]).then_inc(ssq_acc, 1)
                else:
                    dve.wait_ge(ssq_acc, n)
                    nc.vector.tensor_tensor(tmp_a[:], tmp_a[:], tmp_b[:], ALU.add).then_inc(ssq_acc, 1)

            def norm_root(nth):
                dve.wait_ge(stat_read, nth + 1)
                nc.vector.reciprocal(rstd[:], rstd[:]).then_inc(rstd_ready, 1)
                dve.wait_ge(rstd_ready, 2 * nth + 1)
                nc.vector.tensor_tensor(diag_rstd[:].rearrange("p (a n) -> p a n", a=TT),
                                        ident[:].unsqueeze(1).to_broadcast([P, TT, P]),
                                        rstd[:].unsqueeze(2).to_broadcast([P, TT, P]), ALU.mult).then_inc(rstd_ready, 1)

            def norm(nth):
                if nth > 0:
                    norm_root(nth)
                    mod_finish(nth)
                dve.wait_ge(rstd_spread, nth + 1)
                for k in range(K + 2):
                    if k < K:
                        nc.vector.tensor_tensor(hf[:, k], xT[:, k], banks[:, STAT_BANK], ALU.mult).then_inc(xr_ready, 1)
                    if k >= 2:
                        dve.wait_ge(hh_done, K * nth + k - 1)
                        nc.vector.tensor_tensor(h_lo[:, k - 2], hf[:, k - 2], h_hi[:, k - 2].bitcast(F32),
                                                ALU.subtract).then_inc(hl_done, 1)
                    if nth == 0 and k in (2, 5):
                        split(k // 3, k // 3)
                    elif nth > 0 and k == 5:
                        split(SECOND[nth], 1)

            def residual(n, m, bank, nth, count):
                dve.wait_ge(gemm_done, count)
                xm = block_of(xT, m)
                gate = mods[:, nth, bass.ds(m + 2 * K, 1)]
                nc.vector.scalar_tensor_tensor(out=xm, in0=banks[:, bank], scalar=gate, in1=xm,
                                               op0=ALU.mult, op1=ALU.add).then_inc(x_upd, 1)
                dve.wait_ge(x_upd, n + 1)
                dve.sem_inc(res_read, 1)

            dve.sem_inc(res_read, 4)
            dve.sem_inc(pair_read, 2)
            for first in (prod_done, al_done, hid_done, at_lo_done):
                dve.sem_inc(first, 1)
            dve.wait_ge(rows_turned, 1)
            nc.vector.tensor_copy(par1[:], banks[:, 4, 0:PT1R]).then_inc(par_ready, 1)
            dve.wait_ge(rows_turned, 2)
            nc.vector.tensor_copy(par2[:], banks[:, 5, 0:R_END]).then_inc(par_ready, 1)
            for k in range(K):
                add_square(k)
            dve.wait_ge(silu_ready, 1)
            for g in range(MG):
                mod_group(g)
                if g == 2:
                    norm_root(0)
            def decays():
                dve.wait_ge(decay_step, 1)
                z, w, w2, acc, low = (small[:, i] for i in (1, 2, 3, 4, 5))
                link(nc.vector.tensor_scalar(w, z, 2.0, None, ALU.add))
                link(nc.vector.reciprocal(w, w))
                link(nc.vector.tensor_tensor(w, w, z, ALU.mult))
                link(nc.vector.tensor_tensor(w2, w, w, ALU.mult))
                link(nc.vector.tensor_scalar(acc, w2, 1.0 / 19, 1.0 / 17, ALU.mult, ALU.add))
                for odd in range(15, 0, -2):
                    link(nc.vector.tensor_tensor(acc, acc, w2, ALU.mult))
                    link(nc.vector.tensor_scalar(acc, acc, 1.0 / odd, None, ALU.add))
                link(nc.vector.tensor_tensor(acc, acc, w, ALU.mult))
                link(nc.vector.tensor_scalar(low, par2[:, R_LAM:R_LAM + 2 * J], -1.0, 0.0, ALU.mult, ALU.max))
                link(nc.vector.scalar_tensor_tensor(out=acc, in0=acc, scalar=2.0, in1=low, op0=ALU.mult, op1=ALU.add))
                nc.vector.tensor_scalar(decay[:, 1], acc, -LRU_C, None, ALU.mult)
                nc.vector.tensor_scalar(decay[:, 0], acc, LRU_C, None, ALU.mult).then_inc(decay_ready, 1)

            def mixer(l):
                u0 = U_WIN[l]
                m_next = 2 * l + 1

                def conv_lru(j):
                    dve.wait_ge(xpad_ready, J * l + j + 1)
                    w = [par2[:, R_CW + 4 * J * l + J * t + j:R_CW + 4 * J * l + J * t + j + 1] for t in range(LT)]
                    b = par2[:, R_CB + J * l + j:R_CB + J * l + j + 1]
                    link(nc.vector.tensor_scalar(xc[:, j], xpad[:, j, LT - 1:LT - 1 + T], w[LT - 1], b, ALU.mult, ALU.add))
                    for t in range(LT - 1):
                        ins = nc.vector.scalar_tensor_tensor(out=xc[:, j], in0=xpad[:, j, t:t + T], scalar=w[t],
                                                             in1=xc[:, j], op0=ALU.mult, op1=ALU.add)
                        if t < LT - 2:
                            link(ins)
                    ins.then_inc(xc_ready, 1)

                def to_v(pair):
                    for b in range(2):
                        dve.wait_ge(ta_ready, 2 * (J * l + 2 * pair + b) + 2)
                        link(nc.vector.tensor_scalar(tr[:, b], tt[:, b], 1.0, None, ALU.add))
                        link(nc.vector.reciprocal(tr[:, b], tr[:, b]))
                        nc.vector.scalar_tensor_tensor(out=tt[:, b], in0=tt[:, b], scalar=2.0, in1=tr[:, b],
                                                       op0=ALU.mult, op1=ALU.mult).then_inc(v_ready, 1)
                        link(nc.vector.tensor_tensor(ti[:, b], ti[:, b], xc[:, 2 * pair + b], ALU.mult))

                def scans(pair):
                    for b in range(2):
                        j = 2 * pair + b
                        dve.wait_ge(s_ready, J * l + j + 1)
                        link(nc.vector.tensor_tensor(ti[:, b], ti[:, b], tt[:, b], ALU.mult))
                        nc.vector.tensor_tensor_scan(xc[:, j], ta[:, b], ti[:, b], 0.0, ALU.mult,
                                                     ALU.add).then_inc(scan_done, 1)
                        dve.wait_ge(scan_done, J * l + j + 1)
                        nc.vector.tensor_tensor(xc[:, j], xc[:, j], gel[:, j], ALU.mult).then_inc(y_ready, 1)

                def gated_conv(j):
                    dve.wait_ge(gemm_done, 2 * (u0 + 8 + j // 2) + 1 + j % 2)
                    link(nc.vector.tensor_tensor(cxpad[:, j % 2, ST - 1:CXW], banks[:, j], csc[:, j], ALU.mult))
                    dve.sem_inc(proj_read, 1)
                    w = [par2[:, R_SW + ST * J * l + J * t + j:R_SW + ST * J * l + J * t + j + 1] for t in range(ST)]
                    link(nc.vector.tensor_scalar(ti[:, j % 2], cxpad[:, j % 2, ST - 1:CXW], w[ST - 1], None, ALU.mult))
                    for t in range(ST - 1):
                        link(nc.vector.scalar_tensor_tensor(out=ti[:, j % 2], in0=cxpad[:, j % 2, t:t + T], scalar=w[t],
                                                            in1=ti[:, j % 2], op0=ALU.mult, op1=ALU.add))
                    nc.vector.tensor_tensor(bsc[:, j], bsc[:, j], ti[:, j % 2], ALU.mult).then_inc(y_ready, 1)

                def group_norm(y, half):
                    dve.wait_ge(groot_done, 2 * l + half + 1)
                    nc.vector.reciprocal(ta[0:GR, 0], ta[0:GR, 0]).then_inc(grstd_done, 1)
                    for j in range(J):
                        col = (R_GS if half else R_GL) + J * l + j
                        dve.wait_ge(gspread_done, 8 * l + 4 * half + j + 1)
                        nc.vector.scalar_tensor_tensor(out=y[:, j], in0=y[:, j], scalar=par2[:, col:col + 1],
                                                       in1=banks[:, SPREAD_BANKS[j % 2]], op0=ALU.mult,
                                                       op1=ALU.mult).then_inc(yn_done, 1)

                def group_lo(y, half, j):
                    dve.wait_ge(yh_done, 8 * l + 4 * half + j + 1)
                    nc.vector.tensor_tensor(y_lo[:, 4 * half + j], y[:, j], y_hi[:, 4 * half + j].bitcast(F32),
                                            ALU.subtract).then_inc(yl_done, 1)

                for u in range(WIN_U):
                    if u == 9:
                        gated_conv(0)
                        gated_conv(1)
                    split(u0 + u + 2, u % 2)
                    if u == 0:
                        dve.wait_ge(pad_ready, 2 * l + 2)
                        conv_lru(0)
                        conv_lru(1)
                    if u == 1:
                        conv_lru(2)
                        conv_lru(3)
                    if u in (2, 4):
                        to_v(u // 2 - 1)
                    if u in (3, 5):
                        scans(u // 2 - 1)
                    if u == 7:
                        group_norm(xc, 0)
                        for j in range(J):
                            group_lo(xc, 0, j)
                gated_conv(2)
                gated_conv(3)
                group_norm(bsc, 1)
                for j in range(J):
                    group_lo(bsc, 1, j)
                n0 = 8 + 16 * l
                for u in range(WOUT_U):
                    for i in range(2):
                        n = n0 + 2 * u + i
                        residual(n, 2 * u + i, (2 * u + i) % 4, 2 * l, 2 * (U_WOUT[l] + u) + 1 + i)
                        if i == 1 and u < WOUT_U - 1:
                            split(U_WOUT[l] + u + 2, u % 2)
                        add_square(n)

            def hidden(g, s, ahead):
                n = g * 2 + s
                dve.wait_ge(gemm_done, (n + U_UP) * 2 + 2)
                dve.wait_ge(silu_done, n + 1)
                dve.wait_ge(ah_done, n + 1)
                dve.wait_ge(al_done, n + 1)
                nc.vector.tensor_tensor(tmp_b[:], banks[:, 2 * s + 1], tmp_a[:], ALU.mult).then_inc(prod_done, 1)
                dve.wait_ge(prod_done, n + 2)
                dve.sem_inc(pair_read, 1)
                dve.wait_ge(ah_done, n + 2)
                nc.vector.tensor_tensor(block_of(act_lo, n), tmp_b[:],
                                        block_of(act_hi, n).bitcast(F32),
                                        ALU.subtract).then_inc(al_done, 1)
                if ahead is None:
                    split(n + (U_UP + 2), s, UF)
                else:
                    split(ahead, s)

            mod_finish(0)
            norm(0)
            decays()
            mixer(0)
            norm(1)
            with dve.Fori(0, UP_U // 2 - 1) as g:
                hidden(g, 0, None)
                hidden(g, 1, None)
            for s in range(2):
                hidden(UP_U // 2 - 1, s, U_DOWN + s)
            link(nc.vector.memset(tmp_a[:], 0.0))

            def down(m, bank, last):
                for s in range(2):
                    if not last:
                        split(m * 2 + (U_DOWN + 2 + s), s, DOWN_F)
                    elif s == 0:
                        split(U_WIN[1], 0)
                residual(m + 16, m, bank, 1, m * 4 + (2 * U_DOWN + 4))
                dve.wait_ge(sq_done, m + 17)
                dve.wait_ge(ssq_acc, m + 16)
                nc.vector.tensor_tensor(tmp_a[:], tmp_a[:], tmp_b[:], ALU.add).then_inc(ssq_acc, 1)

            with dve.Fori(0, K // 2 - 1) as mm:
                for i in range(2):
                    down(mm * 2 + i, i, False)
            for i in range(2):
                down(K - 2 + i, i, i == 1)
            norm(2)
            mixer(1)

            norm_root(3)
            mod_finish(3)
            dve.wait_ge(rstd_spread, 4)
            for k in range(K):
                nc.vector.tensor_tensor(hf3[:, k], xT[:, k], banks[:, STAT_BANK], ALU.mult).then_inc(xr_ready, 1)
            dve.wait_ge(iota_ready, 1)
            link(nc.vector.tensor_copy(iota_f[:], iota_i[:]))
            logits, best, best_i, m1, m2, mask, pre, tot, slot = (rt[:, n] for n in range(9))
            dve.wait_ge(logits_done, 1)
            dve.wait_ge(rw_loaded, 32)
            nc.vector.tensor_scalar(lg[0:E], banks[0:E, 0], rb[0:E], None, ALU.add).then_inc(logits_read, 1)
            dve.wait_ge(logits_done, 2)
            link(nc.vector.tensor_copy(logits, banks[:, LOGIT_BANK, 0:TT * E].rearrange("p (a e) -> p a e", a=TT)))
            for a in range(TT):
                note(nc.vector.max(best[:, a], logits[:, a]))
            linked()
            for a in range(TT):
                note(nc.vector.max_index(rt_u[:, a], best[:, a], logits[:, a]))
            linked()
            link(nc.vector.tensor_copy(best_i, rt_u[:]))
            for a in range(TT):
                for m, n in ((m1, 0), (m2, 1)):
                    note(nc.vector.tensor_scalar(m[:, a], iota_f[:, 0:E], best_i[:, a, n:n + 1], None, ALU.is_equal))
            linked()
            nc.vector.tensor_tensor(mask, m1, m2, ALU.add).then_inc(mask_ready, 1)
            diff, e2 = rt[:, 12, 0, 0:TT], rt[:, 13, 0, 0:TT]
            nc.vector.tensor_tensor(diff, best[:, :, 1], best[:, :, 0], ALU.subtract).then_inc(diff_ready, 1)
            dve.wait_ge(count_done, 1)
            link(nc.vector.tensor_copy(pre, banks[:, 5, 0:TT * E].rearrange("p (a e) -> p a e", a=TT)))
            link(nc.vector.tensor_copy(tot, banks[:, 5, TT * E:2 * TT * E].rearrange("p (a e) -> p a e", a=TT)))
            count, tiles_n, trips_n, tile_c, trip_c, one8, tile0, trip0, run = (ex[:, n] for n in range(9))
            link(nc.vector.tensor_tensor(count, tot[:, 0], tot[:, 1], ALU.add))
            for a in range(2, TT):
                link(nc.vector.tensor_tensor(count, count, tot[:, a], ALU.add))
            link(nc.vector.memset(one8, 1.0))
            link(nc.vector.tensor_scalar(tiles_n, count, 0.0, None, ALU.is_gt))
            for n in range(1, TT):
                link(nc.vector.scalar_tensor_tensor(out=tiles_n, in0=count, scalar=float(P * n), in1=tiles_n,
                                                    op0=ALU.is_gt, op1=ALU.add))
            link(nc.vector.tensor_scalar(trips_n, count, 0.0, None, ALU.is_gt))
            for n in range(1, TT // 2):
                link(nc.vector.scalar_tensor_tensor(out=trips_n, in0=count, scalar=float(2 * P * n), in1=trips_n,
                                                    op0=ALU.is_gt, op1=ALU.add))
            link(nc.vector.tensor_tensor_scan(tile_c, one8, tiles_n, 0.0, ALU.mult, ALU.add))
            link(nc.vector.tensor_tensor_scan(trip_c, one8, trips_n, 0.0, ALU.mult, ALU.add))
            link(nc.vector.tensor_tensor(tile0, tile_c, tiles_n, ALU.subtract))
            link(nc.vector.tensor_tensor(trip0, trip_c, trips_n, ALU.subtract))
            link(nc.vector.tensor_scalar(run, tile0, float(P), None, ALU.mult))
            for a in range(TT):
                link(nc.vector.tensor_tensor(slot[:, a], pre[:, a], run, ALU.add))
                if a < TT - 1:
                    link(nc.vector.tensor_tensor(run, run, tot[:, a], ALU.add))
            for which, m in enumerate((m1, m2)):
                link(nc.vector.tensor_tensor(rt[:, 9 + which], m, slot, ALU.mult))
                link(nc.vector.tensor_reduce(rt[:, 11, which, 0:TT], rt[:, 9 + which], AX.X, ALU.add))
                ins = nc.vector.tensor_copy(slots_i[:, which], rt[:, 11, which, 0:TT])
                if which == 0:
                    link(ins)
            ins.then_inc(slots_ready, 1)
            expert, first, after, one = (tb[:, n] for n in range(4))
            begun, over, theirs, theirs_c = (tv[:, n] for n in range(4))
            number = iota_f[:, 0:TR]
            numbers = number.unsqueeze(2).to_broadcast([P, TR, E])

            def per_trip(v):
                return v.unsqueeze(1).to_broadcast([P, TR, E])

            note(nc.vector.scalar_tensor_tensor(out=run, in0=trip0, scalar=-2.0, in1=tile0, op0=ALU.mult, op1=ALU.add))
            note(nc.vector.tensor_tensor(begun, numbers, per_trip(trip0), ALU.is_ge))
            note(nc.vector.tensor_tensor(over, numbers, per_trip(trip_c), ALU.is_ge))
            linked()
            note(nc.vector.tensor_reduce(expert, over, AX.X, ALU.add))
            link(nc.vector.tensor_tensor(begun, begun, over, ALU.subtract))
            note(nc.vector.tensor_tensor(theirs, begun, per_trip(run), ALU.mult))
            note(nc.vector.tensor_tensor(theirs_c, begun, per_trip(tile_c), ALU.mult))
            linked()
            note(nc.vector.tensor_reduce(first, theirs, AX.X, ALU.add))
            note(nc.vector.tensor_reduce(after, theirs_c, AX.X, ALU.add))
            linked()
            link(nc.vector.scalar_tensor_tensor(out=first, in0=number, scalar=2.0, in1=first, op0=ALU.mult, op1=ALU.add))
            link(nc.vector.tensor_tensor(one, after, first, ALU.subtract))
            link(nc.vector.tensor_scalar(one, one, 2.0, None, ALU.is_ge))
            link(nc.vector.tensor_scalar(expert, expert, float(E - 1), None, ALU.min))
            link(nc.vector.tensor_scalar(first, first, float(MAX_TILES - 1), None, ALU.min))
            link(nc.vector.tensor_copy(table[:, 0], expert))
            link(nc.vector.tensor_copy(table[:, 1], first))
            link(nc.vector.tensor_copy(table[:, 2], one))
            nc.vector.tensor_copy(table[:, 3, 0:1], trip_c[:, E - 1:E]).then_inc(table_ready, 1)
            dve.wait_ge(diff_exp, 1)
            link(nc.vector.tensor_scalar(pick_w[:, 0], e2, 1.0, None, ALU.add))
            link(nc.vector.reciprocal(pick_w[:, 0], pick_w[:, 0]))
            link(nc.vector.tensor_tensor(pick_w[:, 1], pick_w[:, 0], e2, ALU.mult))

            def ht_split(i):
                for n in range(4):
                    bank = (4, 5, 0, 1)[n]
                    part = (slice(None), slice(4 * (n % 2), 4 * (n % 2) + 4), slice(P * (n // 2), P * (n // 2) + P))
                    dve.wait_ge(ht_hi_done, i * 4 + (n + 1))
                    nc.vector.tensor_tensor(ht_lo[part], banks[:, bank].rearrange("p (k n) -> p k n", k=4),
                                            ht_hi[part].bitcast(F32), ALU.subtract).then_inc(ht_lo_done, 1)

            def e_split(i, j):
                n = K * EC if j < 2 * EG else (W2_CUT[j - 2 * EG + 1] - W2_CUT[j - 2 * EG]) * D
                dve.wait_ge(e_hi_done, i * EU + (j + 1))
                nc.vector.tensor_tensor(e_lo[:, j % RAWS, 0:n], e_raw[:, j % RAWS, 0:n],
                                        e_hi[:, j % RAWS, 0:n].bitcast(F32),
                                        ALU.subtract).then_inc(e_lo_done, 1)

            def trip(i, tiles):
                def at_split(g):
                    f0, f1 = WHOLE[g], WHOLE[g + 1]
                    dve.wait_ge(at_hi_done, i * EG + (g + 1))
                    for a in range(tiles):
                        part = (slice(None), slice(f0, f1), slice(P * a, P * a + P))
                        ins = nc.vector.tensor_tensor(at_lo[part],
                                                      banks[:, 4 + a, 0:P * (f1 - f0)].rearrange("p (f n) -> p f n", n=P),
                                                      at_hi[part].bitcast(F32), ALU.subtract)
                    ins.then_inc(at_lo_done, 1)

                e_split(i, 2)
                for j in range(2 * EG + 1):
                    g = j // 2
                    if j < 2 * EG and j % 2 == 1:
                        dve.wait_ge(e_used, i * EU + (j + 1 + RAWS))
                        dve.wait_ge(e_silu_done, i * EG + (g + 2))
                        nc.vector.tensor_tensor(hid[:, 0:tiles, EC * g:EC * g + EC], banks[:, 2:2 + tiles, 0:EC],
                                                e_silu[:, 0:tiles], ALU.mult).then_inc(hid_done, 1)
                    e_split(i, j + 3)
                    if j in (3, 5, 7):
                        at_split((j - 3) // 2)
                    if j == 8:
                        at_split(3)
                e_split(i + 1, 0)
                ht_split(i + 1)
                e_split(i + 1, 1)

            for j in range(AHEAD):
                e_split(0, j)
            ht_split(0)
            trips = dve.value_load(table[0:1, 3, 0:1], min_val=1, max_val=MAX_TRIPS)
            with dve.Fori(0, trips) as i:
                two = dve.value_load(table[0:1, 2, bass.ds(i, 1)], min_val=0, max_val=1)
                with dve.If(two > 0):
                    trip(i, 2)
                with dve.Else():
                    trip(i, 1)
                dve.nop()

            dve.wait_ge(e_lo_done, trips * EU + AHEAD)
            dve.wait_ge(e_used, trips * EU + RAWS)
            for k in range(K):
                nc.vector.tensor_scalar(diag[:, 0, k], ident[:], mods[:, 3, 2 * K + k:2 * K + k + 1], None,
                                        ALU.mult).then_inc(diag_ready, 1)
            for k in range(K):
                nc.vector.tensor_scalar(diag[:, 1, k], ident[:], par2[:, R_FN + k:R_FN + k + 1], None,
                                        ALU.mult).then_inc(diag_ready, 1)
            def last_norm(a):
                dve.wait_ge(oroot_ready, a + 1)
                link(nc.vector.reciprocal(sums[:, 2, a:a + 1], sums[:, 1, a:a + 1]))
                nc.vector.scalar_tensor_tensor(out=mix[:, a], in0=x_tok[:, a], scalar=sums[:, 2, a:a + 1],
                                               in1=gain_row[:], op0=ALU.mult, op1=ALU.mult).then_inc(o_ready, 1)

            def add_second(a):
                dve.wait_ge(weighed, a + 1)
                nc.vector.scalar_tensor_tensor(out=picked[:, a, 0], in0=picked[:, a, 1], scalar=pick_w[:, 1, a:a + 1],
                                               in1=picked[:, a, 0], op0=ALU.mult, op1=ALU.add).then_inc(mix_done, 1)

            def add_stream(a):
                dve.wait_ge(gated, a + 1)
                nc.vector.tensor_tensor(x_tok[:, a], x_tok[:, a], picked[:, a, 0], ALU.add).then_inc(xo_ready, 1)

            dve.wait_ge(row_ready, 4)
            for step in range(TT + 3):
                if step < TT:
                    add_second(step)
                if 0 <= step - 2 < TT:
                    add_stream(step - 2)
                if 0 <= step - 3 < TT:
                    last_norm(step - 3)

        @block.tensor
        def _(pe):
            def product(ps, hi, lo, x_hi, x_lo, start, stop):
                nc.tensor.matmul(ps, hi, x_hi, start=start, stop=False)
                nc.tensor.matmul(ps, hi, x_lo, start=False, stop=False)
                return nc.tensor.matmul(ps, lo, x_hi, start=False, stop=stop)

            def mod_sum(n):
                pe.wait_ge(mod_part, (n - MG) * 7 + 7)
                for b in range(MC // P):
                    last = nc.tensor.matmul(banks[:, MODS_BANK, bass.ds(n * 3 + b, 1)], mod_acc[:, b * P:(b + 1) * P],
                                            ones[:], start=True, stop=True)
                last.then_inc(mod_mm, 1)

            def first_sum(n):
                pe.wait_ge(mod_step, n * K + K)
                for b in range(MC // P):
                    for h in range(2):
                        last = nc.tensor.matmul(banks[:, MODS_BANK, n * 3 + b:n * 3 + b + 1],
                                                first_acc[n % 2][h][:, b * P:(b + 1) * P], ones[:], start=(h == 0),
                                                stop=(h == 1))
                last.then_inc(mod_mm, 1)

            def unit_of_two(u, s, x_hi, x_lo, bank, credit, chunks=None, between=None):
                pe.wait_ge(lo_done, u + 1)

                def step(i, k):
                    cols = slice(2 * P * k + P * i, 2 * P * k + P * i + P)
                    last = product(banks[:, bank + i], w_hi[:, s, cols], w_lo[:, s, cols], x_hi[:, k], x_lo[:, k],
                                   k == 0, k == K - 1)
                    if k == K - 1:
                        last.then_inc(gemm_done, 1)

                if chunks is None:
                    for i in range(2):
                        pe.wait_ge(*credit(i))
                        for k in range(K):
                            step(i, k)
                else:
                    for i in range(2):
                        pe.wait_ge(*credit(i))
                    for k in range(K):
                        if between is not None and k == J:
                            between()
                        pe.wait_ge(chunks[0], chunks[1] + k + 1)
                        for i in range(2):
                            step(i, k)

            pe.sem_inc(mod_mm, 1)
            pe.wait_ge(const_ready, 13)
            pe.wait_ge(rows_loaded, 16 * 16)
            nc.tensor.transpose(banks[:, 4, 0:PT1R], rows[0:PT1R, 0, :], ident[0:PT1R, 0:PT1R]).then_inc(rows_turned, 1)
            nc.tensor.transpose(banks[:, 5, 0:R_END], rows[0:R_END, 1, :], ident[0:R_END, 0:R_END]).then_inc(rows_turned, 1)
            pe.wait_ge(x_loaded, 16)
            for k in range(K):
                if k >= 4:
                    pe.wait_ge(x_upd, k - 3)
                for a in range(TT):
                    last = nc.tensor.transpose(banks[:, k % 4, a * P:(a + 1) * P], xrow[:, a, k * P:(k + 1) * P], ident[:])
                last.then_inc(xt_turned, 1)

            def norm(nth):
                pe.wait_ge(ssq_acc, K * (nth + 1))
                for a in range(TT):
                    last = nc.tensor.matmul(banks[:, STAT_BANK, a:a + 1], tmp_a[:, P * a:P * a + P], ones[:], start=True,
                                            stop=True)
                last.then_inc(stat_done, 1)
                if nth > 0:
                    spread_root(nth)

            def spread_root(nth):
                pe.wait_ge(rstd_ready, 2 * nth + 2)
                nc.tensor.matmul(banks[:, STAT_BANK], ones_all[:], diag_rstd[:], start=True, stop=True
                                 ).then_inc(rstd_spread, 1)

            def mixer(l):
                u0, m_next = U_WIN[l], 2 * l + 1
                norm(2 * l)
                if l == 0:
                    for g in range(MG):
                        first_sum(g)
                        if g == 2:
                            spread_root(0)

                def trip(q, between=None):
                    for s in range(2):
                        if s and between is not None:
                            between()
                        unit_of_two(q * 2 + (u0 + s), s, h_hi, h_lo, 2 * s,
                                    lambda i: (proj_read, q * 4 + (20 * l + 2 * s + i + 1)),
                                    None if s else (hl_done, K * (2 * l)))
                        if s == 0:
                            mod_sum(q + MG * m_next)

                def gates(pair):
                    pe.wait_ge(gw_loaded, 64 * (l + 1))
                    for b in range(2):
                        j = 2 * pair + b
                        pe.wait_ge(xc_ready, J * l + j + 1)
                        for g in range(2):
                            n = 8 * l + 2 * j + g
                            if n >= 3:
                                pe.wait_ge(gate_read, n - 2)
                            nc.tensor.matmul(banks[:, GATE_BANKS[n % 3]], gate_w[:, g, j], xc[:, j], start=True,
                                             stop=True).then_inc(gate_done, 1)

                def group_sums(half):
                    for j in range(J):
                        pe.wait_ge(ysq_done, 8 * l + 4 * half + j + 1)
                        nc.tensor.matmul(banks[0:GR, GROUP_BANK], head_sel[:, GR - 2 - 2 * j:2 * GR - 2 - 2 * j],
                                         tt[:, j % 2], start=(j == 0), stop=(j == J - 1)).then_inc(gsum_done, 1)

                def group_spread(half):
                    pe.wait_ge(grstd_done, 2 * l + half + 1)
                    for j in range(J):
                        if j >= 2 or half:
                            pe.wait_ge(yn_done, 8 * l + 4 * half + j - 1)
                        nc.tensor.matmul(banks[:, SPREAD_BANKS[j % 2]],
                                         spread[0:GR, j],
                                         ta[0:GR, 0], start=True, stop=True).then_inc(gspread_done, 1)

                trip(0)
                trip(1, lambda: gates(0))
                trip(2, lambda: gates(1))
                trip(3)
                pe.wait_ge(gate_read, 8 * (l + 1))
                group_sums(0)
                trip(4, lambda: group_spread(0))
                mod_sum(MG * m_next + 5)
                group_sums(1)
                for q in range(WOUT_U // 2):
                    for s in range(2):
                        unit_of_two(q * 2 + (U_WOUT[l] + s), s, y_hi, y_lo, 2 * s,
                                    lambda i: (res_read, q * 4 + (16 * l + 2 * s + i + 1)),
                                    (yl_done, 8 * l) if q == s == 0 else None,
                                    lambda: group_spread(1))
                    mod_sum(q + (MG * m_next + 6))

            def up(n, s):
                pe.wait_ge(lo_done, n + (U_UP + 1))
                pe.wait_ge(pair_read, n + 1)
                for w in range(2):
                    for k in range(K):
                        if s == w == 0:
                            pe.wait_ge(hl_done, K + k + 1)
                        cols = slice(P * (K * w + k), P * (K * w + k) + P)
                        last = product(banks[:, 2 * s + w], w_hi[:, s, cols], w_lo[:, s, cols], h_hi[:, k], h_lo[:, k],
                                       k == 0, k == K - 1)
                    last.then_inc(gemm_done, 1)

            mixer(0)
            norm(1)
            with pe.Fori(0, MG) as g:
                for s in range(2):
                    up(g * 2 + s, s)
                mod_sum(g + 2 * MG)
            with pe.Fori(MG, UP_U // 2) as g:
                for s in range(2):
                    up(g * 2 + s, s)
            pe.wait_ge(al_done, FB + 1)
            with pe.Fori(0, K // 2) as mm:
                for i in range(2):
                    pe.wait_ge(res_read, mm * 2 + (8 + i + 3))
                    for h in range(2):
                        pe.wait_ge(lo_done, mm * 4 + (U_DOWN + 2 * i + h + 1))
                        for f in range(FH):
                            cols = slice(P * f, P * f + P)
                            last = product(banks[:, i], w_hi[:, h, cols], w_lo[:, h, cols], act_hi[:, h * FH + f],
                                           act_lo[:, h * FH + f], h == 0 and f == 0, h == 1 and f == FH - 1)
                        last.then_inc(gemm_done, 2)
            mixer(1)

            norm(3)

            def token_major(src, first, n):
                m = first + n
                if m >= 4:
                    pe.wait_ge(tok_read, m - 3)
                for q in range(4):
                    last = nc.tensor.transpose(banks[:, TOK_BANKS[n % 4], P * q:P * q + P],
                                               src[:, 4 * (n % 2) + q, P * (n // 2):P * (n // 2) + P], ident[:])
                last.then_inc(tok_turned, 1)

            pe.wait_ge(mods_ready, 4)
            pe.wait_ge(rw_loaded, 32)
            for k in range(K):
                pe.wait_ge(hf_done, 3 * K + k + 1)
                last = nc.tensor.matmul(banks[0:E, 0], rw[:, k], hf3[:, k], start=(k == 0), stop=(k == K - 1))
            last.then_inc(logits_done, 1)
            token_major(hf3, 0, 0)
            pe.wait_ge(logits_read, 1)
            for a in range(TT):
                last = nc.tensor.transpose(banks[:, LOGIT_BANK, E * a:E * a + E], lg[0:E, P * a:P * a + P], ident[0:E, 0:E])
            last.then_inc(logits_done, 1)
            for n in range(1, 4):
                token_major(hf3, 0, n)
            pe.wait_ge(mask_ready, 1)
            mask = rt[:, 5].rearrange("p a e -> p (a e)")
            nc.tensor.matmul(banks[:, 5, 0:TT * E], before[:], mask, start=True, stop=True)
            nc.tensor.matmul(banks[:, 5, TT * E:2 * TT * E], ones_all[:], mask, start=True, stop=True).then_inc(count_done, 1)
            for n in range(4, 2 * TT):
                token_major(hf3, 0, n)
            for n in range(2 * TT):
                token_major(xT, 2 * TT, n)

            def turn_rows(i):
                pe.wait_ge(rows_in, i * 16 + 16)
                for n in range(4):
                    for q in range(4):
                        k = 4 * (n % 2) + q
                        last = nc.tensor.transpose(banks[:, (4, 5, 0, 1)[n], P * q:P * q + P],
                                                   h_rows[:, n // 2, P * k:P * k + P], ident[:])
                    last.then_inc(ht_turned, 1)

            def trip(i, tiles):
                def turn_hidden(g):
                    pe.wait_ge(hid_done, i * EG + (g + 2))
                    pe.wait_ge(at_lo_done, i * EG + (g + 1))
                    for a in range(tiles):
                        for q, f in enumerate(range(WHOLE[g], WHOLE[g + 1])):
                            last = nc.tensor.transpose(banks[:, 4 + a, P * q:P * q + P], hid[:, a, P * f:P * f + P], ident[:])
                    last.then_inc(at_turned, 1)

                pe.wait_ge(ht_lo_done, i * 4 + 4)
                for j in range(EU):
                    s = j % RAWS
                    pe.wait_ge(e_lo_done, i * EU + (j + 1))
                    if j < 2 * EG:
                        g, w = j // 2, j % 2
                        if w == 0:
                            pe.wait_ge(e_silu_done, i * EG + (g + 1))
                        else:
                            pe.wait_ge(hid_done, i * EG + (g + 1))
                            if g == 0:
                                pe.wait_ge(y_read, i + 1)
                        for a in range(tiles):
                            for k in range(K):
                                cols = slice(EC * k, EC * k + EC)
                                part = (slice(None), k, slice(P * a, P * a + P))
                                last = product(banks[:, 2 * w + a, 0:EC], ht_hi[part], ht_lo[part], e_hi[:, s, cols],
                                               e_lo[:, s, cols], k == 0, k == K - 1)
                    else:
                        if j == 2 * EG:
                            pe.wait_ge(y_read, i + 1)
                        f0, f1 = W2_CUT[j - 2 * EG], W2_CUT[j - 2 * EG + 1]
                        whole = min(g for g in range(EG + 1) if WHOLE[g] >= f1)
                        pe.wait_ge(at_lo_done, i * EG + (whole + 1))
                        for a in range(tiles):
                            if j == 2 * EG and a == 1:
                                pe.wait_ge(hid_done, i * EG + (EG + 1))
                            for half in range(2):
                                for f in range(f0, f1):
                                    cols = slice(D * (f - f0) + 512 * half, D * (f - f0) + 512 * half + 512)
                                    part = (slice(None), f, slice(P * a, P * a + P))
                                    last = product(banks[:, (6, 2)[a] + half], at_hi[part], at_lo[part], e_hi[:, s, cols],
                                                   e_lo[:, s, cols], f == 0, f == FEB - 1)
                    last.then_inc(e_used, 1)
                    if j in (3, 5, 7):
                        turn_hidden((j - 3) // 2)
                    if j == 8:
                        turn_hidden(3)
                    if j == 9:
                        pe.wait_ge(at_lo_done, i * EG + (EG + 1))
                        turn_rows(i + 1)

            pe.sem_inc(e_used, RAWS)
            pe.wait_ge(sorted_stored, 16 * 2 * TT)
            pe.wait_ge(tok_read, 4 * TT)
            pe.wait_ge(table_ready, 1)
            turn_rows(0)
            trips = pe.value_load(table[0:1, 3, 0:1], min_val=1, max_val=MAX_TRIPS)
            with pe.Fori(0, trips) as i:
                two = pe.value_load(table[0:1, 2, bass.ds(i, 1)], min_val=0, max_val=1)
                with pe.If(two > 0):
                    trip(i, 2)
                with pe.Else():
                    trip(i, 1)
                pe.nop()
            pe.wait_ge(y_read, trips + 1)
            for which in range(2):
                for k in range(K):
                    pe.wait_ge(diag_ready, K * which + k + 1)
                    last = nc.tensor.matmul(banks[:, 2 * which + k // 4, P * (k % 4):P * (k % 4) + P], ones_all[:],
                                            diag[:, which, k], start=True, stop=True)
                    if k % 4 == 3:
                        last.then_inc(row_done, 1)
    return None


INPUTS = ["x", "c", "mix_norm", "mix_mod_w", "mix_mod_b", "w_in", "lru_conv_w", "lru_conv_b", "lru_wa", "lru_ba",
          "lru_wi", "lru_bi", "lru_lambda", "sc_conv_w", "gn_lru", "gn_sc", "w_out", "ffn_norm", "ffn_mod_w",
          "ffn_mod_b", "dense_w1", "dense_w3", "dense_w2", "router_w", "router_b", "exp_w1", "exp_w3", "exp_w2",
          "final_norm"]


def kernel(**inputs):
    import numpy as np
    import concourse.bacc as bacc
    from concourse.bass_utils import run_bass_kernel_spmd

    nc = bacc.Bacc("TRN2", target_bir_lowering=False, num_devices=1)
    arrays = {f"in_{n}": np.ascontiguousarray(inputs[n]) for n in INPUTS}
    args = {n: nc.dram_tensor(f"in_{n}", arrays[f"in_{n}"].shape, F32, kind="ExternalInput").ap() for n in INPUTS}
    out = nc.dram_tensor("out", arrays["in_x"].shape, F32, kind="ExternalOutput")
    trunk_kernel(nc, out=out.ap(), **args)
    result = run_bass_kernel_spmd(nc, [arrays], core_ids=[0])
    return result.results[0]["out"]
```
